# Optimizing a Trainium2 kernel written in Bass

```python
import jax, jax.numpy as jnp
from jax import lax
import numpy as np
import math

D_MODEL = 2048
BATCH = 1
SEQ = 256
DEPTH = 4

N_MIXERS = 3
RMS_EPS = 1e-6

RWKV_HEAD_DIM = 64
RWKV_HEADS = D_MODEL // RWKV_HEAD_DIM
DECAY_LORA = 96
AAA_LORA = 96
MV_LORA = 64
RWKV_LN_EPS = 64e-5

ATT_HEAD_DIM = 128
DILATED_CONFIG = ((128, 1), (512, 4), (2048, 16))
ATT_GROUPS = len(DILATED_CONFIG)
ATT_HEADS_PER_GROUP = D_MODEL // (2 * ATT_HEAD_DIM)
ATT_BRANCH = ATT_HEADS_PER_GROUP * ATT_HEAD_DIM
ATT_QKV = 3 * ATT_GROUPS * ATT_BRANCH
ATT_BLOCK = 128
ROPE_THETA = 500000.0
ROPE_DIM = ATT_HEAD_DIM // 4

POOL_WINDOWS = (2, 4, 8, 16)
POOL_WIDTH = D_MODEL
POOL_GROUP = POOL_WIDTH // len(POOL_WINDOWS)


def _rms_norm(x, w):
    xf = x.astype(jnp.float32)
    y = xf * lax.rsqrt(jnp.mean(xf * xf, axis=-1, keepdims=True) + RMS_EPS)
    return (y * w.astype(jnp.float32)).astype(x.dtype)

def _rwkv7_scan(r, w, k, v, a, b):
    B, S, H, N = r.shape

    def step(state, inp):
        r_t, w_t, k_t, v_t, a_t, b_t = inp
        sa = jnp.einsum('bhij,bhj->bhi', state, a_t)
        state = (state * w_t[:, :, None, :] + sa[..., None] * b_t[:, :, None, :]
                 + v_t[..., None] * k_t[:, :, None, :])
        y_t = jnp.einsum('bhij,bhj->bhi', state, r_t)
        return state, y_t

    xs = tuple(jnp.moveaxis(t, 1, 0) for t in (r, w, k, v, a, b))
    init = jnp.zeros((B, H, N, N), jnp.float32)
    _, ys = lax.scan(step, init, xs)
    return jnp.moveaxis(ys, 0, 1)

def _head_group_norm(y, w, b):
    B, S, H, N = y.shape
    mu = jnp.mean(y, axis=-1, keepdims=True)
    yc = y - mu
    var = jnp.mean(yc * yc, axis=-1, keepdims=True)
    yn = (yc * lax.rsqrt(var + RWKV_LN_EPS)).reshape(B, S, H * N)
    return yn * w.astype(jnp.float32) + b.astype(jnp.float32)

def _rwkv7_mixer(h, mu, w_in, w0, w1, w2, a0, a1, a2, k_k, k_a, r_k, lnx_w, lnx_b,
                 w_out, v_first, vres):
    B, S, D = h.shape
    H, N = RWKV_HEADS, RWKV_HEAD_DIM
    heads = lambda t: t.reshape(B, S, H, N)
    xx = jnp.pad(h, ((0, 0), (1, 0), (0, 0)))[:, :S] - h
    r, k, v, g = [(h + xx * mu[j]) @ w_in[j] for j in range(4)]
    xw = h + xx * mu[4]
    xa = h + xx * mu[5]
    w_log = -jax.nn.softplus(-(w0 + jnp.tanh(xw @ w1) @ w2).astype(jnp.float32)) - 0.5
    decay = jnp.exp(-jnp.exp(w_log))
    if vres is None:
        v_first = v
    else:
        v0, v1, v2 = vres
        xv = h + xx * mu[2]
        v = v + (v_first - v) * jax.nn.sigmoid(v0 + (xv @ v1) @ v2)
    a = jax.nn.sigmoid(a0 + (xa @ a1) @ a2)
    kk = heads(k * k_k).astype(jnp.float32)
    kk = kk / jnp.maximum(jnp.sqrt(jnp.sum(kk * kk, axis=-1, keepdims=True)), 1e-12)
    k = k * (1 + (a - 1) * k_a)
    af = heads(a).astype(jnp.float32)
    vf = heads(v).astype(jnp.float32)
    y = _rwkv7_scan(heads(r).astype(jnp.float32), heads(decay), heads(k).astype(jnp.float32),
                    vf, -kk, kk * af)
    y = _head_group_norm(y, lnx_w, lnx_b)
    bonus = jnp.sum(heads(r * k).astype(jnp.float32) * r_k.astype(jnp.float32),
                    axis=-1, keepdims=True) * vf
    y = (y + bonus.reshape(B, S, D)).astype(h.dtype) * jax.nn.silu(g)
    return y @ w_out, v_first

def _rope_tables(positions):
    inv_freq = ROPE_THETA ** (-jnp.arange(0, ROPE_DIM, 2, dtype=jnp.float32) / ROPE_DIM)
    ang = positions.astype(jnp.float32)[..., None] * inv_freq
    return jnp.cos(ang), jnp.sin(ang)

def _apply_partial_rope(x, cos, sin):
    half = ROPE_DIM // 2
    c = cos[:, :, None, None, :].astype(x.dtype)
    s = sin[:, :, None, None, :].astype(x.dtype)
    x1 = x[..., :half]
    x2 = x[..., half:ROPE_DIM]
    return jnp.concatenate([x1 * c - x2 * s, x1 * s + x2 * c, x[..., ROPE_DIM:]], axis=-1)

def _dilated_window_attention(q, k, v, window, dilation):
    B, S, H, Dh = q.shape
    steps = window // dilation
    L = S // dilation
    nblk = -(-L // ATT_BLOCK)
    pad = nblk * ATT_BLOCK - L

    def gather(t):
        t = t.reshape(B, L, dilation, H, Dh).transpose(0, 2, 3, 1, 4)
        t = jnp.pad(t, ((0, 0), (0, 0), (0, 0), (0, pad), (0, 0)))
        return t.reshape(B, dilation, H, nblk, ATT_BLOCK, Dh)

    def with_prev(t):
        prev = jnp.pad(t[:, :, :, :-1], ((0, 0), (0, 0), (0, 0), (1, 0), (0, 0), (0, 0)))
        return jnp.concatenate([prev, t], axis=4)

    qb = gather(q)
    kc = with_prev(gather(k))
    vc = with_prev(gather(v))
    qi = jnp.arange(ATT_BLOCK)[:, None]
    kj = jnp.arange(2 * ATT_BLOCK)[None, :]
    dist = ATT_BLOCK + qi - kj
    key_idx = (jnp.arange(nblk)[:, None, None] - 1) * ATT_BLOCK + kj[None]
    mask = (dist >= 0)[None] & (dist <= steps)[None] & (key_idx >= 0)
    s = jnp.einsum('bghnqe,bghnke->bghnqk', qb, kc).astype(jnp.float32) * (Dh ** -0.5)
    s = jnp.where(mask, s, -jnp.inf)
    m = jnp.max(s, axis=-1, keepdims=True)
    p = jnp.exp(s - m)
    l = jnp.sum(p, axis=-1, keepdims=True)
    o = jnp.einsum('bghnqk,bghnke->bghnqe', p, vc.astype(jnp.float32)) / l
    lse = (m + jnp.log(l))[..., 0]
    o = o.reshape(B, dilation, H, nblk * ATT_BLOCK, Dh)[:, :, :, :L]
    o = o.transpose(0, 3, 1, 2, 4).reshape(B, S, H, Dh)
    lse = lse.reshape(B, dilation, H, nblk * ATT_BLOCK)[:, :, :, :L]
    lse = lse.transpose(0, 3, 1, 2).reshape(B, S, H)
    return o, lse

def _dilated_attn_mixer(h, positions, w_in, qn_w, kn_w, w_out):
    B, S, _ = h.shape
    proj = h @ w_in
    qkv = proj[..., :ATT_QKV].reshape(B, S, 3, ATT_GROUPS, ATT_HEADS_PER_GROUP, ATT_HEAD_DIM)
    gate = proj[..., ATT_QKV:]
    cos, sin = _rope_tables(positions)
    q = _apply_partial_rope(_rms_norm(qkv[:, :, 0], qn_w[:, None, :]), cos, sin)
    k = _apply_partial_rope(_rms_norm(qkv[:, :, 1], kn_w[:, None, :]), cos, sin)
    v = qkv[:, :, 2]
    outs, lses = [], []
    for gi, (window, dilation) in enumerate(DILATED_CONFIG):
        o_g, lse_g = _dilated_window_attention(q[:, :, gi], k[:, :, gi], v[:, :, gi], window, dilation)
        outs.append(o_g)
        lses.append(lse_g)
    wts = jax.nn.softmax(jnp.stack(lses, axis=0), axis=0)
    o = jnp.sum(wts[..., None] * jnp.stack(outs, axis=0), axis=0)
    o = o.astype(h.dtype).reshape(B, S, ATT_BRANCH)
    return (o * jax.nn.silu(gate)) @ w_out

def _pool_mixer(h, w_in, w_grp, scale, w_out):
    B, S, _ = h.shape
    u, gate = jnp.split(h @ w_in, 2, axis=-1)
    c = jnp.pad(jnp.cumsum(u.astype(jnp.float32), axis=1), ((0, 0), (1, 0), (0, 0)))
    t = jnp.arange(S)
    pooled = []
    for j, win in enumerate(POOL_WINDOWS):
        cg = c[..., j * POOL_GROUP:(j + 1) * POOL_GROUP]
        lower = jnp.pad(cg[:, :S + 1 - win], ((0, 0), (win - 1, 0), (0, 0)))
        cnt = jnp.minimum(t + 1, win).astype(jnp.float32)[None, :, None]
        pooled.append((cg[:, 1:] - lower) / cnt)
    pooled = jnp.stack(pooled, axis=2).astype(h.dtype)
    diff = pooled - u.reshape(B, S, len(POOL_WINDOWS), POOL_GROUP)
    y = jnp.einsum('bsgc,gce->bsge', diff, w_grp).reshape(B, S, POOL_WIDTH) * scale
    return (y * jax.nn.silu(gate)) @ w_out

def first_inputs(seed: int = 0) -> dict:
    key = jax.random.key(seed)
    ks = iter(jax.random.split(key, 40))
    f32 = jnp.float32
    n_a = (DEPTH + 2) // 3
    n_b = (DEPTH + 1) // 3
    n_c = DEPTH // 3
    D, H, N = D_MODEL, RWKV_HEADS, RWKV_HEAD_DIM

    def nrm(shape, scale):
        return jax.random.normal(next(ks), shape, f32) * scale

    x = jax.random.normal(next(ks), (BATCH, SEQ, D), f32)
    offset = jax.random.randint(next(ks), (BATCH, 1), 0, 4096, dtype=jnp.int32)
    positions = offset + jnp.arange(SEQ, dtype=jnp.int32)[None, :]
    norm_w = 1.0 + nrm((DEPTH, D), 0.1)
    lin = jnp.linspace(0.0, 1.0, D, dtype=f32)
    inp = {
        'x': x,
        'positions': positions,
        'norm_w': norm_w,
        'a_mu': jax.random.uniform(next(ks), (n_a, 6, D), f32),
        'a_w_in': nrm((n_a, 4, D, D), D ** -0.5),
        'a_w0': (-6.5 + 5.0 * lin ** 1.5)[None, :] + nrm((n_a, D), 0.1),
        'a_w1': nrm((n_a, D, DECAY_LORA), D ** -0.5),
        'a_w2': nrm((n_a, DECAY_LORA, D), 0.1 * DECAY_LORA ** -0.5),
        'a_a0': nrm((n_a, D), 0.3),
        'a_a1': nrm((n_a, D, AAA_LORA), D ** -0.5),
        'a_a2': nrm((n_a, AAA_LORA, D), 0.3 * AAA_LORA ** -0.5),
        'a_k_k': 0.85 + nrm((n_a, D), 0.05),
        'a_k_a': 1.0 + nrm((n_a, D), 0.05),
        'a_r_k': nrm((n_a, H, N), 0.1),
        'a_lnx_w': 1.0 + nrm((n_a, D), 0.1),
        'a_lnx_b': nrm((n_a, D), 0.02),
        'a_v0': 1.0 + nrm((n_a - 1, D), 0.1),
        'a_v1': nrm((n_a - 1, D, MV_LORA), D ** -0.5),
        'a_v2': nrm((n_a - 1, MV_LORA, D), 0.3 * MV_LORA ** -0.5),
        'a_w_out': nrm((n_a, D, D), 0.5 * D ** -0.5),
        'b_w_in': nrm((n_b, D, ATT_QKV + ATT_BRANCH), D ** -0.5),
        'b_qn_w': 1.0 + nrm((n_b, ATT_GROUPS, ATT_HEAD_DIM), 0.1),
        'b_kn_w': 1.0 + nrm((n_b, ATT_GROUPS, ATT_HEAD_DIM), 0.1),
        'b_w_out': nrm((n_b, ATT_BRANCH, D), 0.5 * ATT_BRANCH ** -0.5),
        'c_w_in': nrm((n_c, D, 2 * POOL_WIDTH), D ** -0.5),
        'c_w_grp': nrm((n_c, len(POOL_WINDOWS), POOL_GROUP, POOL_GROUP), POOL_GROUP ** -0.5),
        'c_scale': 1.0 + nrm((n_c, POOL_WIDTH), 0.1),
        'c_w_out': nrm((n_c, POOL_WIDTH, D), 0.5 * POOL_WIDTH ** -0.5),
    }
    return inp

def first_block(x, positions, norm_w, a_mu, a_w_in, a_w0, a_w1, a_w2, a_a0, a_a1, a_a2,
              a_k_k, a_k_a, a_r_k, a_lnx_w, a_lnx_b, a_v0, a_v1, a_v2, a_w_out,
              b_w_in, b_qn_w, b_kn_w, b_w_out, c_w_in, c_w_grp, c_scale, c_w_out):
    ia = ib = ic = 0
    v_first = None
    for i in range(DEPTH):
        h = _rms_norm(x, norm_w[i])
        kind = i % N_MIXERS
        if kind == 0:
            vres = None if ia == 0 else (a_v0[ia - 1], a_v1[ia - 1], a_v2[ia - 1])
            y, vf = _rwkv7_mixer(h, a_mu[ia], a_w_in[ia], a_w0[ia], a_w1[ia], a_w2[ia],
                                 a_a0[ia], a_a1[ia], a_a2[ia], a_k_k[ia], a_k_a[ia], a_r_k[ia],
                                 a_lnx_w[ia], a_lnx_b[ia], a_w_out[ia], v_first, vres)
            if v_first is None:
                v_first = vf
            ia += 1
        elif kind == 1:
            y = _dilated_attn_mixer(h, positions, b_w_in[ib], b_qn_w[ib], b_kn_w[ib], b_w_out[ib])
            ib += 1
        else:
            y = _pool_mixer(h, c_w_in[ic], c_w_grp[ic], c_scale[ic], c_w_out[ic])
            ic += 1
        x = x + y
    return x


DEPTH_2 = 2

EPS = 1e-6
GRID_W = 64
HEAD_DIM = 128
ATTN_HEADS = D_MODEL // 256
KV_HEADS = max(1, ATTN_HEADS // 4)
ATTN_WIDTH = ATTN_HEADS * HEAD_DIM
KV_WIDTH = KV_HEADS * HEAD_DIM
Q_BLOCK = 128
ROPE_THETA_2 = 10000.0
ROPE_HALF = HEAD_DIM // 2
LRU_WIDTH = D_MODEL // 2
LRU_BLOCKS = 8
LRU_BLOCK = LRU_WIDTH // LRU_BLOCKS
LRU_C = 8.0
CONV_W = 4
CONV_PAD = (2, 1)
EVEN_IN = ATTN_WIDTH + 2 * KV_WIDTH + ATTN_WIDTH + 2 * LRU_WIDTH
EVEN_MIX = ATTN_WIDTH + LRU_WIDTH
MLSTM_HEADS = 8
MLSTM_V_DIM = D_MODEL // MLSTM_HEADS
MLSTM_QK_DIM = MLSTM_V_DIM // 2
MLSTM_WIDTH = MLSTM_HEADS * MLSTM_V_DIM
MLSTM_QK_WIDTH = MLSTM_HEADS * MLSTM_QK_DIM
MLSTM_CHUNK = 128
N_GATE_SETS = 4
ODD_IN = 2 * MLSTM_QK_WIDTH + 3 * MLSTM_WIDTH + N_GATE_SETS * MLSTM_HEADS
N_EVEN = (DEPTH_2 + 1) // 2
N_ODD = DEPTH_2 // 2


def rmsnorm(x, g):
    xf = x.astype(jnp.float32)
    y = xf * lax.rsqrt(jnp.mean(xf * xf, axis=-1, keepdims=True) + EPS) * g.astype(jnp.float32)
    return y.astype(x.dtype)

def split_at(t, sizes):
    idx = np.cumsum(sizes)[:-1].tolist()
    return jnp.split(t, idx, axis=-1)

def axial_angles(seq_len):
    rows = seq_len // GRID_W
    row = jnp.repeat(jnp.arange(rows), GRID_W).astype(jnp.float32)
    col = jnp.tile(jnp.arange(GRID_W), rows).astype(jnp.float32)
    inv = ROPE_THETA_2 ** (-jnp.arange(0, ROPE_HALF, 2, dtype=jnp.float32) / ROPE_HALF)
    return row[:, None] * inv, col[:, None] * inv

def rotate_half_pairs(x, ang):
    x1, x2 = jnp.split(x, 2, axis=-1)
    c = jnp.cos(ang)[None, :, None, :]
    s = jnp.sin(ang)[None, :, None, :]
    return jnp.concatenate([x1 * c - x2 * s, x1 * s + x2 * c], axis=-1)

def axial_rope(x, ang_row, ang_col):
    xr, xc = jnp.split(x, 2, axis=-1)
    return jnp.concatenate([rotate_half_pairs(xr, ang_row), rotate_half_pairs(xc, ang_col)], axis=-1)

def block_attention(q, k, v):
    B, S, H, D = q.shape
    G = H // KV_HEADS
    nb = S // Q_BLOCK
    qb = q.reshape(B, nb, Q_BLOCK, KV_HEADS, G, D).transpose(1, 0, 3, 4, 2, 5)
    scale = HEAD_DIM ** -0.5

    def one_block(qi):
        s = jnp.einsum('bkgqd,bskd->bkgqs', qi, k) * scale
        p = jax.nn.softmax(s, axis=-1)
        return jnp.einsum('bkgqs,bskd->bkgqd', p, v)

    o = lax.map(one_block, qb)
    return o.transpose(1, 0, 4, 2, 3, 5).reshape(B, S, H * D)

def lru_combine(e1, e2):
    a1, b1 = e1
    a2, b2 = e2
    return a1 * a2, a2 * b1 + b2

def rg_lru(xc, wa, ba, wx, bx, lam, reverse):
    B, S, W = xc.shape
    xb = xc.reshape(B, S, LRU_BLOCKS, LRU_BLOCK)
    r = jax.nn.sigmoid(jnp.einsum('bsnc,ncd->bsnd', xb, wa).reshape(B, S, W) + ba)
    i = jax.nn.sigmoid(jnp.einsum('bsnc,ncd->bsnd', xb, wx).reshape(B, S, W) + bx)
    log_a = LRU_C * r * jax.nn.log_sigmoid(lam)
    a = jnp.exp(log_a)
    u = jnp.sqrt(-jnp.expm1(2.0 * log_a)) * (i * xc)
    _, h = lax.associative_scan(lru_combine, (a, u), reverse=reverse, axis=1)
    return h

def even_layer(h, w_in, w_out, q_gain, k_gain, conv_w, conv_b, wa, ba, wx, bx, lam):
    B, S, _ = h.shape
    f32 = jnp.float32
    proj = h @ w_in
    q, k, v, g_attn, x_lru, g_lru = split_at(
        proj, [ATTN_WIDTH, KV_WIDTH, KV_WIDTH, ATTN_WIDTH, LRU_WIDTH, LRU_WIDTH])
    q = rmsnorm(q.reshape(B, S, ATTN_HEADS, HEAD_DIM).astype(f32), q_gain)
    k = rmsnorm(k.reshape(B, S, KV_HEADS, HEAD_DIM).astype(f32), k_gain)
    v = v.reshape(B, S, KV_HEADS, HEAD_DIM).astype(f32)
    ang_row, ang_col = axial_angles(S)
    q = axial_rope(q, ang_row, ang_col)
    k = axial_rope(k, ang_row, ang_col)
    attn = block_attention(q, k, v)
    xc = lax.conv_general_dilated(
        x_lru, conv_w[:, None, :], window_strides=(1,), padding=[CONV_PAD],
        dimension_numbers=('NWC', 'WIO', 'NWC'), feature_group_count=LRU_WIDTH) + conv_b
    xc = xc.astype(f32)
    y = (rg_lru(xc, wa[0], ba[0], wx[0], bx[0], lam[0], reverse=False)
         + rg_lru(xc, wa[1], ba[1], wx[1], bx[1], lam[1], reverse=True))
    mix = jnp.concatenate([attn * jax.nn.silu(g_attn.astype(f32)),
                           y * jax.nn.silu(g_lru.astype(f32))], axis=-1)
    return mix.astype(h.dtype) @ w_out

def mlstm_chunkwise(q, k, v, ig, lf):
    B, H, S, dk = q.shape
    dv = v.shape[-1]
    L = MLSTM_CHUNK
    nc = S // L

    def to_chunks(t):
        return jnp.moveaxis(t.reshape((B, H, nc, L) + t.shape[3:]), 2, 0)

    mask = jnp.tril(jnp.ones((L, L), dtype=bool))

    def step(carry, inp):
        C, n, m = carry
        qi, ki, vi, ii, fi = inp
        b = jnp.cumsum(fi, axis=-1)
        logd = jnp.where(mask, b[..., :, None] - b[..., None, :] + ii[..., None, :], -jnp.inf)
        m_inter = b + m[..., None]
        m_t = jnp.maximum(m_inter, jnp.max(logd, axis=-1))
        sc = jnp.einsum('bhld,bhsd->bhls', qi, ki) * jnp.exp(logd - m_t[..., None])
        inter = jnp.exp(m_inter - m_t)
        num = jnp.einsum('bhls,bhsv->bhlv', sc, vi) + inter[..., None] * jnp.einsum('bhld,bhvd->bhlv', qi, C)
        den = jnp.sum(sc, axis=-1) + inter * jnp.einsum('bhld,bhd->bhl', qi, n)
        hout = num / jnp.maximum(jnp.abs(den), jnp.exp(-m_t))[..., None]
        b_last = b[..., -1]
        w = b_last[..., None] - b + ii
        m_new = jnp.maximum(b_last + m, jnp.max(w, axis=-1))
        decay = jnp.exp(b_last + m - m_new)
        ws = jnp.exp(w - m_new[..., None])
        C_new = decay[..., None, None] * C + jnp.einsum('bhsv,bhsd->bhvd', vi * ws[..., None], ki)
        n_new = decay[..., None] * n + jnp.einsum('bhs,bhsd->bhd', ws, ki)
        return (C_new, n_new, m_new), hout

    init = (jnp.zeros((B, H, dv, dk), jnp.float32), jnp.zeros((B, H, dk), jnp.float32),
            jnp.zeros((B, H), jnp.float32))
    _, hc = lax.scan(step, init, (to_chunks(q), to_chunks(k), to_chunks(v), to_chunks(ig), to_chunks(lf)))
    return jnp.moveaxis(hc, 0, 2).reshape(B, H, S, dv)

def odd_layer(h, w_in, gate_bias, norm_gain, w_out):
    B, S, _ = h.shape
    f32 = jnp.float32
    proj = h @ w_in
    q, k, v, o, z, gates = split_at(
        proj, [MLSTM_QK_WIDTH, MLSTM_QK_WIDTH, MLSTM_WIDTH, MLSTM_WIDTH, MLSTM_WIDTH, N_GATE_SETS * MLSTM_HEADS])

    def heads(t, d):
        return t.reshape(B, S, MLSTM_HEADS, d).transpose(0, 2, 1, 3).astype(f32)

    q = heads(q, MLSTM_QK_DIM)
    k = heads(k, MLSTM_QK_DIM) * (MLSTM_QK_DIM ** -0.5)
    v = heads(v, MLSTM_V_DIM)
    g = gates.astype(f32).reshape(B, S, N_GATE_SETS, MLSTM_HEADS) + gate_bias.astype(f32)
    i_f, i_b, f_f, f_b = g.transpose(2, 0, 3, 1)
    h_f = mlstm_chunkwise(q, k, v, i_f, jax.nn.log_sigmoid(f_f))
    flip = lambda t: jnp.flip(t, axis=2)
    h_b = flip(mlstm_chunkwise(flip(q), flip(k), flip(v), flip(i_b), flip(jax.nn.log_sigmoid(f_b))))
    hs = (h_f + h_b).transpose(0, 2, 1, 3)
    hs = jax.nn.sigmoid(o.astype(f32)).reshape(B, S, MLSTM_HEADS, MLSTM_V_DIM) * hs
    hs = rmsnorm(hs, norm_gain.reshape(MLSTM_HEADS, MLSTM_V_DIM))
    hs = hs.reshape(B, S, MLSTM_WIDTH) * jax.nn.silu(z.astype(f32))
    return hs.astype(h.dtype) @ w_out

def second_inputs(seed: int = 0) -> dict:
    key = jax.random.key(seed)
    ks = jax.random.split(key, 24)
    f32 = jnp.float32
    nrm = lambda k, shape, scale: jax.random.normal(k, shape, f32) * scale
    x = nrm(ks[0], (BATCH, SEQ, D_MODEL), 1.0)
    norm_gain = 1.0 + nrm(ks[1], (DEPTH_2, D_MODEL), 0.05)
    final_gain = 1.0 + nrm(ks[2], (D_MODEL,), 0.05)
    even_w_in = nrm(ks[3], (N_EVEN, D_MODEL, EVEN_IN), D_MODEL ** -0.5)
    even_w_out = nrm(ks[4], (N_EVEN, EVEN_MIX, D_MODEL), EVEN_MIX ** -0.5)
    q_norm_gain = 1.0 + nrm(ks[5], (N_EVEN, HEAD_DIM), 0.05)
    k_norm_gain = 1.0 + nrm(ks[6], (N_EVEN, HEAD_DIM), 0.05)
    conv_w = nrm(ks[7], (N_EVEN, CONV_W, LRU_WIDTH), CONV_W ** -0.5)
    conv_b = nrm(ks[8], (N_EVEN, LRU_WIDTH), 0.02)
    lru_wa = nrm(ks[9], (N_EVEN, 2, LRU_BLOCKS, LRU_BLOCK, LRU_BLOCK), LRU_BLOCK ** -0.5)
    lru_ba = nrm(ks[10], (N_EVEN, 2, LRU_WIDTH), 0.1)
    lru_wx = nrm(ks[11], (N_EVEN, 2, LRU_BLOCKS, LRU_BLOCK, LRU_BLOCK), LRU_BLOCK ** -0.5)
    lru_bx = nrm(ks[12], (N_EVEN, 2, LRU_WIDTH), 0.1)
    a0 = jax.random.uniform(ks[13], (N_EVEN, 2, LRU_WIDTH), f32, minval=0.9, maxval=0.999)
    p = a0 ** (1.0 / LRU_C)
    lru_lambda = jnp.log(p) - jnp.log1p(-p)
    odd_w_in = nrm(ks[14], (N_ODD, D_MODEL, ODD_IN), D_MODEL ** -0.5)
    i_bias = nrm(ks[15], (N_ODD, 2, MLSTM_HEADS), 0.1)
    f_bias = jnp.broadcast_to(jnp.linspace(3.0, 6.0, MLSTM_HEADS, dtype=f32), (N_ODD, 2, MLSTM_HEADS)) \
        + nrm(ks[16], (N_ODD, 2, MLSTM_HEADS), 0.1)
    odd_gate_bias = jnp.concatenate([i_bias, f_bias], axis=1)
    odd_norm_gain = 1.0 + nrm(ks[17], (N_ODD, MLSTM_WIDTH), 0.05)
    odd_w_out = nrm(ks[18], (N_ODD, MLSTM_WIDTH, D_MODEL), MLSTM_WIDTH ** -0.5)
    return {'x': x, 'norm_gain': norm_gain, 'final_gain': final_gain,
            'even_w_in': even_w_in, 'even_w_out': even_w_out,
            'q_norm_gain': q_norm_gain, 'k_norm_gain': k_norm_gain,
            'conv_w': conv_w, 'conv_b': conv_b,
            'lru_wa': lru_wa, 'lru_ba': lru_ba, 'lru_wx': lru_wx, 'lru_bx': lru_bx,
            'lru_lambda': lru_lambda,
            'odd_w_in': odd_w_in, 'odd_gate_bias': odd_gate_bias,
            'odd_norm_gain': odd_norm_gain, 'odd_w_out': odd_w_out}

def second_block(x, norm_gain, final_gain, even_w_in, even_w_out, q_norm_gain, k_norm_gain,
              conv_w, conv_b, lru_wa, lru_ba, lru_wx, lru_bx, lru_lambda,
              odd_w_in, odd_gate_bias, odd_norm_gain, odd_w_out):
    for layer in range(DEPTH_2):
        hn = rmsnorm(x, norm_gain[layer])
        j = layer // 2
        if layer % 2 == 0:
            out = even_layer(hn, even_w_in[j], even_w_out[j], q_norm_gain[j], k_norm_gain[j],
                             conv_w[j], conv_b[j], lru_wa[j], lru_ba[j], lru_wx[j], lru_bx[j],
                             lru_lambda[j])
        else:
            out = odd_layer(hn, odd_w_in[j], odd_gate_bias[j], odd_norm_gain[j], odd_w_out[j])
        x = x + out.astype(x.dtype)
    return rmsnorm(x, final_gain)


def setup_inputs(seed=0):
    out = dict(first_inputs(seed))
    for name, value in second_inputs(seed + 1).items():
        if name != "x":
            out[name + "_2"] = value
    return out


def reference(
    x, positions, norm_w, a_mu, a_w_in, a_w0, a_w1, a_w2, a_a0, a_a1, a_a2, a_k_k, a_k_a, a_r_k,
    a_lnx_w, a_lnx_b, a_v0, a_v1, a_v2, a_w_out, b_w_in, b_qn_w, b_kn_w, b_w_out, c_w_in,
    c_w_grp, c_scale, c_w_out, norm_gain_2, final_gain_2, even_w_in_2, even_w_out_2,
    q_norm_gain_2, k_norm_gain_2, conv_w_2, conv_b_2, lru_wa_2, lru_ba_2, lru_wx_2, lru_bx_2,
    lru_lambda_2, odd_w_in_2, odd_gate_bias_2, odd_norm_gain_2, odd_w_out_2,
):
    x = first_block(
        x, positions, norm_w, a_mu, a_w_in, a_w0, a_w1, a_w2, a_a0, a_a1, a_a2, a_k_k, a_k_a,
        a_r_k, a_lnx_w, a_lnx_b, a_v0, a_v1, a_v2, a_w_out, b_w_in, b_qn_w, b_kn_w, b_w_out,
        c_w_in, c_w_grp, c_scale, c_w_out,
    )
    return second_block(
        x, norm_gain_2, final_gain_2, even_w_in_2, even_w_out_2, q_norm_gain_2, k_norm_gain_2,
        conv_w_2, conv_b_2, lru_wa_2, lru_ba_2, lru_wx_2, lru_bx_2, lru_lambda_2, odd_w_in_2,
        odd_gate_bias_2, odd_norm_gain_2, odd_w_out_2,
    )


_drawn_inputs = setup_inputs


def setup_inputs(seed=0):
    import zlib

    import numpy as np

    out = dict(_drawn_inputs(seed))
    spreads = {}
    factors = {'a_w1': 8.0,
     'a_w2': 8.0,
     'a_lnx_b': 3.488,
     'a_v0': 21.453,
     'b_qn_w': 6.572,
     'b_kn_w': 6.23,
     'q_norm_gain_2': 8.0,
     'k_norm_gain_2': 8.0,
     'lru_ba_2': 5.103,
     'lru_bx_2': 2.967,
     'a_v1': 8.0,
     'a_v2': 7.338}
    for name, (base, spread) in spreads.items():
        noise = np.random.default_rng([zlib.crc32(name.encode()), seed]).standard_normal(out[name].shape)
        drawn = base * np.exp(spread * noise) if base else spread * noise
        out[name] = __import__('jax').numpy.asarray(drawn.astype(out[name].dtype))
    for name, factor in factors.items():
        out[name] = (out[name] * factor).astype(out[name].dtype)
    return out
```

```python
from contextlib import ExitStack

import numpy as np
import concourse.bass as bass
from concourse import mybir
from concourse.alu_op_type import AluOpType as ALU

F32 = mybir.dt.float32
I32 = mybir.dt.int32
ACT = mybir.ActivationFunctionType
AX = mybir.AxisListType

T = 256
D = 2048
P = 128
KC = D // P
SLOTS = 4
CH = 64
NU = T // CH
TS = T // P
LEVELS = 5
DECAY = float(np.exp(-0.5))
LN2_8 = float(8 * np.log(2.0))
HEADS = 8
GROUPS = 3
LORA = 96
MVL = 64
MASKED = -1e30


class Phase:

    def __init__(self, b, t, blocks, tiles):
        self.b, self.t, self.blocks, self.tiles = b, t, blocks, tiles


STREAM = [
    ("lora0", 2, 2), ("rwkv0", 64, 64), ("out0", 16, 16),
    ("heads1", 80, 80), ("out1", 8, 16),
    ("pool_u", 16, 16), ("pool_gate", 16, 16), ("pool_mix", 4, 16), ("out2", 16, 16),
    ("lora3", 3, 3), ("rwkv3", 64, 64), ("out3", 16, 16),
    ("kv4", 4, 4), ("heads4", 16, 16), ("lru4", 16, 16), ("out4", 16, 16),
    ("gates5", 0, 1), ("heads5", 64, 64), ("out5", 16, 16),
]


def plan(names=None):
    at, b, t = {}, 0, 0
    for name, blocks, tiles in STREAM:
        if names is not None and name not in names:
            continue
        at[name] = Phase(b=b, t=t, blocks=blocks, tiles=tiles)
        b, t = b + blocks, t + tiles
    return at, b



def constants():
    p = np.arange(P)
    half, off = p // CH, p % CH
    same = (half[:, None] == half[None, :])
    row, col = off[:, None], off[None, :]
    c = {}
    c["ident"] = np.eye(P)
    c["ones"] = np.ones((P, P))
    c["headones"] = same * 1.0
    c["strict"] = same * (row < col)
    c["incl"] = (off[:, None] <= np.arange(CH)[None, :]) * 1.0
    c["mask1"] = same * (row < col) * (row // 2 == col // 2)
    for l in range(LEVELS):
        s = 4 << l
        c[f"level{l}"] = same * (row > col) * (row // s == col // s) * (row // (s // 2) != col // (s // 2))
    c["idstack"] = (off[:, None] == np.arange(CH)[None, :]) * 1.0
    c["zeros"] = np.zeros((P, CH))
    t = np.arange(T)
    for tt in range(TS):
        n = P * (tt + 1)
        q, k = (p + P * tt)[:, None], np.arange(n)[None, :]
        parts = []
        for window, dil in ((128, 1), (512, 4), (2048, 16)):
            d = q - k
            parts.append(np.where((d >= 0) & (d % dil == 0) & (d <= window), 0.0, MASKED))
        c[f"att{tt}"] = np.concatenate(parts, 1)
    rot = np.zeros((P, P))
    for i in range(16):
        rot[i + 16, i], rot[i, i + 16] = -1.0, 1.0
    c["rot16"] = rot
    rot = np.zeros((P, P))
    for base in (0, 64):
        for i in range(32):
            rot[base + i + 32, base + i], rot[base + i, base + i + 32] = -1.0, 1.0
    c["rotax"] = rot
    inv = (10000.0 ** (-np.arange(0, 64, 2, dtype=np.float32) / np.float32(64))).astype(np.float32)
    ang = np.zeros((P, T), np.float32)
    for i in range(P):
        pos = (t // 64 if i < 64 else t % 64).astype(np.float32)
        ang[i] = pos * inv[i % 32]
    c["axcos"], c["axsin"] = np.cos(ang), np.sin(ang)
    f = (500000.0 ** (-np.arange(0, 32, 2, dtype=np.float32) / np.float32(32))).astype(np.float32)
    c["invfreq"] = f[p % 16][:, None]
    c["poolcnt"] = np.tile(np.concatenate(
        [1.0 / np.minimum(t + 1, w) for w in (2, 4, 8, 16)]).astype(np.float32)[None, :], (P, 1))
    c["triu"] = np.where(p[:, None] <= p[None, :], 0.0, MASKED)
    c["tril"] = np.where(p[:, None] >= p[None, :], 0.0, MASKED)
    for name, v in (("eps", 1e-6), ("lneps", 64e-5), ("ln2_8", LN2_8), ("negdecay", -0.5 * DECAY),
                    ("one", 1.0), ("halfpi", float(np.pi / 2))):
        c[name] = np.full((P, 1), v)
    return {k: np.asarray(v, np.float32) for k, v in c.items()}


CONST = constants()
LATER = {"attention": ["att0", "att1", "rot16", "invfreq"], "pool": ["poolcnt"],
         "even": ["axcos", "axsin", "rotax"], "odd": ["triu", "tril"]}
RESIDENT = [k for k in CONST if not any(k in v for v in LATER.values())]


def place(names):
    where, w = {}, 0
    for k in names:
        where[k] = (w, CONST[k].shape[1])
        w += CONST[k].shape[1]
    return where, w


CONST_AT, NCONST = place(RESIDENT)
LATER_AT = {k: place(v)[0] for k, v in LATER.items()}
NLATER = {k: place(v)[1] for k, v in LATER.items()}

PARAMS = [("norm_w", 4 * KC), ("a_mu", 2 * 6 * KC), ("a_w0", 2 * KC), ("a_a0", 2 * KC), ("a_k_k", 2 * KC),
          ("a_k_a", 2 * KC), ("a_r_k", 2 * KC), ("a_lnx_w", 2 * KC), ("a_lnx_b", 2 * KC), ("a_v0", KC),
          ("b_qn_w", GROUPS), ("b_kn_w", GROUPS), ("c_scale", KC), ("norm_gain_2", 2 * KC),
          ("final_gain_2", KC), ("q_norm_gain_2", 1), ("k_norm_gain_2", 1), ("conv_w_2", 4 * 8),
          ("conv_b_2", 8), ("lru_ba_2", 16), ("lru_bx_2", 16), ("lru_lambda_2", 16),
          ("odd_norm_gain_2", KC), ("gate_bias", 2)]
PARAM_AT, _w = {}, 0
for _k, _v in PARAMS:
    PARAM_AT[_k] = _w
    _w += _v
NPARAM = _w


class Steps:

    def __init__(self, eng, sem):
        self.eng, self.sem, self.base, self.k, self.i, self.per = eng, sem, 0, 0, 0, 0

    def did(self, ins):
        ins.then_inc(self.sem, 1)
        self.k += 1

    def wait(self):
        self.eng.wait_ge(self.sem, self.base + self.k + (self.i * self.per if self.per else 0))

    def enter(self, i, per):
        self.base, self.k, self.i, self.per = self.base + self.k, 0, i, per

    def leave(self, turns):
        assert self.k == self.per, f"a turn has {self.k} steps, not {self.per}"
        self.base, self.k, self.i, self.per = self.base + self.per * turns, 0, 0, 0


PER = {"rwkv_scalar": 3, "rwkv_vector0": 19, "rwkv_vector1": 22}


def build(nc, a, phases=None, layers=(0, 1, 2, 3, 4, 5), final=True):
    at, nblocks = plan(phases)
    ctx = ExitStack()
    with ctx:
        def sb(name, shape, dt=F32):
            return ctx.enter_context(nc.sbuf_tensor(name, shape, dt))

        ARENA = 14700
        ring = sb("ring", [P, SLOTS, D])
        x = sb("x", [P, KC, T])
        obuf = sb("obuf", [P, KC, T])
        work = sb("work", [P, 4 * KC * T])
        arena = sb("arena", [P, ARENA])
        const = sb("consts", [P, NCONST])
        par = sb("params", [P, NPARAM])
        half = sb("half", [P, NPARAM])
        lora_w = sb("lora_w", [LORA, 3, P])
        rstd = sb("rstd", [P, T])
        lora_h = sb("lora_h", [LORA, 3, T])
        h = arena[:, 0:KC * (T + 1)].rearrange("p (k t) -> p k t", k=KC)
        HCOLS = KC * (T + 1)
        LATER0 = 4 * KC * T - max(NLATER.values())
        bank = [ctx.enter_context(nc.psum_tensor(f"bank{i}", [P, 512], F32)) for i in range(8)]
        v_first = nc.dram_tensor("v_first", [KC, P, T], F32).ap()

        def cst(name, rows=P):
            o, w = CONST_AT[name]
            return const[0:rows, o:o + w]

        def later(layer, name):
            o, w = LATER_AT[layer][name]
            return work[:, LATER0 + o:LATER0 + o + w]

        def pcol(name, i, tile=None):
            return (par if tile is None else tile)[:, bass.ds(PARAM_AT[name] + i, 1)]

        loaded = [ctx.enter_context(nc.semaphore(f"block_loaded{i}")) for i in range(SLOTS)]
        taken = [ctx.enter_context(nc.semaphore(f"tile_taken{i}")) for i in range(2)]
        names = (
            "tile_ready consts_loaded half_ready act_steps dve_steps out_stored later_loaded "
            "x_tiles squares norm_sum norm_rstd h_chunks o_tiles zeros_ready final_ready "
            "mixed_chunks xx_ready lora_h_ready lora_loaded "
            "lora_ps kk_ps bonus_ps tokA_ps tokB_ps tokK_ps tokV_ps s1_ps s2_ps xt_ps yl_ps zl_ps "
            "q0_ps gh_ps r2m_ps seq_ps pt_ps mean_ps var_ps "
            "ta_ready wdec_ready kraw_ready ksq_ready kinv_ready rraw_ready ssc_ready gt_ready gs_ready "
            "at_ready abd_ready bbd_ready kbd_ready v_ready vbd_ready ars_ready rkr_ready bon_ready k2_ready "
            "tok_act tok_dve vtok_ready atri_ready arb_ready ark_ready z_ready xt_ready ym_ready "
            "q0_act q0_dve gh_ready r2m_ready sbd_ready pbd_ready y_ready yc_ready ysq_ready yrstd_ready "
            "v_stored vf_loaded vt_ready "
            "qsq_ready qstat_ps qrs_ready qn_ready rot_ps rope_ready scores_ps smax_ready exp_ready probs_ready "
            "probt_ps probt_ready av_ready pv_ps ggate_ready agate_ready angles_ready tables_ready "
            "diff_ready pgate_tanh pgate_ready "
            "ksq2_ready kstat_ps krs_ready kn_ready krot_ps kv4_ready qsq4_ready vcur_ready "
            "lru_wait lam_ready lruw_loaded xl_ready xc_ready lru_ps lgate_tanh lgate_ready lrt_ready lr_ready la_ready "
            "lm_ready lsq_ready "
            "gates_dve gates_act gt_ps mh_ready mbc_ps mk_ready ms_ps me_ready "
            "mden_ps mv_ready mw_ready mpv_ps mhsq_ready mstat_ps mdn_ready mm2_ready mexp_ready mo_ready mhs_ready "
            "mrs_ready mz_ready mzs_ready").split()
        S = {n: ctx.enter_context(nc.semaphore(n)) for n in names}

        block = ctx.enter_context(nc.Block())

        def block_loaded(pe, b, turn=0, per=0):
            pe.wait_ge(loaded[b % SLOTS], turn * (16 * per // SLOTS) + 16 * (b // SLOTS + 1))

        def bank_free(pe, t, turn=0, per=0):
            if t >= 2 or per:
                pe.wait_ge(taken[t % 2], turn * (per // 2) + t // 2)

        def tile_done(eng, t, turn=0, per=0):
            eng.wait_ge(S["tile_ready"], turn * per + t + 1)

        def project(pe, rhs, b, t, turn=0, perb=0, pert=0, width=1, kc=KC):
            w = ring[:, b % SLOTS, :].rearrange("p (k n) -> p k n", k=kc)
            block_loaded(pe, b, turn, perb)
            for j in range(width):
                bank_free(pe, t + j, turn, pert)
                for k in range(kc):
                    ins = nc.tensor.matmul(bank[(t + j) % 2][:, 0:T], w[:, k, j * P:(j + 1) * P], rhs(k),
                                           start=(k == 0), stop=(k == kc - 1))
                ins.then_inc(S["tile_ready"], 1)

        def norm_scalar(act, c, n):
            sq = work[:, 0:KC * T].rearrange("p (q k t) -> p q k t", q=4, k=4)
            for q in range(4):
                if n > 0:
                    act.wait_ge(S["x_tiles"], KC * (n - 1) + 4 * (q + 1))
                nc.scalar.activation(sq[:, q], x[:, 4 * q:4 * q + 4, :], ACT.Square).then_inc(S["squares"], 1)
            act.wait_ge(S["norm_sum"], n + 1)
            c.did(nc.scalar.activation(rstd[:, :], bank[3][:, 0:T], ACT.Ln, bias=cst("eps"), scale=1.0 / D))
            c.wait()
            nc.scalar.activation(rstd[:, :], rstd[:, :], ACT.Exp, scale=-0.5).then_inc(S["norm_rstd"], 1)

        def norm_tensor(pe, n):
            sq = work[:, 0:KC * T].rearrange("p (k t) -> p k t", k=KC)
            for k in range(KC):
                if k % 4 == 0:
                    pe.wait_ge(S["squares"], 4 * n + k // 4 + 1)
                ins = nc.tensor.matmul(bank[3][:, 0:T], cst("ones"), sq[:, k, :], start=(k == 0), stop=(k == KC - 1))
            ins.then_inc(S["norm_sum"], 1)

        def norm_vector(dve, n, gain, first):
            dve.wait_ge(S["norm_rstd"], n + 1)
            nc.vector.memset(h[:, :, 0:1], 0.0)
            for k in range(KC):
                nc.vector.scalar_tensor_tensor(h[:, k, 1:T + 1], x[:, k, :], pcol(gain, first + k),
                                               rstd[:, :], ALU.mult, ALU.mult).then_inc(S["h_chunks"], 1)

        def out_tensor(pe, name, kc, o_needed):
            p = at[name]
            width = KC // kc
            pe.wait_ge(S["o_tiles"], o_needed)
            with pe.Fori(0, p.blocks // SLOTS) as i:
                for j in range(SLOTS):
                    project(pe, lambda k: obuf[:, k, :], p.b + j, p.t + j * width, i, SLOTS, SLOTS * width,
                            width=width, kc=kc)

        def out_vector(dve, name, n):
            p = at[name]
            with dve.Fori(0, KC // 2) as i:
                for j in range(2):
                    tile_done(dve, p.t + j, i, 2)
                    xc = x[:, bass.ds(2 * i + j, 1), :].rearrange("p a t -> p (a t)")
                    nc.vector.tensor_tensor(xc, bank[(p.t + j) % 2][:, 0:T], xc, ALU.add)\
                        .then_inc(S["x_tiles"], 1)
                    dve.wait_ge(S["x_tiles"], n * KC + 2 * i + j + 1)
                    dve.sem_inc(taken[(p.t + j) % 2], 1)

        mixed = [work[:, j * KC * T:(j + 1) * KC * T].rearrange("p (k t) -> p k t", k=KC) for j in range(4)]
        MU = {"r": 0, "k": 1, "v": 2, "g": 3, "w": 4, "a": 5}
        MIX_ORDER = "wavkrg"

        def mixed_count(m, L):
            return KC * (6 * L + MIX_ORDER.index(m) + 1)

        xx = arena[:, HCOLS:HCOLS + KC * T].rearrange("p (k t) -> p k t", k=KC)

        B, cur = {}, 0
        for name in "kraw ksq kkc kinv rraw vraw vf gs wdec asig bvec k2 rkr bon yc ysq".split():
            B[name] = arena[:, cur:cur + T]
            cur += T
        for name in "rd ars abd bbd kbd vbd atri ktri z xm ym vtok ghin rb rk gbd hbd r2m".split():
            B[name] = arena[:, cur:cur + 512].rearrange("p (u a c) -> p u a c", u=NU, a=2)
            cur += 512
        for name in ("wx", "sf"):
            B[name] = arena[:, cur:cur + NU * (CH + 1)].rearrange("p (u c) -> p u c", u=NU)
            cur += NU * (CH + 1)
        for name in ("at", "y"):
            B[name] = arena[:, cur:cur + T].rearrange("p (u c) -> p u c", u=NU)
            cur += T
        B["sbd"] = arena[:, cur:cur + P].rearrange("p (a c) -> p a c", a=2)
        B["pbd"] = arena[:, cur + P:cur + 2 * P]
        cur += 2 * P
        B["iwc"] = arena[:, cur:cur + NU]
        cur += NU
        assert cur <= ARENA, cur
        R = B

        def chunks(v):
            return v.rearrange("p (u c) -> p u c", u=NU)

        def flat(v):
            return v.rearrange("p u a c -> p (u a c)")

        def units(v):
            return v.rearrange("p u a c -> p u (a c)")

        def both(v):
            return v.unsqueeze(2).to_broadcast([P, NU, 2, CH])

        def mask4(name):
            return cst(name).rearrange("p (a c) -> p a c", a=2).unsqueeze(1).to_broadcast([P, NU, 2, CH])

        halves = [(slice(0, CH), 0), (slice(CH, P), 1)]

        def lora_tensor(pe, L):
            p = at[f"lora{3 * L}"]
            for j, (m, src) in enumerate([("w", obuf), ("a", mixed[3]), ("v", mixed[2])][:p.tiles]):
                pe.wait_ge(S["mixed_chunks"], mixed_count(m, L))
                project(pe, lambda k, src=src: src[:, k, :], p.b + j, p.t + j)

        def mix_vector(dve, c, L):
            dve.wait_ge(S["h_chunks"], KC * (NORM_OF[3 * L] + 1))
            nc.vector.tensor_tensor(xx, h[:, :, 0:T], h[:, :, 1:T + 1], ALU.subtract).then_inc(S["xx_ready"], 1)
            dve.wait_ge(S["xx_ready"], L + 1)
            p = at[f"lora{3 * L}"]
            for m, dst in (("w", obuf), ("a", mixed[3]), ("v", mixed[2]), ("k", mixed[0]), ("r", mixed[1]),
                           ("g", mixed[3])):
                if m == "g":
                    tile_done(dve, p.t + 1)
                for k in range(KC):
                    nc.vector.scalar_tensor_tensor(dst[:, k, :], xx[:, k, :], pcol("a_mu", (6 * L + MU[m]) * KC + k),
                                                   h[:, k, 1:T + 1], ALU.mult, ALU.add)\
                        .then_inc(S["mixed_chunks"], 1)

        def lora_scalar(act, L):
            p = at[f"lora{3 * L}"]
            for j in range(p.tiles):
                t = p.t + j
                rows = MVL if j == 2 else LORA
                tile_done(act, t)
                nc.scalar.activation(lora_h[0:rows, j, :], bank[t % 2][0:rows, 0:T], ACT.Tanh if j == 0 else ACT.Copy)\
                    .then_inc(S["lora_h_ready"], 1)
                act.wait_ge(S["lora_h_ready"], 2 * L + j + 1)
                act.sem_inc(taken[t % 2], 1)


        def group_tensor(pe, L, i, ng, ns, pb, pt, first, project_it, scan_it):
            made = [0]

            def gemm(count):
                for _ in range(count if project_it else 0):
                    q, k = divmod(made[0], KC)
                    if q == 4:
                        return
                    made[0] += 1
                    b, t = pb + q, pt + q
                    if k == 0:
                        block_loaded(pe, b, i, 4)
                        bank_free(pe, t, i, 4)
                        if first:
                            pe.wait_ge(S["mixed_chunks"], mixed_count("krvg"[q], L))
                    w = ring[:, b % SLOTS, :].rearrange("p (k n) -> p k n", k=KC)
                    ins = nc.tensor.matmul(bank[t % 2][:, 0:T], w[:, k, :], mixed[q][:, k, :],
                                           start=(k == 0), stop=(k == KC - 1))
                    if k == KC - 1:
                        if q == 2 and L:
                            ins = nc.tensor.matmul(bank[t % 2][:, T:2 * T], lora_w[0:MVL, 2, :],
                                                   lora_h[0:MVL, 2, :], start=True, stop=True)
                        ins.then_inc(S["tile_ready"], 1)

            def each(out_bank, lhs, rhs, sig):
                for u in range(NU):
                    ins = nc.tensor.matmul(bank[out_bank][:, u * P:(u + 1) * P], lhs[:, u, :], rhs[:, u, :],
                                           start=True, stop=True)
                ins.then_inc(sig, 1)

            def transposes(out_bank, src, sig):
                for u in range(NU):
                    ins = nc.tensor.transpose(bank[out_bank][:, u * P:(u + 1) * P], src[:, u, :], cst("ident"))
                ins.then_inc(sig, 1)

            def kk_norm():
                pe.wait_ge(S["ksq_ready"], ng)
                if scan_it:
                    pe.wait_ge(S["bon_ready"], ns)
                nc.tensor.matmul(bank[3][:, 0:T], cst("headones"), R["ksq"], start=True, stop=True)\
                    .then_inc(S["kk_ps"], 1)

            def lora():
                pe.wait_ge(S["lora_loaded"], 16 * ng)
                if first:
                    p = at[f"lora{3 * L}"]
                    pe.wait_ge(S["lora_h_ready"], [2, 5][L])
                if not (first and L == 0):
                    pe.wait_ge(S["wdec_ready"], ng - 1)
                nc.tensor.matmul(bank[2][:, 0:T], lora_w[:, 0, :], lora_h[:, 0, :], start=True, stop=True)
                nc.tensor.matmul(bank[2][:, T:2 * T], lora_w[:, 1, :], lora_h[:, 1, :], start=True, stop=True)\
                    .then_inc(S["lora_ps"], 1)

            ars, atri, ktri, z, xm, ym = (units(v) for v in (R["ars"], R["atri"], R["ktri"], R["z"], R["xm"], R["ym"]))
            vtok, ghin, rb, rk, gbd, hbd, r2m = (units(v) for v in (R["vtok"], R["ghin"], R["rb"], R["rk"], R["gbd"], R["hbd"], R["r2m"]))
            if not scan_it:
                lora()
                gemm(2 * KC)
                kk_norm()
                gemm(2 * KC)
                return
            pe.wait_ge(S["rkr_ready"], ns)
            nc.tensor.matmul(bank[3][:, 0:T], cst("headones"), R["rkr"], start=True, stop=True).then_inc(S["bonus_ps"], 1)
            pe.wait_ge(S["abd_ready"], ns)
            transposes(4, units(R["abd"]), S["tokA_ps"])
            pe.wait_ge(S["bbd_ready"], ns)
            transposes(5, units(R["bbd"]), S["tokB_ps"])
            pe.wait_ge(S["kbd_ready"], ns)
            if not (isinstance(ns, int) and ns == 1):
                pe.wait_ge(S["yrstd_ready"], ns - 1)
            transposes(6, units(R["kbd"]), S["tokK_ps"])
            pe.wait_ge(S["vbd_ready"], ns)
            transposes(7, units(R["vbd"]), S["tokV_ps"])
            gemm(3)
            pe.wait_ge(S["ars_ready"], ns)
            pe.wait_ge(S["tok_act"], 3 * ns - 2)
            pe.wait_ge(S["tok_dve"], 3 * ns - 2)
            each(4, units(R["bbd"]), ars, S["s1_ps"])
            gemm(2)
            pe.wait_ge(S["tok_act"], 3 * ns - 1)
            pe.wait_ge(S["tok_dve"], 3 * ns - 1)
            each(5, units(R["kbd"]), ars, S["s2_ps"])
            gemm(2)
            pe.wait_ge(S["tok_act"], 3 * ns)
            pe.wait_ge(S["tok_dve"], 3 * ns)
            pe.wait_ge(S["z_ready"], (LEVELS + 1) * ns - LEVELS)
            transposes(6, z, S["xt_ps"])
            if project_it:
                lora()
            pe.wait_ge(S["vtok_ready"], ns)
            pe.wait_ge(S["arb_ready"], ns)
            for l in range(LEVELS):
                gemm(3)
                if project_it and l == 3:
                    kk_norm()
                pe.wait_ge(S["xt_ready"], LEVELS * ns - LEVELS + 1 + l)
                each(7, atri, xm, S["yl_ps"])
                gemm(2)
                pe.wait_ge(S["ym_ready"], LEVELS * ns - LEVELS + 1 + l)
                each(4, ym, z, S["zl_ps"])
                gemm(2)
                if l == 0:
                    pe.wait_ge(S["ark_ready"], ns)
                    each(5, ktri, vtok, S["q0_ps"])
                pe.wait_ge(S["z_ready"], (LEVELS + 1) * ns - LEVELS + 1 + l)
                if l < LEVELS - 1:
                    transposes(6, z, S["xt_ps"])
            pe.wait_ge(S["q0_act"], ns)
            pe.wait_ge(S["q0_dve"], ns)
            each(7, z, ghin, S["gh_ps"])
            gemm(3)
            pe.wait_ge(S["gh_ready"], ns)
            each(4, gbd, rb, S["r2m_ps"])
            for u in range(NU):
                o = bank[5 + u % 2][:, 0:P]
                if u >= 2:
                    pe.wait_ge(S["y_ready"], NU * ns - NU + u - 1)
                nc.tensor.matmul(o, hbd[:, u, :], rb[:, u, :], start=True, stop=False)
                ins = nc.tensor.matmul(o, vtok[:, u, :], rk[:, u, :], start=False, stop=(u == 0))
                gemm(2)
                if u:
                    if u == 1:
                        pe.wait_ge(S["r2m_ready"], ns)
                    pe.wait_ge(S["pbd_ready"], (NU - 1) * ns - NU + 1 + u)
                    ins = nc.tensor.matmul(o, R["pbd"], r2m[:, u, :], start=False, stop=True)
                ins.then_inc(S["seq_ps"], 1)
                gemm(2)
                if u < NU - 1:
                    pe.wait_ge(S["sbd_ready"], (NU - 1) * ns - NU + 2 + u)
                    nc.tensor.transpose(bank[7][:, 0:P], R["sbd"].rearrange("p a c -> p (a c)"), cst("ident"))\
                        .then_inc(S["pt_ps"], 1)
            gemm(2)
            pe.wait_ge(S["y_ready"], NU * ns)
            nc.tensor.matmul(bank[6][:, 0:T], cst("headones"), R["y"].rearrange("p u c -> p (u c)"),
                             start=True, stop=True).then_inc(S["mean_ps"], 1)
            gemm(3)
            pe.wait_ge(S["ysq_ready"], ns)
            nc.tensor.matmul(bank[6][:, 0:T], cst("headones"), R["ysq"], start=True, stop=True).then_inc(S["var_ps"], 1)
            gemm(4 * KC)

        def release(eng, sig, n, t):
            eng.wait_ge(sig, n)
            eng.sem_inc(taken[t % 2], 1)

        def group_scalar(act, c, L, i, ng, ns, jg, js, pt, first, project_it, scan_it):
            def half_rows(dst, b, ps, sig):
                rows, _ = halves[0]
                act.wait_ge(ps, ns)
                nc.scalar.copy(dst[rows], bank[b][rows, :].rearrange("p (u a c) -> p u a c", u=NU, a=2)[:, :, 0, :])\
                    .then_inc(sig, 1)

            def lora():
                if not (first and L == 0):
                    act.wait_ge(S["k2_ready"], ng - 1)
                act.wait_ge(S["lora_ps"], ng)
                nc.scalar.activation(R["asig"], bank[2][:, T:2 * T], ACT.Tanh, bias=pcol("a_a0", L * KC + jg, half),
                                     scale=0.5).then_inc(S["ta_ready"], 1)
                c.did(nc.scalar.activation(R["wdec"], bank[2][:, 0:T], ACT.Tanh, bias=pcol("a_w0", L * KC + jg, half),
                                           scale=0.5))
                c.wait()
                nc.scalar.activation(R["wdec"], R["wdec"], ACT.Exp, bias=cst("negdecay"), scale=-0.5 * DECAY)\
                    .then_inc(S["wdec_ready"], 1)

            def k_tile():
                tile_done(act, pt, i, 4)
                if not (first and L == 0):
                    act.wait_ge(S["k2_ready"], ng - 1)
                nc.scalar.copy(R["kraw"], bank[pt % 2][:, 0:T]).then_inc(S["kraw_ready"], 1)
                release(act, S["kraw_ready"], ng, pt)
                nc.scalar.activation(R["ksq"], R["kraw"], ACT.Square, scale=pcol("a_k_k", L * KC + jg))\
                    .then_inc(S["ksq_ready"], 1)

            def r_tile():
                act.wait_ge(S["ssc_ready"], ng)
                c.did(nc.scalar.activation(R["kinv"], R["kinv"], ACT.Ln, scale=65536.0))
                c.wait()
                nc.scalar.activation(R["kinv"], R["kinv"], ACT.Exp, bias=cst("ln2_8"), scale=-0.5).then_inc(S["kinv_ready"], 1)
                tile_done(act, pt + 1, i, 4)
                nc.scalar.copy(R["rraw"], bank[(pt + 1) % 2][:, 0:T]).then_inc(S["rraw_ready"], 1)
                release(act, S["rraw_ready"], ng, pt + 1)
                act.wait_ge(S["at_ready"], ng)
                for rows, blk in halves:
                    ins = nc.scalar.copy(R["abd"][rows, :, blk, :], R["at"][rows])
                ins.then_inc(S["abd_ready"], 1)

            if scan_it:
                half_rows(R["ghin"][:, :, 0, :], 4, S["tokA_ps"], S["tok_act"])
                half_rows(R["rb"][:, :, 1, :], 5, S["tokB_ps"], S["tok_act"])
                half_rows(R["rk"][:, :, 1, :], 6, S["tokK_ps"], S["tok_act"])
                act.wait_ge(S["tokV_ps"], ns)
                nc.scalar.copy(flat(R["vtok"]), bank[7][:, :]).then_inc(S["vtok_ready"], 1)
                for l in range(LEVELS):
                    act.wait_ge(S["xt_ps"], LEVELS * ns - LEVELS + 1 + l)
                    nc.scalar.copy(flat(R["xm"]), bank[6][:, :]).then_inc(S["xt_ready"], 1)
                    if project_it and l == 0:
                        lora()
                    if l == 1:
                        half_rows(R["ghin"][:, :, 1, :], 5, S["q0_ps"], S["q0_act"])
                    if project_it and l == 2:
                        k_tile()
            else:
                lora()
                k_tile()
            if project_it:
                r_tile()
            if scan_it:
                for u in range(NU - 1):
                    act.wait_ge(S["pt_ps"], (NU - 1) * ns - NU + 2 + u)
                    nc.scalar.copy(R["pbd"], bank[7][:, 0:P]).then_inc(S["pbd_ready"], 1)
                act.wait_ge(S["yc_ready"], ns)
                nc.scalar.activation(R["ysq"], R["yc"], ACT.Square).then_inc(S["ysq_ready"], 1)
                act.wait_ge(S["var_ps"], ns)
                c.did(nc.scalar.activation(R["ysq"], bank[6][:, 0:T], ACT.Ln, bias=cst("lneps"), scale=1.0 / CH))
                c.wait()
                nc.scalar.activation(R["ysq"], R["ysq"], ACT.Exp, scale=-0.5).then_inc(S["yrstd_ready"], 1)
            if project_it:
                tv = pt + 2
                tile_done(act, tv, i, 4)
                if L == 0:
                    if scan_it:
                        act.wait_ge(S["bon_ready"], ns)
                        act.wait_ge(S["v_stored"], 16 * ns)
                    nc.scalar.copy(R["vraw"], bank[tv % 2][:, 0:T]).then_inc(S["v_ready"], 1)
                    release(act, S["v_ready"], ng, tv)
                else:
                    nc.scalar.activation(R["kinv"], bank[tv % 2][:, T:2 * T], ACT.Tanh, bias=pcol("a_v0", jg, half),
                                         scale=0.5).then_inc(S["vt_ready"], 1)
                    act.wait_ge(S["v_ready"], ng)
                for rows, blk in halves:
                    ins = nc.scalar.copy(R["vbd"][rows, :, blk, :], chunks(R["vraw"])[rows])
                ins.then_inc(S["vbd_ready"], 1)
                tile_done(act, pt + 3, i, 4)
                if scan_it:
                    act.wait_ge(S["o_tiles"], O_BEFORE[3 * L] + jg)
                nc.scalar.activation(R["gs"], bank[(pt + 3) % 2][:, 0:T], ACT.Tanh, scale=0.5).then_inc(S["gt_ready"], 1)

        def group_vector(dve, c, L, i, ng, ns, jg, js, pt, first, project_it, scan_it):
            def half_rows(dst, b, ps, sig):
                rows, _ = halves[1]
                dve.wait_ge(ps, ns)
                nc.vector.tensor_copy(dst[rows], bank[b][rows, :].rearrange("p (u a c) -> p u a c", u=NU, a=2)[:, :, 1, :])\
                    .then_inc(sig, 1)

            def psum4(b):
                return bank[b][:, :].rearrange("p (u a c) -> p u a c", u=NU, a=2)

            def decays():
                dve.wait_ge(S["ta_ready"], ng)
                c.did(nc.vector.tensor_scalar(R["asig"], R["asig"], 0.5, 0.5, ALU.mult, ALU.add))
                dve.wait_ge(S["wdec_ready"], ng)
                w = chunks(R["wdec"])
                for u in range(NU):
                    c.did(nc.vector.tensor_tensor_scan(R["wx"][:, u, 1:CH + 1], w[:, u, :], cst("zeros"), 1.0,
                                                       ALU.mult, ALU.add))
                    c.did(nc.vector.tensor_tensor_scan(R["sf"][:, u, CH - 1::-1], w[:, u, ::-1], cst("zeros"), 1.0,
                                                       ALU.mult, ALU.add))
                c.wait()
                c.did(nc.vector.reciprocal(R["iwc"], R["wx"][:, :, CH]))

            def kk_floor():
                dve.wait_ge(S["kk_ps"], ng)
                nc.vector.tensor_scalar(R["kinv"], bank[3][:, 0:T], 1e-24, None, ALU.max).then_inc(S["ssc_ready"], 1)

            def prep_a():
                dve.wait_ge(S["kinv_ready"], ng)
                c.did(nc.vector.scalar_tensor_tensor(R["kkc"], R["kraw"], pcol("a_k_k", L * KC + jg), R["kinv"],
                                                     ALU.mult, ALU.mult))
                c.wait()
                nc.vector.scalar_tensor_tensor(R["at"], R["wx"][:, :, 0:CH], -1.0, chunks(R["kkc"]), ALU.mult, ALU.mult)\
                    .then_inc(S["at_ready"], 1)

            def prep_bk():
                c.did(nc.vector.tensor_tensor(R["bvec"], R["kkc"], R["asig"], ALU.mult))
                c.did(nc.vector.tensor_scalar(R["k2"], R["asig"], 1.0, pcol("a_k_a", L * KC + jg), ALU.subtract, ALU.mult))
                c.wait()
                nc.vector.scalar_tensor_tensor(R["k2"], R["k2"], 1.0, R["kraw"], ALU.add, ALU.mult).then_inc(S["k2_ready"], 1)
                for rows, blk in halves:
                    ins = nc.vector.tensor_tensor(R["bbd"][rows, :, blk, :], chunks(R["bvec"])[rows], R["sf"][rows, :, 1:CH + 1],
                                                  ALU.mult)
                ins.then_inc(S["bbd_ready"], 1)
                dve.wait_ge(S["k2_ready"], ng)
                for rows, blk in halves:
                    ins = nc.vector.tensor_tensor(R["kbd"][rows, :, blk, :], chunks(R["k2"])[rows], R["sf"][rows, :, 1:CH + 1],
                                                  ALU.mult)
                ins.then_inc(S["kbd_ready"], 1)

            def prep_r():
                dve.wait_ge(S["rraw_ready"], ng)
                nc.vector.scalar_tensor_tensor(R["rkr"], R["rraw"], pcol("a_r_k", L * KC + jg), R["k2"], ALU.mult, ALU.mult)\
                    .then_inc(S["rkr_ready"], 1)
                c.did(nc.vector.tensor_tensor(R["rd"][:, :, 0, :], R["wx"][:, :, 1:CH + 1], chunks(R["rraw"]), ALU.mult))
                c.did(nc.vector.tensor_tensor(R["rd"][:, :, 1, :], cst("idstack").unsqueeze(1).to_broadcast([P, NU, CH]),
                                              R["wx"][:, :, CH:CH + 1].to_broadcast([P, NU, CH]), ALU.mult))
                dve.wait_ge(S["at_ready"], ng)
                inv = R["iwc"].unsqueeze(2).to_broadcast([P, NU, CH])
                nc.vector.tensor_tensor(R["ars"][:, :, 0, :], R["at"], inv, ALU.mult)
                c.wait()
                nc.vector.tensor_tensor(R["ars"][:, :, 1, :], R["rd"][:, :, 0, :], inv, ALU.mult).then_inc(S["ars_ready"], 1)

            if scan_it:
                dve.wait_ge(S["bonus_ps"], ns)
                nc.vector.tensor_tensor(R["bon"], bank[3][:, 0:T], R["vraw"], ALU.mult).then_inc(S["bon_ready"], 1)
                half_rows(R["ghin"][:, :, 0, :], 4, S["tokA_ps"], S["tok_dve"])
                half_rows(R["rb"][:, :, 1, :], 5, S["tokB_ps"], S["tok_dve"])
                half_rows(R["rk"][:, :, 1, :], 6, S["tokK_ps"], S["tok_dve"])
                dve.wait_ge(S["s1_ps"], ns)
                nc.vector.tensor_tensor(R["atri"], both(psum4(4)[:, :, 0, :]), mask4("strict"), ALU.mult)\
                    .then_inc(S["atri_ready"], 1)
                nc.vector.tensor_tensor(R["rb"][:, :, 0, :], psum4(4)[:, :, 1, :],
                                        cst("incl").unsqueeze(1).to_broadcast([P, NU, CH]), ALU.mult)\
                    .then_inc(S["arb_ready"], 1)
                dve.wait_ge(S["atri_ready"], ns)
                c.did(nc.vector.tensor_tensor(R["z"], R["atri"], mask4("mask1"), ALU.mult))
                c.wait()
                nc.vector.tensor_tensor(R["z"], R["z"], mask4("ident"), ALU.add).then_inc(S["z_ready"], 1)
                dve.wait_ge(S["s2_ps"], ns)
                nc.vector.tensor_tensor(R["ktri"], both(psum4(5)[:, :, 0, :]), mask4("strict"), ALU.mult)
                nc.vector.tensor_tensor(R["rk"][:, :, 0, :], psum4(5)[:, :, 1, :],
                                        cst("incl").unsqueeze(1).to_broadcast([P, NU, CH]), ALU.mult)\
                    .then_inc(S["ark_ready"], 1)
                for l in range(LEVELS):
                    dve.wait_ge(S["yl_ps"], LEVELS * ns - LEVELS + 1 + l)
                    nc.vector.tensor_tensor(R["ym"], psum4(7), mask4(f"level{l}"), ALU.mult).then_inc(S["ym_ready"], 1)
                    if project_it and l == 0:
                        decays()
                    if l == 1:
                        half_rows(R["ghin"][:, :, 1, :], 5, S["q0_ps"], S["q0_dve"])
                    dve.wait_ge(S["zl_ps"], LEVELS * ns - LEVELS + 1 + l)
                    dve.wait_ge(S["z_ready"], (LEVELS + 1) * ns - LEVELS + l)
                    nc.vector.tensor_tensor(R["z"], psum4(4), R["z"], ALU.add).then_inc(S["z_ready"], 1)
                    if project_it and l == 3:
                        kk_floor()
                dve.wait_ge(S["gh_ps"], ns)
                nc.vector.tensor_tensor(R["gbd"], both(psum4(7)[:, :, 0, :]), mask4("headones"), ALU.mult)
                nc.vector.tensor_tensor(R["hbd"], both(psum4(7)[:, :, 1, :]), mask4("headones"), ALU.mult)\
                    .then_inc(S["gh_ready"], 1)
            else:
                decays()
                kk_floor()
            if project_it:
                prep_a()
            if scan_it:
                dve.wait_ge(S["r2m_ps"], ns)
                nc.vector.tensor_tensor(R["r2m"], psum4(4), R["rd"], ALU.add).then_inc(S["r2m_ready"], 1)
                for u in range(NU):
                    dve.wait_ge(S["seq_ps"], NU * ns - NU + 1 + u)
                    o = bank[5 + u % 2]
                    if u < NU - 1:
                        nc.vector.tensor_tensor(R["sbd"], o[:, CH:P].unsqueeze(1).to_broadcast([P, 2, CH]),
                                                cst("headones").rearrange("p (a c) -> p a c", a=2), ALU.mult)\
                            .then_inc(S["sbd_ready"], 1)
                    nc.vector.tensor_copy(R["y"][:, u, :], o[:, 0:CH]).then_inc(S["y_ready"], 1)
                    if project_it and u == 0:
                        prep_bk()
            elif project_it:
                prep_bk()
            if scan_it:
                dve.wait_ge(S["mean_ps"], ns)
                dve.wait_ge(S["y_ready"], NU * ns)
                nc.vector.scalar_tensor_tensor(R["yc"], bank[6][:, 0:T], -1.0 / CH, R["y"].rearrange("p u c -> p (u c)"),
                                               ALU.mult, ALU.add).then_inc(S["yc_ready"], 1)
            if project_it:
                prep_r()
            if scan_it:
                dve.wait_ge(S["yrstd_ready"], ns)
                dve.wait_ge(S["yc_ready"], ns)
                c.did(nc.vector.tensor_tensor(R["yc"], R["yc"], R["ysq"], ALU.mult))
                c.wait()
                c.did(nc.vector.tensor_scalar(R["yc"], R["yc"], pcol("a_lnx_w", L * KC + js), pcol("a_lnx_b", L * KC + js),
                                              ALU.mult, ALU.add))
                c.wait()
                dve.wait_ge(S["bon_ready"], ns)
                c.did(nc.vector.tensor_tensor(R["yc"], R["yc"], R["bon"], ALU.add))
                c.wait()
                dve.wait_ge(S["gs_ready"], ns)
                nc.vector.scalar_tensor_tensor(obuf[:, bass.ds(js, 1), :].rearrange("p a t -> p (a t)"), R["yc"], 0.5,
                                               R["gs"], ALU.mult, ALU.mult).then_inc(S["o_tiles"], 1)
            if project_it:
                if L:
                    tv = bank[(pt + 2) % 2][:, 0:T]
                    dve.wait_ge(S["vt_ready"], ng - KC)
                    c.did(nc.vector.tensor_scalar(R["kinv"], R["kinv"], 0.5, 0.5, ALU.mult, ALU.add))
                    dve.wait_ge(S["vf_loaded"], 16 * (ng - KC))
                    c.did(nc.vector.scalar_tensor_tensor(R["vf"], tv, -1.0, R["vf"], ALU.mult, ALU.add))
                    c.wait()
                    c.did(nc.vector.tensor_tensor(R["vf"], R["vf"], R["kinv"], ALU.mult))
                    c.wait()
                    nc.vector.tensor_tensor(R["vraw"], tv, R["vf"], ALU.add).then_inc(S["v_ready"], 1)
                    release(dve, S["v_ready"], ng, pt + 2)
                dve.wait_ge(S["gt_ready"], ng)
                nc.vector.scalar_tensor_tensor(R["gs"], R["gs"], 1.0, bank[(pt + 3) % 2][:, 0:T], ALU.add, ALU.mult)\
                    .then_inc(S["gs_ready"], 1)
                release(dve, S["gs_ready"], ng, pt + 3)

        def groups(L, eng, run, c=None, per=0):
            p, base = at[f"rwkv{3 * L}"], KC * L
            run(0, base + 1, base, 0, -1, p.b, p.t, True, True, False)
            with eng.Fori(0, KC - 1) as i:
                if c:
                    c.enter(i, per)
                run(i, i + (base + 2), i + (base + 1), i + 1, i, p.b + 4, p.t + 4, False, True, True)
            if c:
                c.leave(KC - 1)
            run(0, base + KC + 1, base + KC, KC, KC - 1, 0, 0, False, False, True)

        def rwkv_tensor(pe, L, n):
            norm_tensor(pe, n)
            lora_tensor(pe, L)
            groups(L, pe, lambda i, ng, ns, jg, js, pb, pt, first, pr, sc:
                   group_tensor(pe, L, i, ng, ns, pb, pt, first, pr, sc))
            out_tensor(pe, f"out{3 * L}", KC, O_BEFORE[3 * L] + KC)

        def rwkv_scalar(act, c, L, n):
            norm_scalar(act, c, n)
            lora_scalar(act, L)
            act.wait_ge(S["zeros_ready"], L + 1)
            groups(L, act, lambda i, ng, ns, jg, js, pb, pt, first, pr, sc:
                   group_scalar(act, c, L, i, ng, ns, jg, js, pt, first, pr, sc), c, PER["rwkv_scalar"])

        def rwkv_vector(dve, c, L, n):
            norm_vector(dve, n, "norm_w", 3 * L * KC)
            mix_vector(dve, c, L)
            dve.wait_ge(S["mixed_chunks"], mixed_count("g", L))
            for v in (R["abd"], R["bbd"], R["kbd"], R["vbd"]):
                nc.vector.memset(flat(v), 0.0)
            nc.vector.memset(R["wx"][:, :, 0:1], 1.0)
            nc.vector.memset(R["sf"][:, :, CH:CH + 1], 1.0).then_inc(S["zeros_ready"], 1)
            dve.wait_ge(S["zeros_ready"], L + 1)
            groups(L, dve, lambda i, ng, ns, jg, js, pb, pt, first, pr, sc:
                   group_vector(dve, c, L, i, ng, ns, jg, js, pt, first, pr, sc), c, PER[f"rwkv_vector{L}"])
            out_vector(dve, f"out{3 * L}", n)
            if L == 0:
                dve.wait_ge(S["v_stored"], 16 * KC)

        def rwkv_gpsimd(pool, L):
            base = KC * L

            def one(j, n, first):
                if not (first and L == 0):
                    pool.wait_ge(S["lora_ps"], n - 1)
                    if L:
                        pool.wait_ge(S["v_ready"], n - 1)
                pool.dma_start(lora_w[:, :, :], a["lora2"][L, bass.ds(j, 1)].rearrange("a p s n -> p (a s) n"))\
                    .then_inc(S["lora_loaded"], 16)
                if L:
                    if first:
                        pool.wait_ge(S["zeros_ready"], L + 1)
                    pool.dma_start(R["vf"], v_first[bass.ds(j, 1)].rearrange("a p t -> p (a t)")).then_inc(S["vf_loaded"], 16)
                else:
                    pool.wait_ge(S["v_ready"], n)
                    pool.dma_start(v_first[bass.ds(j, 1)].rearrange("a p t -> p (a t)"), R["vraw"])\
                        .then_inc(S["v_stored"], 16)

            one(0, base + 1, True)
            with pool.Fori(0, KC - 1) as i:
                one(i + 1, i + (base + 2), False)
            if L == 0:
                pool.wait_ge(S["v_stored"], 16 * KC)

        def final_scalar(act, c, n):
            norm_scalar(act, c, n)
            act.wait_ge(S["final_ready"], 1)
            act.dma_start(a["out"], obuf[:, :, :]).then_inc(S["out_stored"], 16)
            act.wait_ge(S["out_stored"], 16)

        def final_vector(dve, c, n):
            dve.wait_ge(S["norm_rstd"], n + 1)
            for k in range(KC):
                ins = nc.vector.scalar_tensor_tensor(obuf[:, k, :], x[:, k, :], pcol("final_gain_2", k),
                                                     rstd[:, :], ALU.mult, ALU.mult)
            ins.then_inc(S["final_ready"], 1)

        def heads(eng, p, base, run, tail, c=None, per=0):
            nb, nt = p.blocks // HEADS, p.tiles // HEADS
            for hh in range(2):
                run(0, base + hh + 1, hh, p.b + hh * nb, p.t + hh * nt, hh == 0)
            with eng.Fori(0, HEADS // 2 - 1) as i:
                if c:
                    c.enter(i, per)
                for hh in range(2):
                    run(i, i * 2 + (base + hh + 3), i * 2 + (hh + 2), p.b + (hh + 2) * nb, p.t + (hh + 2) * nt, False)
            if c:
                c.leave(HEADS // 2 - 1)
            if tail:
                tail(base + HEADS + 1, HEADS)

        def token_tile(pe, b, t, turn=0, perb=0, pert=0):
            w = ring[:, b % SLOTS, :].rearrange("p (k n) -> p k n", k=KC)
            block_loaded(pe, b, turn, perb)
            bank_free(pe, t, turn, pert)
            for tt in range(TS):
                for k in range(KC):
                    ins = nc.tensor.matmul(bank[t % 2][:, tt * P:(tt + 1) * P], h[:, k, 1 + tt * P:1 + (tt + 1) * P],
                                           w[:, k, :], start=(k == 0), stop=(k == KC - 1))
            ins.then_inc(S["tile_ready"], 1)

        def hk(k):
            return h[:, k, 1:T + 1]

        def bank_now_free(eng, t, turn=0, per=0):
            eng.wait_ge(taken[t % 2], turn * (per // 2) + t // 2 + 1)

        def wcarve(at0, sizes):
            out = {}
            for name, dims in sizes.items():
                n = int(np.prod(dims))
                v = work[:, at0:at0 + n]
                if len(dims) > 1:
                    names = "abcd"[:len(dims)]
                    v = v.rearrange("p (" + " ".join(names) + ") -> p " + " ".join(names), **dict(zip(names, dims)))
                out[name] = v
                at0 += n
            assert at0 <= LATER0, at0
            return out

        NQ = 2 * GROUPS
        NS = [GROUPS * P, GROUPS * T]
        NB = 3 * GROUPS
        Q = wcarve(KC * T, dict(qk=(NQ, T), sq=(NQ, T), rs=(NQ, T), t1=(NQ, T), v=(GROUPS, T), sc=(NS[0] + NS[1],),
                                pt=(NB, P), gs=(T,), cos=(T,), sin=(T,), pos=(T,), mx=(TS,), sum=(TS,), inv=(TS,)))
        ATT_SCALE = float(P) ** -0.5
        span = [slice(0, NS[0]), slice(NS[0], NS[0] + NS[1])]

        def att_tensor(pe, n):
            norm_tensor(pe, n)
            p = at["heads1"]
            base = HEAD_BASE[1]

            def finish(n):
                pe.wait_ge(S["probs_ready"], n)
                for g in range(GROUPS):
                    for j, src in ((2 * g, slice(g * P, (g + 1) * P)),
                                   (2 * g + 1, slice(NS[0] + g * T, NS[0] + g * T + P)),
                                   (2 * GROUPS + g, slice(NS[0] + g * T + P, NS[0] + (g + 1) * T))):
                        ins = nc.tensor.transpose(bank[2 + j // 4][:, (j % 4) * P:(j % 4 + 1) * P], Q["sc"][:, src],
                                                  cst("ident"))
                ins.then_inc(S["probt_ps"], 1)
                pe.wait_ge(S["probt_ready"], n)
                pe.wait_ge(S["av_ready"], GROUPS * n)
                for g in range(GROUPS):
                    nc.tensor.matmul(bank[5][:, 0:T], Q["v"][:, g, 0:P], Q["pt"][:, 2 * g:2 * g + 2, :],
                                     start=(g == 0), stop=False)
                for g in range(GROUPS):
                    ins = nc.tensor.matmul(bank[5][:, P:T], Q["v"][:, g, P:T], Q["pt"][:, 2 * GROUPS + g, :],
                                           start=False, stop=(g == GROUPS - 1))
                ins.then_inc(S["pv_ps"], 1)

            def run(i, n, hh, b, t, first):
                if first:
                    pe.wait_ge(S["h_chunks"], KC * (NORM_OF[1] + 1))
                for j in range(NQ):
                    project(pe, hk, b + j, t + j, i, 20, 20)
                if not first:
                    finish(n - 1)
                pe.wait_ge(S["qsq_ready"], NQ * n)
                for j in range(GROUPS):
                    ins = nc.tensor.matmul(bank[2 + j][:, :], cst("ones"), Q["sq"][:, 2 * j:2 * j + 2, :],
                                           start=True, stop=True)
                ins.then_inc(S["qstat_ps"], 1)
                token_tile(pe, b + 6, t + 6, i, 20, 20)
                pe.wait_ge(S["qn_ready"], n)
                for j in range(GROUPS):
                    ins = nc.tensor.matmul(bank[2 + j][:, :], later("attention", "rot16"),
                                           Q["qk"][:, 2 * j:2 * j + 2, :], start=True, stop=True)
                ins.then_inc(S["rot_ps"], 1)
                token_tile(pe, b + 7, t + 7, i, 20, 20)
                pe.wait_ge(S["rope_ready"], n)
                if not first:
                    pe.wait_ge(S["o_tiles"], O_BEFORE[1] + (n - base - 1))
                for g in range(GROUPS):
                    nc.tensor.matmul(bank[5][:, g * P:(g + 1) * P], Q["qk"][:, g, 0:P], Q["qk"][:, GROUPS + g, 0:P],
                                     start=True, stop=True)
                for g in range(GROUPS):
                    o = bank[6][:, g * T:(g + 1) * T] if g < 2 else bank[7][:, 0:T]
                    ins = nc.tensor.matmul(o, Q["qk"][:, g, P:T], Q["qk"][:, GROUPS + g, :], start=True, stop=True)
                ins.then_inc(S["scores_ps"], 1)
                token_tile(pe, b + 8, t + 8, i, 20, 20)
                project(pe, hk, b + 9, t + 9, i, 20, 20)

            heads(pe, p, base, run, lambda n, hh: finish(n - 1))
            out_tensor(pe, "out1", HEADS, O_BEFORE[1] + HEADS)

        def att_scalar(act, c, n):
            norm_scalar(act, c, n)
            p = at["heads1"]
            base = HEAD_BASE[1]

            act.wait_ge(S["angles_ready"], 1)
            nc.scalar.activation(Q["sin"][0:32], Q["sin"][0:32], ACT.Sin)
            nc.scalar.activation(Q["cos"][0:32], Q["cos"][0:32], ACT.Sin).then_inc(S["tables_ready"], 1)

            def finish(n):
                act.wait_ge(S["probt_ps"], n)
                for j, m in ((0, 4), (1, 4), (2, 1)):
                    ins = nc.scalar.copy(Q["pt"][:, 4 * j:4 * j + m, :],
                                         bank[2 + j][:, 0:m * P].rearrange("p (a b) -> p a b", a=m))
                ins.then_inc(S["probt_ready"], 1)

            def run(i, n, hh, b, t, first):
                for j in range(NQ):
                    tile_done(act, t + j, i, 20)
                    if not first and j == 0:
                        act.wait_ge(S["scores_ps"], n - 1)
                    nc.scalar.copy(Q["qk"][:, j, :], bank[(t + j) % 2][:, 0:T]).then_inc(taken[(t + j) % 2], 1)
                    bank_now_free(act, t + j, i, 20)
                    nc.scalar.activation(Q["sq"][:, j, :], Q["qk"][:, j, :], ACT.Square).then_inc(S["qsq_ready"], 1)
                if not first:
                    finish(n - 1)
                act.wait_ge(S["qstat_ps"], n)
                for j in range(GROUPS):
                    ins = nc.scalar.activation(Q["rs"][:, 2 * j:2 * j + 2, :],
                                               bank[2 + j][:, :].rearrange("p (a b) -> p a b", a=2), ACT.Ln,
                                               bias=cst("eps"), scale=1.0 / P)
                c.did(ins)
                c.wait()
                nc.scalar.activation(Q["rs"], Q["rs"], ACT.Exp, scale=-0.5).then_inc(S["qrs_ready"], 1)
                for g in range(GROUPS):
                    tt = t + NQ + g
                    tile_done(act, tt, i, 20)
                    nc.scalar.copy(Q["v"][:, g, :], bank[tt % 2][:, 0:T]).then_inc(S["av_ready"], 1)
                    act.wait_ge(S["av_ready"], GROUPS * n - GROUPS + g + 1)
                    act.sem_inc(taken[tt % 2], 1)
                act.wait_ge(S["smax_ready"], n)
                for tt in range(TS):
                    ins = nc.scalar.activation(Q["sc"][:, span[tt]], Q["sc"][:, span[tt]], ACT.Exp, bias=Q["mx"][:, tt:tt + 1],
                                               accum_out=Q["sum"][:, tt:tt + 1])
                ins.then_inc(S["exp_ready"], 1)
                tile_done(act, t + 9, i, 20)
                nc.scalar.activation(Q["gs"], bank[(t + 9) % 2][:, 0:T], ACT.Tanh, scale=0.5).then_inc(S["ggate_ready"], 1)

            heads(act, p, base, run, lambda n, hh: finish(n - 1), c, 2)

        def att_vector(dve, c, n):
            norm_vector(dve, n, "norm_w", KC)
            p = at["heads1"]
            base = HEAD_BASE[1]
            two_pi = 2 * np.pi
            c1 = 6.28125
            c2 = float(np.float32(np.floor((two_pi - c1) * 2 ** 20) / 2 ** 20))
            c3 = float(np.float32(two_pi - c1 - c2))
            r, k = Q["sin"][0:32], Q["cos"][0:32]
            dve.wait_ge(S["later_loaded"], LATER_COUNT[1])
            posi = Q["pos"][0:32].bitcast(I32)

            def step(ins):
                c.did(ins)
                c.wait()

            step(nc.vector.tensor_copy(r, posi))
            step(nc.vector.tensor_scalar(r, r, later("attention", "invfreq")[0:32], None, ALU.mult))
            step(nc.vector.tensor_scalar(k, r, float(1 / two_pi), 12582912.0, ALU.mult, ALU.add))
            step(nc.vector.tensor_scalar(k, k, 12582912.0, None, ALU.subtract))
            for part in (c1, c2, c3):
                step(nc.vector.scalar_tensor_tensor(r, k, -part, r, ALU.mult, ALU.add))
            edge = 3.1415925
            step(nc.vector.tensor_scalar(r, r, edge, -edge, ALU.min, ALU.max))
            step(nc.vector.tensor_scalar(k, r, float(np.pi / 2), None, ALU.is_gt))
            step(nc.vector.scalar_tensor_tensor(k, k, -float(two_pi), r, ALU.mult, ALU.add))
            step(nc.vector.tensor_scalar(k, k, float(np.pi / 2), None, ALU.add))
            nc.vector.tensor_scalar(k, k, edge, -edge, ALU.min, ALU.max).then_inc(S["angles_ready"], 1)
            dve.wait_ge(S["tables_ready"], 1)

            def finish(n, hh):
                dve.wait_ge(S["pv_ps"], n)
                dve.wait_ge(S["agate_ready"], n)
                nc.vector.scalar_tensor_tensor(obuf[:, bass.ds(hh, 1), :].rearrange("p a t -> p (a t)"),
                                               bank[5][:, 0:T], 0.5, Q["gs"], ALU.mult, ALU.mult).then_inc(S["o_tiles"], 1)

            def run(i, n, hh, b, t, first):
                if not first:
                    finish(n - 1, hh - 1)
                dve.wait_ge(S["qrs_ready"], n)
                for j in range(NQ):
                    gain = pcol("b_qn_w", j) if j < GROUPS else pcol("b_kn_w", j - GROUPS)
                    ins = nc.vector.scalar_tensor_tensor(Q["qk"][:, j, :], Q["qk"][:, j, :], gain, Q["rs"][:, j, :],
                                                         ALU.mult, ALU.mult)
                ins.then_inc(S["qn_ready"], 1)
                dve.wait_ge(S["qn_ready"], n)
                c.did(nc.vector.tensor_tensor(Q["t1"][0:32], Q["qk"][0:32], Q["cos"][0:32].unsqueeze(1).to_broadcast([32, NQ, T]),
                                              ALU.mult))
                dve.wait_ge(S["rot_ps"], n)
                for j in range(GROUPS):
                    ins = nc.vector.tensor_tensor(Q["rs"][0:32, 2 * j:2 * j + 2, :],
                                                  bank[2 + j][0:32, :].rearrange("p (a b) -> p a b", a=2),
                                                  Q["sin"][0:32].unsqueeze(1).to_broadcast([32, 2, T]), ALU.mult)
                c.did(ins)
                c.wait()
                nc.vector.tensor_tensor(Q["qk"][0:32], Q["t1"][0:32], Q["rs"][0:32], ALU.add).then_inc(S["rope_ready"], 1)
                dve.wait_ge(S["scores_ps"], n)
                s0, s1 = NS[0], NS[0] + 2 * T
                nc.vector.scalar_tensor_tensor(Q["sc"][:, 0:s0], bank[5][:, 0:s0], ATT_SCALE, later("attention", "att0"),
                                               ALU.mult, ALU.add)
                nc.vector.scalar_tensor_tensor(Q["sc"][:, s0:s1], bank[6][:, :], ATT_SCALE,
                                               later("attention", "att1")[:, 0:2 * T], ALU.mult, ALU.add)
                c.did(nc.vector.scalar_tensor_tensor(Q["sc"][:, s1:s1 + T], bank[7][:, 0:T], ATT_SCALE,
                                                     later("attention", "att1")[:, 2 * T:3 * T], ALU.mult, ALU.add))
                c.wait()
                for tt in range(TS):
                    ins = nc.vector.tensor_reduce(Q["mx"][:, tt:tt + 1], Q["sc"][:, span[tt]], AX.X, ALU.max, negate=True)
                ins.then_inc(S["smax_ready"], 1)
                dve.wait_ge(S["exp_ready"], n)
                c.did(nc.vector.reciprocal(Q["inv"], Q["sum"]))
                c.wait()
                for tt in range(TS):
                    ins = nc.vector.tensor_scalar(Q["sc"][:, span[tt]], Q["sc"][:, span[tt]], Q["inv"][:, tt:tt + 1], None,
                                                  ALU.mult)
                ins.then_inc(S["probs_ready"], 1)
                dve.wait_ge(S["ggate_ready"], n)
                nc.vector.scalar_tensor_tensor(Q["gs"], Q["gs"], 1.0, bank[(t + 9) % 2][:, 0:T], ALU.add, ALU.mult)\
                    .then_inc(S["agate_ready"], 1)
                release(dve, S["agate_ready"], n, t + 9)

            heads(dve, p, base, run, lambda n, hh: finish(n - 1, hh - 1), c, 8)
            out_vector(dve, "out1", NORM_OF[1])

        PADT = 16
        W = wcarve(0, dict(diff=(KC, T), gate=(KC, T), u=(4, PADT + T), s1=(4, PADT + T), s2=(4, PADT + T)))

        def four(v):
            return v[:, :, PADT:PADT + T]

        def pool_tensor(pe, n):
            norm_tensor(pe, n)
            pe.wait_ge(S["h_chunks"], KC * (NORM_OF[2] + 1))
            for name in ("pool_u", "pool_gate"):
                p = at[name]
                with pe.Fori(0, KC // SLOTS) as i:
                    for j in range(SLOTS):
                        project(pe, hk, p.b + j, p.t + j, i, SLOTS, SLOTS)
            p = at["pool_mix"]
            for g in range(4):
                pe.wait_ge(S["diff_ready"], g + 1)
                project(pe, lambda k: W["diff"][:, 4 * g + k, :], p.b + g, p.t + 4 * g, width=4, kc=4)
            out_tensor(pe, "out2", KC, O_BEFORE[2] + KC)

        def pool_scalar(act, c, n):
            norm_scalar(act, c, n)
            p = at["pool_gate"]
            with act.Fori(0, KC // 2) as i:
                for j in range(2):
                    tile_done(act, p.t + j, i, 2)
                    nc.scalar.activation(W["gate"][:, bass.ds(2 * i + j, 1), :].rearrange("p a t -> p (a t)"),
                                         bank[(p.t + j) % 2][:, 0:T], ACT.Tanh, scale=0.5).then_inc(S["pgate_tanh"], 1)

        def pool_vector(dve, c, n):
            norm_vector(dve, n, "norm_w", 2 * KC)
            dve.wait_ge(S["later_loaded"], LATER_COUNT[2])
            p = at["pool_u"]
            for v in (W["u"], W["s1"], W["s2"]):
                c.did(nc.vector.memset(v[:, :, 0:PADT], 0.0))
            c.wait()
            for g in range(4):
                for j in range(4):
                    t = p.t + 4 * g + j
                    tile_done(dve, t)
                    nc.vector.tensor_copy(W["u"][:, j, PADT:], bank[t % 2][:, 0:T]).then_inc(taken[t % 2], 1)
                    bank_now_free(dve, t)
                src = W["u"]
                for l in range(g + 1):
                    dst = (W["s1"], W["s2"])[l % 2]
                    s = 1 << l
                    c.did(nc.vector.tensor_tensor(four(dst), four(src), src[:, :, PADT - s:PADT - s + T], ALU.add))
                    c.wait()
                    src = dst
                inv = later("pool", "poolcnt")[:, g * T:(g + 1) * T].unsqueeze(1).to_broadcast([P, 4, T])
                c.did(nc.vector.tensor_tensor(four(src), four(src), inv, ALU.mult))
                c.wait()
                nc.vector.tensor_tensor(W["diff"][:, 4 * g:4 * g + 4, :], four(src), four(W["u"]), ALU.subtract)\
                    .then_inc(S["diff_ready"], 1)
                dve.wait_ge(S["diff_ready"], g + 1)
            p = at["pool_gate"]
            with dve.Fori(0, KC // 2) as i:
                for j in range(2):
                    dve.wait_ge(S["pgate_tanh"], 2 * i + (j + 1))
                    gm = W["gate"][:, bass.ds(2 * i + j, 1), :].rearrange("p a t -> p (a t)")
                    nc.vector.scalar_tensor_tensor(gm, gm, 1.0, bank[(p.t + j) % 2][:, 0:T], ALU.add, ALU.mult)\
                        .then_inc(S["pgate_ready"], 1)
                    release(dve, S["pgate_ready"], 2 * i + (j + 1), p.t + j)
            p = at["pool_mix"]
            with dve.Fori(0, KC // 2) as i:
                for j in range(2):
                    tile_done(dve, p.t + j, i, 2)
                    m = 2 * i + j
                    nc.vector.scalar_tensor_tensor(
                        obuf[:, bass.ds(m, 1), :].rearrange("p a t -> p (a t)"), bank[(p.t + j) % 2][:, 0:T],
                        pcol("c_scale", m, half), W["gate"][:, bass.ds(m, 1), :].rearrange("p a t -> p (a t)"),
                        ALU.mult, ALU.mult).then_inc(S["o_tiles"], 1)
                    release(dve, S["o_tiles"], m + (O_BEFORE[2] + 1), p.t + j)
            out_vector(dve, "out2", NORM_OF[2])

        def later_gpsimd(pool, l):
            if NORM_OF[l]:
                pool.wait_ge(S["x_tiles"], KC * NORM_OF[l])
            name = {1: "attention", 2: "pool", 4: "even", 5: "odd"}[l]
            pool.dma_start(work[:, LATER0:LATER0 + NLATER[name]], a["const_" + name]).then_inc(S["later_loaded"], 16)
            if l == 1:
                pool.dma_start(Q["pos"][0:32].bitcast(I32), a["positions"]).then_inc(S["later_loaded"], 16)
            if l == 5:
                pool.wait_ge(S["norm_sum"], NORM_OF[5] + 1)
                pool.dma_start(gw, a["gates_w"]).then_inc(S["later_loaded"], 16)

        KV = 2
        E = wcarve(KC * T, dict(k=(KV, T), v=(KV, T), q=(T,), sq=(T,), rs=(T,), t1=(T,), vcur=(T,), p=(TS, T), pt=(4, P),
                                gs=(T,), mx=(TS,), sum=(TS,), inv=(TS,)))
        G = wcarve(0, dict(xl=(T + 3,), xc=(T,), r=(4, T), a=(2, T), th=(2, T), m=(2, T), u=(2, T), hf=(T,), hb=(T,),
                           gs=(T,), w=(4, P), lam=(16,), e=(16,), z=(16,), z2=(16,), s=(16,), nlam=(16,)))
        HP = float(P) ** -0.5

        def even_tensor(pe, n):
            norm_tensor(pe, n)
            pe.wait_ge(S["h_chunks"], KC * (NORM_OF[4] + 1))
            p = at["kv4"]
            for j in range(KV):
                project(pe, hk, p.b + j, p.t + j)
            for j in range(KV):
                token_tile(pe, p.b + KV + j, p.t + KV + j)
            pe.wait_ge(S["later_loaded"], LATER_COUNT[4])
            for j in range(KV):
                pe.wait_ge(S["ksq2_ready"], j + 1)
                nc.tensor.matmul(bank[2 + j][:, 0:T], cst("ones"), E["rs"] if j else E["sq"], start=True, stop=True)\
                    .then_inc(S["kstat_ps"], 1)
            for j in range(KV):
                pe.wait_ge(S["kn_ready"], j + 1)
                nc.tensor.matmul(bank[2 + j][:, 0:T], later("even", "rotax"), E["k"][:, j, :], start=True, stop=True)\
                    .then_inc(S["krot_ps"], 1)
            p = at["heads4"]
            base = HEAD_BASE[4]

            def finish(n):
                pe.wait_ge(S["probs_ready"], n)
                for s in range(TS):
                    for t in range(TS):
                        ins = nc.tensor.transpose(bank[5][:, (s * TS + t) * P:(s * TS + t + 1) * P],
                                                  E["p"][:, t, s * P:(s + 1) * P], cst("ident"))
                ins.then_inc(S["probt_ps"], 1)
                pe.wait_ge(S["probt_ready"], n)
                pe.wait_ge(S["vcur_ready"], n - base)
                for s in range(TS):
                    ins = nc.tensor.matmul(bank[6][:, 0:T], E["vcur"][:, s * P:(s + 1) * P],
                                           E["pt"][:, TS * s:TS * s + TS, :], start=(s == 0), stop=(s == TS - 1))
                ins.then_inc(S["pv_ps"], 1)

            def run(i, n, hh, b, t, first):
                project(pe, hk, b, t, i, 4, 4)
                pe.wait_ge(S["qsq4_ready"], n - base)
                if first:
                    pe.wait_ge(S["kv4_ready"], KV)
                nc.tensor.matmul(bank[2][:, 0:T], cst("ones"), E["sq"], start=True, stop=True).then_inc(S["qstat_ps"], 1)
                if not first:
                    finish(n - 1)
                project(pe, hk, b + 1, t + 1, i, 4, 4)
                pe.wait_ge(S["qn_ready"], n)
                nc.tensor.matmul(bank[3][:, 0:T], later("even", "rotax"), E["q"], start=True, stop=True)\
                    .then_inc(S["rot_ps"], 1)
                pe.wait_ge(S["rope_ready"], n)
                for tt in range(TS):
                    ins = nc.tensor.matmul(bank[4][:, tt * T:(tt + 1) * T], E["q"][:, tt * P:(tt + 1) * P], E["t1"],
                                           start=True, stop=True)
                ins.then_inc(S["scores_ps"], 1)

            heads(pe, p, base, run, lambda n, hh: finish(n - 1))

            p = at["lru4"]
            pe.wait_ge(S["lru_wait"], 1)

            def lru(i, n, hh, b, t, first):
                project(pe, hk, b, t, i, 4, 4)
                project(pe, hk, b + 1, t + 1, i, 4, 4)
                pe.wait_ge(S["lruw_loaded"], 16 * n)
                pe.wait_ge(S["xc_ready"], n)
                for j in range(4):
                    ins = nc.tensor.matmul(bank[2 + j // 2][:, (j % 2) * T:(j % 2 + 1) * T], G["w"][:, j, :], G["xc"],
                                           start=True, stop=True)
                ins.then_inc(S["lru_ps"], 1)

            heads(pe, p, 0, lru, None)
            out_tensor(pe, "out4", KC, O_BEFORE[4] + KC)

        def even_scalar(act, c, n):
            norm_scalar(act, c, n)
            p = at["kv4"]
            for j in range(KV):
                t = p.t + j
                tile_done(act, t)
                nc.scalar.copy(E["k"][:, j, :], bank[t % 2][:, 0:T]).then_inc(taken[t % 2], 1)
                bank_now_free(act, t)
                nc.scalar.activation(E["rs"] if j else E["sq"], E["k"][:, j, :], ACT.Square).then_inc(S["ksq2_ready"], 1)
            for j in range(KV):
                t = p.t + KV + j
                tile_done(act, t)
                nc.scalar.copy(E["v"][:, j, :], bank[t % 2][:, 0:T]).then_inc(taken[t % 2], 1)
                bank_now_free(act, t)
            for j in range(KV):
                act.wait_ge(S["kstat_ps"], j + 1)
                if j:
                    act.wait_ge(S["kn_ready"], 1)
                c.did(nc.scalar.activation(E["gs"], bank[2 + j][:, 0:T], ACT.Ln, bias=cst("eps"), scale=1.0 / P))
                c.wait()
                nc.scalar.activation(E["gs"], E["gs"], ACT.Exp, scale=-0.5).then_inc(S["krs_ready"], 1)
            p = at["heads4"]
            base = HEAD_BASE[4]

            def finish(n):
                act.wait_ge(S["probt_ps"], n)
                nc.scalar.copy(E["pt"], bank[5][:, :].rearrange("p (a b) -> p a b", a=4)).then_inc(S["probt_ready"], 1)

            def run(i, n, hh, b, t, first):
                tile_done(act, t, i, 4)
                if not first:
                    act.wait_ge(S["scores_ps"], n - 1)
                nc.scalar.copy(E["q"], bank[t % 2][:, 0:T]).then_inc(taken[t % 2], 1)
                bank_now_free(act, t, i, 4)
                if first:
                    act.wait_ge(S["kstat_ps"], KV)
                nc.scalar.activation(E["sq"], E["q"], ACT.Square).then_inc(S["qsq4_ready"], 1)
                act.wait_ge(S["qstat_ps"], n)
                if first:
                    act.wait_ge(S["kv4_ready"], KV)
                c.did(nc.scalar.activation(E["rs"], bank[2][:, 0:T], ACT.Ln, bias=cst("eps"), scale=1.0 / P))
                c.wait()
                nc.scalar.activation(E["rs"], E["rs"], ACT.Exp, scale=-0.5).then_inc(S["qrs_ready"], 1)
                if not first:
                    finish(n - 1)
                tile_done(act, t + 1, i, 4)
                if not first:
                    act.wait_ge(S["o_tiles"], O_BEFORE[4] + hh)
                nc.scalar.activation(E["gs"], bank[(t + 1) % 2][:, 0:T], ACT.Tanh, scale=0.5).then_inc(S["ggate_ready"], 1)
                act.wait_ge(S["smax_ready"], n)
                for tt in range(TS):
                    ins = nc.scalar.activation(E["p"][:, tt, :], bank[4][:, tt * T:(tt + 1) * T], ACT.Exp,
                                               bias=E["mx"][:, tt:tt + 1], scale=HP, accum_out=E["sum"][:, tt:tt + 1])
                ins.then_inc(S["exp_ready"], 1)

            heads(act, p, base, run, lambda n, hh: finish(n - 1), c, 2)

            act.wait_ge(S["lru_wait"], 1)
            lam = par[:, PARAM_AT["lru_lambda_2"]:PARAM_AT["lru_lambda_2"] + 16]
            c.did(nc.scalar.activation(G["e"], lam, ACT.Abs))
            c.wait()
            nc.scalar.activation(G["e"], G["e"], ACT.Exp, scale=-1.0).then_inc(S["lam_ready"], 1)
            act.wait_ge(S["lam_ready"], 2)
            p = at["lru4"]

            def lru(i, n, hh, b, t, first):
                tile_done(act, t, i, 4)
                if not first:
                    act.wait_ge(S["xc_ready"], n - 1)
                nc.scalar.copy(G["xl"][:, 2:T + 2], bank[t % 2][:, 0:T]).then_inc(S["xl_ready"], 1)
                release(act, S["xl_ready"], n, t)
                tile_done(act, t + 1, i, 4)
                if not first:
                    act.wait_ge(S["o_tiles"], O_BEFORE[4] + HEADS + hh)
                nc.scalar.activation(G["gs"], bank[(t + 1) % 2][:, 0:T], ACT.Tanh, scale=0.5).then_inc(S["lgate_tanh"], 1)
                act.wait_ge(S["lru_ps"], n)
                for j in range(4):
                    name = "lru_ba_2" if j < 2 else "lru_bx_2"
                    ins = nc.scalar.activation(G["r"][:, j, :], bank[2 + j // 2][:, (j % 2) * T:(j % 2 + 1) * T], ACT.Tanh,
                                               bias=pcol(name, hh + 8 * (j % 2), half), scale=0.5)
                ins.then_inc(S["lrt_ready"], 1)
                act.wait_ge(S["lr_ready"], n)
                for j in range(2):
                    c.did(nc.scalar.activation(G["a"][:, j, :], G["r"][:, j, :], ACT.Exp, scale=G["lam"][:, bass.ds(hh + 8 * j, 1)]))
                    ins = nc.scalar.activation(G["th"][:, j, :], G["r"][:, j, :], ACT.Tanh,
                                               scale=G["nlam"][:, bass.ds(hh + 8 * j, 1)])
                ins.then_inc(S["la_ready"], 1)
                act.wait_ge(S["lm_ready"], n)
                nc.scalar.activation(G["m"], G["m"], ACT.Sqrt).then_inc(S["lsq_ready"], 1)

            heads(act, p, 0, lru, None, c, 4)

        def even_vector(dve, c, n):
            norm_vector(dve, n, "norm_gain_2", 0)
            dve.wait_ge(S["later_loaded"], LATER_COUNT[4])
            axcos, axsin, base = later("even", "axcos"), later("even", "axsin"), HEAD_BASE[4]
            for j in range(KV):
                dve.wait_ge(S["krs_ready"], j + 1)
                nc.vector.scalar_tensor_tensor(E["k"][:, j, :], E["k"][:, j, :], pcol("k_norm_gain_2", 0), E["gs"],
                                               ALU.mult, ALU.mult).then_inc(S["kn_ready"], 1)
            for j in range(KV):
                dve.wait_ge(S["krot_ps"], j + 1)
                if not j:
                    dve.wait_ge(S["kn_ready"], KV)
                c.did(nc.vector.tensor_tensor(E["k"][:, j, :], E["k"][:, j, :], axcos, ALU.mult))
                c.did(nc.vector.tensor_tensor(E["rs"], bank[2 + j][:, 0:T], axsin, ALU.mult))
                c.wait()
                nc.vector.tensor_tensor(E["k"][:, j, :], E["k"][:, j, :], E["rs"], ALU.add).then_inc(S["kv4_ready"], 1)
                dve.wait_ge(S["kv4_ready"], j + 1)
            p = at["heads4"]

            def finish(n, hh):
                dve.wait_ge(S["pv_ps"], n)
                dve.wait_ge(S["agate_ready"], n)
                nc.vector.scalar_tensor_tensor(obuf[:, bass.ds(hh, 1), :].rearrange("p a t -> p (a t)"),
                                               bank[6][:, 0:T], 0.5, E["gs"], ALU.mult, ALU.mult).then_inc(S["o_tiles"], 1)

            def run(i, n, hh, b, t, first):
                dve.wait_ge(S["qrs_ready"], n)
                nc.vector.scalar_tensor_tensor(E["q"], E["q"], pcol("q_norm_gain_2", 0), E["rs"], ALU.mult, ALU.mult)\
                    .then_inc(S["qn_ready"], 1)
                if not first:
                    finish(n - 1, hh - 1)
                dve.wait_ge(S["rot_ps"], n)
                dve.wait_ge(S["qn_ready"], n)
                c.did(nc.vector.tensor_tensor(E["rs"], bank[3][:, 0:T], axsin, ALU.mult))
                c.did(nc.vector.tensor_tensor(E["q"], E["q"], axcos, ALU.mult))
                kv = hh // 4 if isinstance(hh, int) else nc.s_assert_within(
                    hh >> 2, 0, KV - 1, skip_runtime_bounds_check_because="there are 8 heads")
                nc.vector.tensor_copy(E["t1"], E["k"][:, bass.ds(kv, 1), :].rearrange("p a t -> p (a t)"))
                nc.vector.tensor_copy(E["vcur"], E["v"][:, bass.ds(kv, 1), :].rearrange("p a t -> p (a t)"))\
                    .then_inc(S["vcur_ready"], 1)
                c.wait()
                nc.vector.tensor_tensor(E["q"], E["q"], E["rs"], ALU.add).then_inc(S["rope_ready"], 1)
                dve.wait_ge(S["scores_ps"], n)
                c.did(nc.vector.tensor_reduce(E["mx"], bank[4][:, :].rearrange("p (a b) -> p a b", a=TS), AX.X, ALU.max))
                c.wait()
                nc.vector.tensor_scalar(E["mx"], E["mx"], -HP, None, ALU.mult).then_inc(S["smax_ready"], 1)
                dve.wait_ge(S["ggate_ready"], n)
                nc.vector.scalar_tensor_tensor(E["gs"], E["gs"], 1.0, bank[(t + 1) % 2][:, 0:T], ALU.add, ALU.mult)\
                    .then_inc(S["agate_ready"], 1)
                release(dve, S["agate_ready"], n, t + 1)
                dve.wait_ge(S["exp_ready"], n)
                c.did(nc.vector.reciprocal(E["inv"], E["sum"]))
                c.wait()
                for tt in range(TS):
                    ins = nc.vector.tensor_scalar(E["p"][:, tt, :], E["p"][:, tt, :], E["inv"][:, tt:tt + 1], None, ALU.mult)
                ins.then_inc(S["probs_ready"], 1)

            heads(dve, p, base, run, lambda n, hh: finish(n - 1, hh - 1), c, 8)

            dve.wait_ge(S["o_tiles"], O_BEFORE[4] + HEADS)
            c.did(nc.vector.memset(G["xl"], 0.0))
            c.wait()
            nc.vector.memset(G["s"], 1.0 / 15.0).then_inc(S["lru_wait"], 1)
            dve.wait_ge(S["lru_wait"], 1)
            dve.wait_ge(S["lam_ready"], 1)

            def step(ins):
                c.did(ins)
                c.wait()

            step(nc.vector.tensor_scalar(G["z"], G["e"], 2.0, None, ALU.add))
            step(nc.vector.reciprocal(G["z"], G["z"]))
            step(nc.vector.tensor_tensor(G["z"], G["z"], G["e"], ALU.mult))
            step(nc.vector.tensor_tensor(G["z2"], G["z"], G["z"], ALU.mult))
            for k in (13, 11, 9, 7, 5, 3, 1):
                step(nc.vector.tensor_tensor(G["s"], G["s"], G["z2"], ALU.mult))
                step(nc.vector.tensor_scalar(G["s"], G["s"], 1.0 / k, None, ALU.add))
            step(nc.vector.tensor_tensor(G["s"], G["s"], G["z"], ALU.mult))
            lam = par[:, PARAM_AT["lru_lambda_2"]:PARAM_AT["lru_lambda_2"] + 16]
            step(nc.vector.tensor_scalar(G["lam"], lam, 0.0, 8.0, ALU.min, ALU.mult))
            step(nc.vector.scalar_tensor_tensor(G["lam"], G["s"], -16.0, G["lam"], ALU.mult, ALU.add))
            nc.vector.tensor_scalar(G["nlam"], G["lam"], -1.0, None, ALU.mult).then_inc(S["lam_ready"], 1)

            def lru(i, n, hh, b, t, first):
                dve.wait_ge(S["xl_ready"], n)
                if not first:
                    dve.wait_ge(S["lru_ps"], n - 1)
                c.did(nc.vector.tensor_scalar(G["xc"], G["xl"][:, 0:T], pcol("conv_w_2", hh), pcol("conv_b_2", hh),
                                              ALU.mult, ALU.add))
                c.wait()
                for j in range(1, 4):
                    ins = nc.vector.scalar_tensor_tensor(G["xc"], G["xl"][:, j:T + j], pcol("conv_w_2", hh + 8 * j), G["xc"],
                                                         ALU.mult, ALU.add)
                    if j < 3:
                        step(ins)
                ins.then_inc(S["xc_ready"], 1)
                dve.wait_ge(S["lgate_tanh"], n)
                nc.vector.scalar_tensor_tensor(G["gs"], G["gs"], 1.0, bank[(t + 1) % 2][:, 0:T], ALU.add, ALU.mult)\
                    .then_inc(S["lgate_ready"], 1)
                release(dve, S["lgate_ready"], n, t + 1)
                dve.wait_ge(S["lrt_ready"], n)
                nc.vector.tensor_scalar(G["r"], G["r"], 0.5, 0.5, ALU.mult, ALU.add).then_inc(S["lr_ready"], 1)
                dve.wait_ge(S["lr_ready"], n)
                dve.wait_ge(S["xc_ready"], n)
                c.did(nc.vector.tensor_tensor(G["u"], G["r"][:, 2:4, :], G["xc"].unsqueeze(1).to_broadcast([P, 2, T]), ALU.mult))
                dve.wait_ge(S["la_ready"], n)
                step(nc.vector.tensor_tensor(G["m"], G["a"], G["a"], ALU.mult))
                step(nc.vector.scalar_tensor_tensor(G["m"], G["m"], 1.0, G["th"], ALU.add, ALU.mult))
                nc.vector.tensor_scalar(G["m"], G["m"], 1e-30, None, ALU.max).then_inc(S["lm_ready"], 1)
                dve.wait_ge(S["lsq_ready"], n)
                step(nc.vector.tensor_tensor(G["u"], G["u"], G["m"], ALU.mult))
                c.did(nc.vector.tensor_tensor_scan(G["hf"], G["a"][:, 0, :], G["u"][:, 0, :], 0.0, ALU.mult, ALU.add))
                step(nc.vector.tensor_tensor_scan(G["hb"][:, ::-1], G["a"][:, 1, ::-1], G["u"][:, 1, ::-1], 0.0,
                                                  ALU.mult, ALU.add))
                step(nc.vector.tensor_tensor(G["hf"], G["hf"], G["hb"], ALU.add))
                dve.wait_ge(S["lgate_ready"], n)
                nc.vector.scalar_tensor_tensor(obuf[:, bass.ds(hh + HEADS, 1), :].rearrange("p a t -> p (a t)"),
                                               G["hf"], 0.5, G["gs"], ALU.mult, ALU.mult).then_inc(S["o_tiles"], 1)

            heads(dve, at["lru4"], 0, lru, None, c, 20)
            out_vector(dve, "out4", NORM_OF[4])

        def even_gpsimd(pool):
            pool.wait_ge(S["lru_wait"], 1)

            def one(j, n):
                if not isinstance(j, int):
                    pool.wait_ge(S["lru_ps"], n - 1)
                pool.dma_start(G["w"], a["lru_w"][bass.ds(j, 1)].rearrange("a p m n -> p (a m) n"))\
                    .then_inc(S["lruw_loaded"], 16)

            one(0, 1)
            with pool.Fori(0, HEADS - 1) as i:
                one(i + 1, i + 2)

        NG = 2 * HEADS
        M = wcarve(KC * T, dict(gi=(T,), gf=(T,), tmp=(T,), bsum=(2, T), g=(2, T), mf=(2, 2, T), gcol=(TS, NG), q=(T,),
                                k=(T,), v=(TS, 2, P), mh=(4, T), fl=(2, T), mm=(2, 2, P), e=(2, TS, T), dn=(2, T),
                                w=(TS, T), osig=(2, T), hs=(2, T), hsq=(2, T), rs=(T,), zs=(2, T)))
        gw = work[:, 0:KC * 32].rearrange("p (k n) -> p k n", k=KC)

        def odd_tensor(pe, n):
            norm_tensor(pe, n)
            p = at["gates5"]
            pe.wait_ge(S["h_chunks"], KC * (NORM_OF[5] + 1))
            pe.wait_ge(S["later_loaded"], LATER_COUNT[5])
            bank_free(pe, p.t)
            for j in range(2):
                for k in range(KC):
                    ins = nc.tensor.matmul(bank[p.t % 2][0:NG, j * T:(j + 1) * T], gw[:, k, NG * j:NG * (j + 1)], hk(k),
                                           start=(k == 0), stop=(k == KC - 1))
            ins.then_inc(S["tile_ready"], 1)
            pe.wait_ge(S["gates_dve"], 3)
            for j in range(2):
                for tt in range(TS):
                    ins = nc.tensor.transpose(bank[2][:, (2 * j + tt) * NG:(2 * j + tt + 1) * NG],
                                              M["g"][0:NG, j, tt * P:(tt + 1) * P], cst("ident")[0:NG, 0:NG])
            ins.then_inc(S["gt_ps"], 1)
            p = at["heads5"]

            def finish(n):
                pe.wait_ge(S["mw_ready"], n)
                for vt in range(2):
                    for s in range(TS):
                        ins = nc.tensor.matmul(bank[6][:, vt * T:(vt + 1) * T], M["v"][:, s, vt, :], M["w"][:, s, :],
                                               start=(s == 0), stop=(s == TS - 1))
                ins.then_inc(S["mpv_ps"], 1)

            def run(i, n, hh, b, t, first):
                project(pe, hk, b, t, i, 16, 16)
                project(pe, hk, b + 1, t + 1, i, 16, 16)
                pe.wait_ge(S["mh_ready"], n)
                if first:
                    pe.wait_ge(S["gates_dve"], 4)
                nc.tensor.matmul(bank[2][:, :], cst("ones")[0:NG, :], M["mh"][0:NG, 0:2, :], start=True, stop=True)
                nc.tensor.matmul(bank[3][:, :], cst("ones")[0:NG, :], M["mh"][0:NG, 2:4, :], start=True, stop=True)\
                    .then_inc(S["mbc_ps"], 1)
                token_tile(pe, b + 2, t + 2, i, 16, 16)
                pe.wait_ge(S["mk_ready"], n)
                for s in range(TS):
                    ins = nc.tensor.matmul(bank[4][:, s * T:(s + 1) * T], M["k"][:, s * P:(s + 1) * P], M["q"],
                                           start=True, stop=True)
                ins.then_inc(S["ms_ps"], 1)
                token_tile(pe, b + 3, t + 3, i, 16, 16)
                pe.wait_ge(S["me_ready"], n)
                for d in range(2):
                    for s in range(TS):
                        ins = nc.tensor.matmul(bank[5][:, d * T:(d + 1) * T], cst("ones"), M["e"][:, d, s, :],
                                               start=(s == 0), stop=(s == TS - 1))
                ins.then_inc(S["mden_ps"], 1)
                project(pe, hk, b + 4, t + 4, i, 16, 16)
                project(pe, hk, b + 5, t + 5, i, 16, 16)
                pe.wait_ge(S["mv_ready"], 2 * n)
                finish(n)
                project(pe, hk, b + 6, t + 6, i, 16, 16)
                pe.wait_ge(S["mhsq_ready"], n)
                for vt in range(2):
                    ins = nc.tensor.matmul(bank[7][:, 0:T], cst("ones"), M["hsq"][:, vt, :], start=(vt == 0), stop=(vt == 1))
                ins.then_inc(S["mstat_ps"], 1)
                project(pe, hk, b + 7, t + 7, i, 16, 16)

            heads(pe, p, 0, run, None)
            out_tensor(pe, "out5", KC, O_BEFORE[5] + KC)

        def odd_scalar(act, c, n):
            norm_scalar(act, c, n)
            g = slice(0, NG)
            act.wait_ge(S["gates_dve"], 1)
            c.did(nc.scalar.activation(M["tmp"][g], M["gf"][g], ACT.Abs))
            c.wait()
            c.did(nc.scalar.activation(M["tmp"][g], M["tmp"][g], ACT.Exp, scale=-1.0))
            c.wait()
            nc.scalar.activation(M["tmp"][g], M["tmp"][g], ACT.Ln, bias=cst("one")[g]).then_inc(S["gates_act"], 1)
            act.wait_ge(S["gates_dve"], 2)
            nc.scalar.activation(M["mf"][g, 1], M["mf"][g, 1], ACT.Exp, scale=-1.0).then_inc(S["gates_act"], 1)
            p = at["heads5"]

            def run(i, n, hh, b, t, first):
                tile_done(act, t, i, 16)
                if not first:
                    act.wait_ge(S["ms_ps"], n - 1)
                nc.scalar.copy(M["q"], bank[t % 2][:, 0:T]).then_inc(taken[t % 2], 1)
                tile_done(act, t + 1, i, 16)
                nc.scalar.mul(M["k"], bank[(t + 1) % 2][:, 0:T], HP).then_inc(S["mk_ready"], 1)
                release(act, S["mk_ready"], n, t + 1)
                act.wait_ge(S["mbc_ps"], n)
                if not first:
                    act.wait_ge(S["mdn_ready"], n - 1)
                c.did(nc.scalar.copy(M["fl"], bank[3][:, :].rearrange("p (a b) -> p a b", a=2)))
                act.wait_ge(S["mm2_ready"], n)
                if not first:
                    act.wait_ge(S["mw_ready"], n - 1)
                gf0, gf1 = (M["gcol"][:, s, bass.ds(hh, 1)] for s in range(2))
                gb0, gb1 = (M["gcol"][:, s, bass.ds(hh + HEADS, 1)] for s in range(2))
                nc.scalar.activation(M["e"][:, 0, 0, 0:P], M["mm"][:, 0, 0, :], ACT.Exp, bias=gf0)
                nc.scalar.activation(M["e"][:, 0, 0, P:T], bank[2][:, P:T], ACT.Exp, bias=gf0, scale=-1.0)
                nc.scalar.activation(M["e"][:, 0, 1, P:T], M["mm"][:, 0, 1, :], ACT.Exp, bias=gf1)
                nc.scalar.activation(M["e"][:, 1, 0, 0:P], M["mm"][:, 1, 0, :], ACT.Exp, bias=gb0)
                nc.scalar.activation(M["e"][:, 1, 1, 0:P], bank[2][:, T:T + P], ACT.Exp, bias=gb1, scale=-1.0)
                nc.scalar.activation(M["e"][:, 1, 1, P:T], M["mm"][:, 1, 1, :], ACT.Exp, bias=gb1).then_inc(S["mexp_ready"], 1)
                for j in range(2):
                    tile_done(act, t + 2 + j, i, 16)
                    if j == 0 and not first:
                        act.wait_ge(S["mpv_ps"], n - 1)
                    nc.scalar.copy(M["v"][:, :, j, :], bank[(t + j) % 2][:, 0:T].rearrange("p (a b) -> p a b", a=TS))\
                        .then_inc(S["mv_ready"], 1)
                    release(act, S["mv_ready"], 2 * n - 1 + j, t + 2 + j)
                for j in range(2):
                    tile_done(act, t + 4 + j, i, 16)
                    nc.scalar.activation(M["osig"][:, j, :], bank[(t + j) % 2][:, 0:T], ACT.Tanh, scale=0.5)\
                        .then_inc(S["mo_ready"], 1)
                    release(act, S["mo_ready"], 2 * n - 1 + j, t + 4 + j)
                act.wait_ge(S["mhs_ready"], n)
                nc.scalar.activation(M["hsq"], M["hs"], ACT.Square).then_inc(S["mhsq_ready"], 1)
                act.wait_ge(S["mstat_ps"], n)
                c.did(nc.scalar.activation(M["rs"], bank[7][:, 0:T], ACT.Ln, bias=cst("eps"), scale=0.25 / (2 * P)))
                c.wait()
                nc.scalar.activation(M["rs"], M["rs"], ACT.Exp, scale=-0.5).then_inc(S["mrs_ready"], 1)
                for j in range(2):
                    tile_done(act, t + 6 + j, i, 16)
                    nc.scalar.activation(M["zs"][:, j, :], bank[(t + j) % 2][:, 0:T], ACT.Tanh, scale=0.5)\
                        .then_inc(S["mz_ready"], 1)

            heads(act, p, 0, run, None, c, 4)

        def odd_vector(dve, c, n):
            norm_vector(dve, n, "norm_gain_2", KC)
            dve.wait_ge(S["later_loaded"], LATER_COUNT[5])
            g = slice(0, NG)
            t = at["gates5"].t
            tile_done(dve, t)

            def step(ins):
                c.did(ins)
                c.wait()

            nc.vector.tensor_scalar(M["gi"][g], bank[t % 2][g, 0:T], pcol("gate_bias", 0)[g], None, ALU.add)
            nc.vector.tensor_scalar(M["gf"][g], bank[t % 2][g, T:2 * T], pcol("gate_bias", 1)[g], None, ALU.add)\
                .then_inc(S["gates_dve"], 1)
            release(dve, S["gates_dve"], 1, t)
            dve.wait_ge(S["gates_act"], 1)
            step(nc.vector.tensor_scalar(M["gf"][g], M["gf"][g], 0.0, None, ALU.min))
            step(nc.vector.tensor_tensor(M["gf"][g], M["gf"][g], M["tmp"][g], ALU.subtract))
            step(nc.vector.memset(M["tmp"][g], 0.0))
            c.did(nc.vector.tensor_tensor_scan(M["bsum"][g, 0, :], M["gf"][g], M["tmp"][g], 0.0, ALU.add, ALU.add))
            step(nc.vector.tensor_tensor_scan(M["bsum"][g, 1, ::-1], M["gf"][g, ::-1], M["tmp"][g], 0.0, ALU.add, ALU.add))
            step(nc.vector.tensor_tensor(M["g"][g], M["gi"][g].unsqueeze(1).to_broadcast([NG, 2, T]), M["bsum"][g], ALU.subtract))
            c.did(nc.vector.tensor_tensor_scan(M["mf"][g, 0, 0, :], M["g"][g, 0, :], M["g"][g, 0, :], 0.0, ALU.max, ALU.max))
            step(nc.vector.tensor_tensor_scan(M["mf"][g, 0, 1, ::-1], M["g"][g, 1, ::-1], M["g"][g, 1, ::-1], 0.0,
                                              ALU.max, ALU.max))
            nc.vector.tensor_tensor(M["mf"][g, 1], M["mf"][g, 0], M["bsum"][g], ALU.add).then_inc(S["gates_dve"], 1)
            nc.vector.memset(M["e"][:, 0, 1, 0:P], 0.0)
            nc.vector.memset(M["e"][:, 1, 0, P:T], 0.0).then_inc(S["gates_dve"], 1)
            dve.wait_ge(S["gt_ps"], 1)
            for j in range(2):
                for tt in range(TS):
                    src = bank[2][:, (2 * j + tt) * NG + HEADS * j:(2 * j + tt) * NG + HEADS * (j + 1)]
                    ins = nc.vector.tensor_copy(M["gcol"][:, tt, HEADS * j:HEADS * (j + 1)], src)
            ins.then_inc(S["gates_dve"], 1)
            dve.wait_ge(S["gates_act"], 2)
            p = at["heads5"]

            def run(i, n, hh, b, t, first):
                if not first:
                    dve.wait_ge(S["mbc_ps"], n - 1)
                for d in range(2):
                    pick = cst("ident")[g, bass.ds(hh + HEADS * d, 1)]
                    nc.vector.tensor_scalar(M["mh"][g, d, :], M["mf"][g, 0, d, :], pick, None, ALU.mult)
                    ins = nc.vector.tensor_scalar(M["mh"][g, 2 + d, :], M["mf"][g, 1, d, :], pick, None, ALU.mult)
                ins.then_inc(S["mh_ready"], 1)
                dve.wait_ge(S["mbc_ps"], n)
                for d, name in ((0, "triu"), (1, "tril")):
                    ins = nc.vector.tensor_tensor(M["mm"][:, d], later("odd", name).unsqueeze(1).to_broadcast([P, TS, P]),
                                                  bank[2][:, d * T:(d + 1) * T].rearrange("p (a b) -> p a b", a=TS),
                                                  ALU.subtract)
                ins.then_inc(S["mm2_ready"], 1)
                dve.wait_ge(S["ms_ps"], n)
                dve.wait_ge(S["mexp_ready"], n)
                for d in range(2):
                    ins = nc.vector.tensor_tensor(M["e"][:, d], M["e"][:, d], bank[4][:, :].rearrange("p (a b) -> p a b", a=TS),
                                                  ALU.mult)
                ins.then_inc(S["me_ready"], 1)
                dve.wait_ge(S["mden_ps"], n)
                den = bank[5][:, :].rearrange("p (a b) -> p a b", a=2)
                step(nc.vector.scalar_tensor_tensor(M["dn"], den, -1.0, M["fl"], ALU.mult, ALU.max))
                nc.vector.tensor_tensor(M["dn"], den, M["dn"], ALU.max).then_inc(S["mdn_ready"], 1)
                dve.wait_ge(S["mdn_ready"], n)
                step(nc.vector.reciprocal(M["dn"], M["dn"]))
                dve.wait_ge(S["me_ready"], n)
                for d in range(2):
                    ins = nc.vector.tensor_tensor(M["e"][:, d], M["e"][:, d],
                                                  M["dn"][:, d, :].unsqueeze(1).to_broadcast([P, TS, T]), ALU.mult)
                step(ins)
                nc.vector.tensor_tensor(M["w"], M["e"][:, 0], M["e"][:, 1], ALU.add).then_inc(S["mw_ready"], 1)
                dve.wait_ge(S["mpv_ps"], n)
                dve.wait_ge(S["mo_ready"], 2 * n)
                nc.vector.scalar_tensor_tensor(M["hs"], M["osig"], 1.0, bank[6][:, :].rearrange("p (a b) -> p a b", a=2),
                                               ALU.add, ALU.mult).then_inc(S["mhs_ready"], 1)
                dve.wait_ge(S["mrs_ready"], n)
                dve.wait_ge(S["mhs_ready"], n)
                for j in range(2):
                    step(nc.vector.scalar_tensor_tensor(M["hs"][:, j, :], M["hs"][:, j, :], pcol("odd_norm_gain_2", hh * 2 + j),
                                                        M["rs"], ALU.mult, ALU.mult))
                for j in range(2):
                    dve.wait_ge(S["mz_ready"], 2 * n - 1 + j)
                    nc.vector.scalar_tensor_tensor(M["zs"][:, j, :], M["zs"][:, j, :], 1.0, bank[(t + j) % 2][:, 0:T],
                                                   ALU.add, ALU.mult).then_inc(S["mzs_ready"], 1)
                    release(dve, S["mzs_ready"], 2 * n - 1 + j, t + 6 + j)
                nc.vector.scalar_tensor_tensor(obuf[:, bass.ds(hh * 2, 2), :], M["hs"], 0.25, M["zs"], ALU.mult, ALU.mult)\
                    .then_inc(S["o_tiles"], 2)

            heads(dve, p, 0, run, None, c, 10)
            out_vector(dve, "out5", NORM_OF[5])

        NORM_OF = {l: n for n, l in enumerate(layers)}
        O_MADE = {0: KC, 1: HEADS, 2: KC, 3: KC, 4: KC, 5: KC}
        O_BEFORE, made = {}, 0
        for l in layers:
            O_BEFORE[l] = made
            made += O_MADE[l]
        HEAD_BASE = {1: 0, 4: HEADS * (1 in layers)}
        LATER_COUNT, made = {}, 0
        for l in layers:
            made += {0: 0, 3: 0, 1: 32, 2: 16, 4: 16, 5: 32}[l]
            LATER_COUNT[l] = made

        @block.sync
        def _(sp):
            where = []
            for name, p in at.items():
                where += [(p.t + (j + 1) * (p.tiles // p.blocks)) for j in range(p.blocks)]

            def load(b, row):
                sp.dma_start(ring[:, b % SLOTS, :], a["stream"][bass.ds(row, 1)].rearrange("a p n -> p (a n)"))\
                    .then_inc(loaded[b % SLOTS], 16)

            for name, p in at.items():
                if not p.blocks:
                    continue
                width = p.tiles // p.blocks
                turns = max(0, (p.blocks - SLOTS) // SLOTS)
                turns = turns if turns > 1 else 0
                for b in range(p.b, p.b + min(SLOTS, p.blocks)):
                    if b >= SLOTS:
                        sp.wait_ge(S["tile_ready"], where[b - SLOTS])
                    load(b, b)
                if turns:
                    with sp.Fori(0, turns) as i:
                        for j in range(SLOTS):
                            sp.wait_ge(S["tile_ready"], i * (SLOTS * width) + (p.t + (j + 1) * width))
                            load(p.b + j, i * SLOTS + (p.b + SLOTS + j))
                for b in range(p.b + SLOTS + turns * SLOTS, p.b + p.blocks):
                    sp.wait_ge(S["tile_ready"], where[b - SLOTS])
                    load(b, b)

        @block.gpsimd
        def _(pool):
            for l in layers:
                if l in (0, 3):
                    rwkv_gpsimd(pool, l // 3)
                else:
                    later_gpsimd(pool, l)
                if l == 4:
                    even_gpsimd(pool)

        @block.scalar
        def _(act):
            act.dma_start(x[:, :, :], a["x_cm"]).then_inc(S["consts_loaded"], 16)
            act.dma_start(const[:, :], a["const"]).then_inc(S["consts_loaded"], 16)
            act.dma_start(par[:, :], a["par"]).then_inc(S["consts_loaded"], 16)
            act.wait_ge(S["consts_loaded"], 48)
            c = Steps(act, S["act_steps"])
            nc.scalar.mul(half[:, :], par[:, :], 0.5).then_inc(S["half_ready"], 1)
            act.wait_ge(S["half_ready"], 1)
            for n, l in enumerate(layers):
                if l in (0, 3):
                    rwkv_scalar(act, c, l // 3, n)
                if l == 1:
                    att_scalar(act, c, n)
                if l == 2:
                    pool_scalar(act, c, n)
                if l == 4:
                    even_scalar(act, c, n)
                if l == 5:
                    odd_scalar(act, c, n)
            if final:
                final_scalar(act, c, len(layers))

        @block.vector
        def _(dve):
            dve.wait_ge(S["consts_loaded"], 48)
            dve.wait_ge(S["half_ready"], 1)
            c = Steps(dve, S["dve_steps"])
            for n, l in enumerate(layers):
                if l in (0, 3):
                    rwkv_vector(dve, c, l // 3, n)
                if l == 1:
                    att_vector(dve, c, n)
                if l == 2:
                    pool_vector(dve, c, n)
                if l == 4:
                    even_vector(dve, c, n)
                if l == 5:
                    odd_vector(dve, c, n)
            if final:
                final_vector(dve, c, len(layers))

        @block.tensor
        def _(pe):
            pe.wait_ge(S["consts_loaded"], 48)
            for n, l in enumerate(layers):
                if l in (0, 3):
                    rwkv_tensor(pe, l // 3, n)
                if l == 1:
                    att_tensor(pe, n)
                if l == 2:
                    pool_tensor(pe, n)
                if l == 4:
                    even_tensor(pe, n)
                if l == 5:
                    odd_tensor(pe, n)
            if final:
                norm_tensor(pe, len(layers))



def blocks(w):
    k, n = w.shape
    cols = D * P // k
    return np.ascontiguousarray(w.reshape(k // P, P, n // cols, cols).transpose(2, 1, 0, 3)).reshape(-1, P, D)


def padded(w):
    return np.concatenate([w, np.zeros((w.shape[0], P - w.shape[1]), w.dtype)], 1)


def chunked(v):
    return v.reshape(-1, P).T


def woven(parts):
    turns = [b.reshape(-1, n, P, D) for b, n in parts]
    return np.concatenate(turns, 1).reshape(-1, P, D)


def stream_parts(i):
    def rwkv(n):
        w = i["a_w_in"][n]
        r, k, v, g = (blocks(w[j]) for j in range(4))
        return woven([(k, 1), (r, 1), (v, 1), (g, 1)])

    def lora(n):
        ws = [i["a_w1"][n], i["a_a1"][n]] + ([i["a_v1"][0]] if n else [])
        return np.concatenate([blocks(padded(w)) for w in ws])

    b = blocks(i["b_w_in"][0])
    qkv = b[:72].reshape(3, GROUPS, HEADS, P, D).transpose(2, 0, 1, 3, 4).reshape(-1, P, D)
    heads1 = woven([(qkv, 9), (b[72:80], 1)])
    c = blocks(i["c_w_in"][0])
    e = blocks(i["even_w_in_2"][0])
    w = i["odd_w_in_2"][0]
    q, k, v, o, z = (blocks(w[:, a0:a1]) for a0, a1 in ((0, 1024), (1024, 2048), (2048, 4096), (4096, 6144),
                                                        (6144, 8192)))
    return {
        "lora0": lora(0), "rwkv0": rwkv(0), "out0": blocks(i["a_w_out"][0]),
        "heads1": heads1, "out1": blocks(i["b_w_out"][0]),
        "pool_u": c[:16], "pool_gate": c[16:], "pool_mix": np.concatenate([blocks(g) for g in i["c_w_grp"][0]]),
        "out2": blocks(i["c_w_out"][0]),
        "lora3": lora(1), "rwkv3": rwkv(1), "out3": blocks(i["a_w_out"][1]),
        "kv4": e[8:12], "heads4": woven([(e[0:8], 1), (e[12:20], 1)]),
        "lru4": woven([(e[20:28], 1), (e[28:36], 1)]), "out4": blocks(i["even_w_out_2"][0]),
        "gates5": np.zeros((0, P, D), np.float32),
        "heads5": woven([(q, 1), (k, 1), (v, 2), (o, 2), (z, 2)]), "out5": blocks(i["odd_w_out_2"][0]),
    }


def layouts(i, phases=None):
    parts = stream_parts(i)
    out = {"stream": np.concatenate([parts[n] for n, _, _ in STREAM if phases is None or n in phases])}
    out["x_cm"] = np.ascontiguousarray(i["x"][0].T.reshape(KC, P, T).transpose(1, 0, 2))
    lay = {"norm_w": 0}
    bias = i["odd_gate_bias_2"][0].reshape(2, 2 * HEADS).T
    special = {"gate_bias": np.concatenate([bias, np.zeros((P - 2 * HEADS, 2), np.float32)], 0)}
    out["par"] = np.concatenate([special[n] if n in special else chunked(i[n]) for n, _ in PARAMS], 1)
    out["const"] = np.concatenate([CONST[k] for k in RESIDENT], 1)
    for layer, names in LATER.items():
        out["const_" + layer] = np.concatenate([CONST[k] for k in names], 1)
    v2 = np.zeros((LORA, D), np.float32)
    v2[:MVL] = i["a_v2"][0]
    lora2 = [np.stack([i["a_w2"][n], i["a_a2"][n], v2 if n else np.zeros((LORA, D), np.float32)], 1) for n in range(2)]
    out["lora2"] = np.ascontiguousarray(np.stack([m.reshape(LORA, 3, KC, P).transpose(2, 0, 1, 3) for m in lora2]))
    wa, wx = i["lru_wa_2"][0], i["lru_wx_2"][0]
    out["lru_w"] = np.ascontiguousarray(np.stack([wa[0], wa[1], wx[0], wx[1]], 2))
    g = i["odd_w_in_2"][0][:, 8192:]
    out["gates_w"] = np.ascontiguousarray(g.reshape(KC, P, 32).transpose(1, 0, 2))
    out["positions"] = np.ascontiguousarray(np.broadcast_to(i["positions"], (32, T)))
    return {k: np.ascontiguousarray(v) for k, v in out.items()}


def kernel(**inputs):
    import concourse.bacc as bacc
    from concourse.bass_utils import run_bass_kernel_spmd

    nc = bacc.Bacc("TRN2", target_bir_lowering=False, num_devices=1)
    arrays = layouts({k: np.asarray(v) for k, v in inputs.items()})
    a = {n: nc.dram_tensor(n, v.shape, mybir.dt.from_np(v.dtype), kind="ExternalInput").ap() for n, v in arrays.items()}
    a["out"] = nc.dram_tensor("out", (P, KC, T), F32, kind="ExternalOutput").ap()
    build(nc, a)
    r = run_bass_kernel_spmd(nc, [arrays], core_ids=[0])
    return r.results[0]["out"].transpose(1, 0, 2).reshape(D, T).T[None]
```

```python
from contextlib import ExitStack

import numpy as np
import concourse.bass as bass
from concourse import mybir
from concourse.alu_op_type import AluOpType as ALU

F32 = mybir.dt.float32
I32 = mybir.dt.int32
ACT = mybir.ActivationFunctionType
AX = mybir.AxisListType

T = 256
D = 2048
P = 128
KC = D // P
SLOTS = 4
CH = 64
NU = T // CH
TS = T // P
LEVELS = 5
DECAY = float(np.exp(-0.5))
LN2_8 = float(8 * np.log(2.0))
HEADS = 8
GROUPS = 3
LORA = 96
MVL = 64
MASKED = -1e30


class Phase:

    def __init__(self, b, t, blocks, tiles):
        self.b, self.t, self.blocks, self.tiles = b, t, blocks, tiles


STREAM = [
    ("lora0", 2, 2), ("rwkv0", 64, 64), ("out0", 16, 16),
    ("heads1", 80, 80), ("out1", 8, 16),
    ("pool_u", 16, 16), ("pool_gate", 16, 16), ("pool_mix", 4, 16), ("out2", 16, 16),
    ("lora3", 3, 3), ("rwkv3", 64, 64), ("out3", 16, 16),
    ("kv4", 4, 4), ("heads4", 16, 16), ("lru4", 16, 16), ("out4", 16, 16),
    ("gates5", 0, 1), ("heads5", 64, 64), ("out5", 16, 16),
]


def plan(names=None):
    at, b, t = {}, 0, 0
    for name, blocks, tiles in STREAM:
        if names is not None and name not in names:
            continue
        at[name] = Phase(b=b, t=t, blocks=blocks, tiles=tiles)
        b, t = b + blocks, t + tiles
    return at, b



def constants():
    p = np.arange(P)
    half, off = p // CH, p % CH
    same = (half[:, None] == half[None, :])
    row, col = off[:, None], off[None, :]
    c = {}
    c["ident"] = np.eye(P)
    c["headones"] = same * 1.0
    c["strict"] = same * (row < col)
    c["incl"] = (off[:, None] <= np.arange(CH)[None, :]) * 1.0
    c["mask1"] = same * (row < col) * (row // 2 == col // 2)
    for l in range(LEVELS):
        s = 4 << l
        c[f"level{l}"] = same * (row > col) * (row // s == col // s) * (row // (s // 2) != col // (s // 2))
    c["idstack"] = (off[:, None] == np.arange(CH)[None, :]) * 1.0
    c["zeros"] = np.zeros((P, CH))
    t = np.arange(T)
    for tt in range(TS):
        n = P * (tt + 1)
        q, k = (p + P * tt)[:, None], np.arange(n)[None, :]
        parts = []
        for window, dil in ((128, 1), (512, 4), (2048, 16)):
            d = q - k
            parts.append(np.where((d >= 0) & (d % dil == 0) & (d <= window), 0.0, MASKED))
        c[f"att{tt}"] = np.concatenate(parts, 1)
    rot = np.zeros((P, P))
    for base in (0, 64):
        for i in range(32):
            rot[base + i + 32, base + i], rot[base + i, base + i + 32] = -1.0, 1.0
    c["rotax"] = rot
    inv = (10000.0 ** (-np.arange(0, 64, 2, dtype=np.float32) / np.float32(64))).astype(np.float32)
    ang = np.zeros((P, T), np.float32)
    for i in range(P):
        pos = (t // 64 if i < 64 else t % 64).astype(np.float32)
        ang[i] = pos * inv[i % 32]
    c["axcos"], c["axsin"] = np.cos(ang), np.sin(ang)
    f = (500000.0 ** (-np.arange(0, 32, 2, dtype=np.float32) / np.float32(32))).astype(np.float32)
    c["invfreq"] = (np.where(p < 16, -1.0, np.where((p >= 32) & (p < 48), 1.0, 0.0)) * f[p % 16])[:, None]
    c["poolcnt"] = np.tile(np.concatenate(
        [1.0 / np.minimum(t + 1, w) for w in (2, 4, 8, 16)]).astype(np.float32)[None, :], (P, 1))
    c["triu"] = np.where(p[:, None] <= p[None, :], 0.0, MASKED)
    c["tril"] = np.where(p[:, None] >= p[None, :], 0.0, MASKED)
    for name, v in (("eps", 1e-6), ("lneps", 64e-5), ("ln2_8", LN2_8), ("negdecay", -0.5 * DECAY),
                    ("one", 1.0), ("halfpi", float(np.pi / 2))):
        c[name] = np.full((P, 1), v)
    return {k: np.asarray(v, np.float32) for k, v in c.items()}


ROPE_ORDER = [*range(0, 16), *range(32, 48), *range(16, 32), *range(48, P)]
RD = 64

CONST = constants()
LATER = {"attention": ["att0", "att1", "invfreq"], "pool": ["poolcnt"],
         "even": ["axcos", "axsin", "rotax"], "odd": ["triu", "tril"]}
RESIDENT = [k for k in CONST if not any(k in v for v in LATER.values())]


def place(names):
    where, w = {}, 0
    for k in names:
        where[k] = (w, CONST[k].shape[1])
        w += CONST[k].shape[1]
    return where, w


CONST_AT, NCONST = place(RESIDENT)
LATER_AT = {k: place(v)[0] for k, v in LATER.items()}
NLATER = {k: place(v)[1] for k, v in LATER.items()}

PARAMS = [("norm_w", 4 * KC), ("a_mu", 2 * 6 * KC), ("a_w0", 2 * KC), ("a_a0", 2 * KC), ("a_k_k", 2 * KC),
          ("a_k_a", 2 * KC), ("a_r_k", 2 * KC), ("a_lnx_w", 2 * KC), ("a_lnx_b", 2 * KC), ("a_v0", KC),
          ("b_qn_w", GROUPS), ("b_kn_w", GROUPS), ("c_scale", KC), ("norm_gain_2", 2 * KC),
          ("final_gain_2", KC), ("q_norm_gain_2", 1), ("k_norm_gain_2", 1), ("conv_w_2", 4 * 8),
          ("conv_b_2", 8), ("lru_ba_2", 16), ("lru_bx_2", 16), ("lru_lambda_2", 16),
          ("odd_norm_gain_2", KC), ("gate_bias", 2)]
PARAM_AT, _w = {}, 0
for _k, _v in PARAMS:
    PARAM_AT[_k] = _w
    _w += _v
NPARAM = _w


class Steps:

    def __init__(self, eng, sem):
        self.eng, self.sem, self.base, self.k, self.i, self.per = eng, sem, 0, 0, 0, 0

    def did(self, ins):
        ins.then_inc(self.sem, 1)
        self.k += 1

    def wait(self):
        self.eng.wait_ge(self.sem, self.base + self.k + (self.i * self.per if self.per else 0))

    def enter(self, i, per):
        self.base, self.k, self.i, self.per = self.base + self.k, 0, i, per

    def leave(self, turns):
        assert self.k == self.per, f"a turn has {self.k} steps, not {self.per}"
        self.base, self.k, self.i, self.per = self.base + self.per * turns, 0, 0, 0


PER = {"rwkv_scalar": 3, "rwkv_vector0": 18, "rwkv_vector1": 21}


def build(nc, a, phases=None, layers=(0, 1, 2, 3, 4, 5), final=True):
    at, nblocks = plan(phases)
    ctx = ExitStack()
    with ctx:
        def sb(name, shape, dt=F32):
            return ctx.enter_context(nc.sbuf_tensor(name, shape, dt))

        ARENA = 14700
        ring = sb("ring", [P, SLOTS, D])
        x = sb("x", [P, KC, T])
        obuf = sb("obuf", [P, KC, T])
        work = sb("work", [P, 4 * KC * T])
        arena = sb("arena", [P, ARENA])
        const = sb("consts", [P, NCONST])
        ones = sb("ones", [P, P])
        par = sb("params", [P, NPARAM])
        half = sb("half", [P, NPARAM])
        lora_w = sb("lora_w", [LORA, 3, P])
        rstd = sb("rstd", [P, T])
        lora_h = sb("lora_h", [LORA, 3, T])
        h = arena[:, 0:KC * (T + 1)].rearrange("p (k t) -> p k t", k=KC)
        HCOLS = KC * (T + 1)
        LATER0 = 4 * KC * T - max(NLATER.values())
        bank = [ctx.enter_context(nc.psum_tensor(f"bank{i}", [P, 512], F32)) for i in range(8)]
        v_first = nc.dram_tensor("v_first", [KC, P, T], F32).ap()

        def cst(name, rows=P):
            o, w = CONST_AT[name]
            return const[0:rows, o:o + w]

        def later(layer, name):
            o, w = LATER_AT[layer][name]
            return work[:, LATER0 + o:LATER0 + o + w]

        def pcol(name, i, tile=None):
            return (par if tile is None else tile)[:, bass.ds(PARAM_AT[name] + i, 1)]

        loaded = [ctx.enter_context(nc.semaphore(f"block_loaded{i}")) for i in range(SLOTS)]
        taken = [ctx.enter_context(nc.semaphore(f"tile_taken{i}")) for i in range(2)]
        x_loaded = [ctx.enter_context(nc.semaphore(f"x_loaded{q}")) for q in range(4)]
        names = (
            "tile_ready ones_ready consts_loaded half_ready act_steps dve_steps out_stored later_loaded "
            "x_tiles squares norm_sum norm_rstd square_sums h_chunks o_tiles zeros_ready final_ready "
            "mixed_chunks mixed_vg vg_scaled xx_ready lora_h_ready lora_loaded "
            "lora_ps kk_ps bonus_ps tokA_ps tokB_ps tokK_ps tokV_ps s1_ps s2_ps xt_ps yl_ps zl_ps "
            "q0_ps gh_ps r2m_ps seq_ps pt_ps mean_ps var_ps "
            "ta_ready wdec_ready kraw_ready ksq_ready kinv_ready rraw_ready ssc_ready gt_ready gs_ready "
            "at_ready abd_ready bbd_ready kbd_ready v_ready vbd_ready ars_ready rkr_ready bon_ready k2_ready "
            "tok_act tok_dve vtok_ready atri_ready arb_ready ark_ready z_ready xt_ready ym_ready "
            "q0_act q0_dve gh_act gh_dve r2m_ready sbd_ready pbd_ready y_ready yc_ready ysq_ready yrstd_ready "
            "v_stored vf_loaded vt_ready "
            "qsq_ready qstat_ps qrs_ready qn_ready rotated rope_ready scores_ps smax_ready exp_ready probs_ready "
            "probt_ps probt_ready av_ready pv_ps ggate_ready agate_ready angles_ready "
            "diff_ready pgate_tanh pgate_ready "
            "ksq2_ready kstat_ps krs_ready kn_ready krotated kv4_ready qsq4_ready vcur_ready "
            "lru_wait lam_ready lruw_loaded xl_ready xc_ready lru_ps lgate_tanh lgate_ready lrt_ready lr_ready la_ready "
            "lm_ready lsq_ready "
            "gates_dve gates_act gt_ps mh_ready mbc_ps mk_ready ms_ps me_ready "
            "mden_ps mv_ready mw_ready mpv_ps mhsq_ready mstat_ps mdn_ready mm2_ready mexp_ready mo_ready mhs_ready "
            "mrs_ready mz_ready mzs_ready").split()
        S = {n: ctx.enter_context(nc.semaphore(n)) for n in names}

        block = ctx.enter_context(nc.Block())

        def block_loaded(pe, b, turn=0, per=0):
            pe.wait_ge(loaded[b % SLOTS], turn * (16 * per // SLOTS) + 16 * (b // SLOTS + 1))

        def bank_free(pe, t, turn=0, per=0):
            if t >= 2 or per:
                pe.wait_ge(taken[t % 2], turn * (per // 2) + t // 2)

        def tile_done(eng, t, turn=0, per=0):
            eng.wait_ge(S["tile_ready"], turn * per + t + 1)

        def project(pe, rhs, b, t, turn=0, perb=0, pert=0, width=1, kc=KC, first=0):
            w = ring[:, b % SLOTS, :].rearrange("p (k n) -> p k n", k=kc)
            block_loaded(pe, b, turn, perb)
            for j in range(width):
                bank_free(pe, t + j, turn, pert)
                for k in range(kc):
                    ins = nc.tensor.matmul(bank[(t + j) % 2][:, 0:T], w[:, k, (first + j) * P:(first + j + 1) * P],
                                           rhs(k), start=(k == 0), stop=(k == kc - 1))
                ins.then_inc(S["tile_ready"], 1)

        def project_part(pe, rhs, b, t, k0, k1, turn=0, perb=0, pert=0):
            w = ring[:, b % SLOTS, :].rearrange("p (k n) -> p k n", k=KC)
            if k0 == 0:
                block_loaded(pe, b, turn, perb)
                bank_free(pe, t, turn, pert)
            for k in range(k0, k1):
                ins = nc.tensor.matmul(bank[t % 2][:, 0:T], w[:, k, :], rhs(k), start=(k == 0), stop=(k == KC - 1))
            if k1 == KC:
                ins.then_inc(S["tile_ready"], 1)

        sq = work[:, 0:KC * T].rearrange("p (k t) -> p k t", k=KC)

        def norm_scalar(act, c, n):
            if n == 0:
                for k in range(KC):
                    if k % 4 == 0:
                        act.wait_ge(x_loaded[k // 4], 16)
                    nc.scalar.activation(sq[:, k, :], x[:, k, :], ACT.Square).then_inc(S["squares"], 1)
            else:
                with act.Fori(0, KC // 2) as i:
                    for j in range(2):
                        act.wait_ge(S["x_tiles"], 2 * i + (KC * (n - 1) + j + 1))
                        nc.scalar.activation(sq[:, bass.ds(2 * i + j, 1), :].rearrange("p a t -> p (a t)"),
                                             x[:, bass.ds(2 * i + j, 1), :].rearrange("p a t -> p (a t)"),
                                             ACT.Square).then_inc(S["squares"], 1)
            nc.scalar.preload_act_table_set("natural_log_exp_and_others")
            act.wait_ge(S["norm_sum"], n + 1)
            act.wait_ge(S["half_ready"], 1)
            c.did(nc.scalar.activation(rstd[:, :], bank[3][:, 0:T], ACT.Ln, bias=cst("eps"), scale=1.0 / D))
            c.wait()
            nc.scalar.activation(rstd[:, :], rstd[:, :], ACT.Exp, scale=-0.5).then_inc(S["norm_rstd"], 1)

        def norm_tensor(pe):
            for k in range(KC):
                pe.wait_ge(S["squares"], k + 1)
                ins = nc.tensor.matmul(bank[3][:, 0:T], ones[:, :], sq[:, k, :], start=(k == 0), stop=(k == KC - 1))
            ins.then_inc(S["norm_sum"], 1)

        def norm_vector(dve, n, gain, first):
            dve.wait_ge(S["norm_rstd"], n + 1)
            nc.vector.memset(h[:, :, 0:1], 0.0)
            for k in range(KC):
                nc.vector.scalar_tensor_tensor(h[:, k, 1:T + 1], x[:, k, :], pcol(gain, first + k),
                                               rstd[:, :], ALU.mult, ALU.mult).then_inc(S["h_chunks"], 1)

        BEGUN = 2

        def out_tensor(pe, name, kc, o_needed, n, begun=0, before_last=None):
            p = at[name]
            width = KC // kc
            turn = SLOTS * width

            def arriving(k):
                if k == kc - 1 and before_last:
                    before_last()
                pe.wait_ge(S["o_tiles"], o_needed - kc + k + 1)
                return obuf[:, k, :]

            def run(b, t, i, perb, pert):
                for j in range(SLOTS):
                    for w in range(width):
                        if isinstance(i, int) and j < begun:
                            project_part(pe, arriving, b + j, t + j, KC - 1, KC)
                            continue
                        project(pe, arriving if b + j + w == p.b else (lambda k: obuf[:, k, :]), b + j, t + j * width + w, i, perb, pert, first=w, kc=kc)

            run(p.b, p.t, 0, 0, 0)
            with pe.Fori(0, p.blocks // SLOTS - 1) as i:
                run(p.b + SLOTS, p.t + turn, i, SLOTS, turn)
            pe.wait_ge(S["square_sums"], (KC - 1) * (n + 1))
            nc.tensor.matmul(bank[3][:, 0:T], ones[:, :], sq[:, 0, :], start=True, stop=True).then_inc(S["norm_sum"], 1)

        def out_vector(dve, name, n):
            p = at[name]

            def take(m, t, i, per):
                tile_done(dve, t, i, per)
                xc = x[:, bass.ds(m, 1), :].rearrange("p a t -> p (a t)")
                nc.vector.tensor_tensor(xc, bank[t % 2][:, 0:T], xc, ALU.add).then_inc(S["x_tiles"], 1)
                dve.wait_ge(S["x_tiles"], m + (n * KC + 1))
                dve.sem_inc(taken[t % 2], 1)

            def add_square(m):
                dve.wait_ge(S["squares"], m + (KC * (n + 1) + 1))
                dve.wait_ge(S["square_sums"], m + ((KC - 1) * n - 1))
                nc.vector.tensor_tensor(sq[:, 0, :], sq[:, 0, :], sq[:, bass.ds(m, 1), :].rearrange("p a t -> p (a t)"),
                                        ALU.add).then_inc(S["square_sums"], 1)

            for j in range(2):
                take(j, p.t + j, 0, 0)
            dve.wait_ge(S["squares"], KC * (n + 1) + 2)
            nc.vector.tensor_tensor(sq[:, 0, :], sq[:, 0, :], sq[:, 1, :], ALU.add).then_inc(S["square_sums"], 1)
            with dve.Fori(0, KC // 2 - 1) as i:
                for j in range(2):
                    take(2 * i + (2 + j), p.t + 2 + j, i, 2)
                    add_square(2 * i + (2 + j))

        mixed = [work[:, j * KC * T:(j + 1) * KC * T].rearrange("p (k t) -> p k t", k=KC) for j in range(4)]
        MU = "rkvgwa"
        MIX_ORDER = ("wakr", "vg")

        def wait_mixed(eng, m, L, k=KC - 1):
            for order, sig in zip(MIX_ORDER, (S["mixed_chunks"], S["mixed_vg"])):
                if m in order:
                    eng.wait_ge(sig, KC * (len(order) * L + order.index(m)) + k + 1)

        xx = arena[:, HCOLS:HCOLS + KC * T].rearrange("p (k t) -> p k t", k=KC)

        B, cur, gh_at = {}, 0, 0
        for name in "kraw ksq kkc kinv rraw vraw vf gs wdec asig bvec k2 rkr bon yc ysq".split():
            B[name] = arena[:, cur:cur + T]
            cur += T
        for name in "rd ars abd bbd kbd vbd atri ktri z xm ym vtok ghin rb rk gbd hbd r2m".split():
            B[name] = arena[:, cur:cur + 512].rearrange("p (u a c) -> p u a c", u=NU, a=2)
            gh_at = cur if name == "gbd" else gh_at
            cur += 512
        for name in ("wx", "sf"):
            B[name] = arena[:, cur:cur + NU * (CH + 1)].rearrange("p (u c) -> p u c", u=NU)
            cur += NU * (CH + 1)
        for name in ("at", "y"):
            B[name] = arena[:, cur:cur + T].rearrange("p (u c) -> p u c", u=NU)
            cur += T
        B["sbd"] = arena[:, cur:cur + P].rearrange("p (a c) -> p a c", a=2)
        B["pbd"] = arena[:, cur + P:cur + 2 * P]
        cur += 2 * P
        B["iwc"] = arena[:, cur:cur + NU]
        cur += NU
        assert cur <= ARENA, cur
        R = B
        gh = arena[:, gh_at:gh_at + 1024].rearrange("p (g u a c) -> p g u a c", g=2, u=NU, a=2)

        def chunks(v):
            return v.rearrange("p (u c) -> p u c", u=NU)

        def flat(v):
            return v.rearrange("p u a c -> p (u a c)")

        def units(v):
            return v.rearrange("p u a c -> p u (a c)")

        def both(v):
            return v.unsqueeze(2).to_broadcast([P, NU, 2, CH])

        def mask4(name):
            return cst(name).rearrange("p (a c) -> p a c", a=2).unsqueeze(1).to_broadcast([P, NU, 2, CH])

        halves = [(slice(0, CH), 0), (slice(CH, P), 1)]

        def lora_tensor(pe, L):
            p = at[f"lora{3 * L}"]
            for j, (m, src) in enumerate([("w", obuf), ("a", mixed[3]), ("v", mixed[2])][:p.tiles]):
                def chunk(k):
                    wait_mixed(pe, m, L, k)
                    return src[:, k, :]

                project(pe, chunk, p.b + j, p.t + j)

        def mix_vector(dve, c, L):
            for m, dst in zip(MIX_ORDER[0], (obuf, mixed[3], mixed[0], mixed[1])):
                for k in range(KC):
                    if m == "w":
                        dve.wait_ge(S["xx_ready"], KC * L + k + 1)
                    nc.vector.scalar_tensor_tensor(dst[:, k, :], xx[:, k, :],
                                                   pcol("a_mu", (6 * L + MU.index(m)) * KC + k), h[:, k, 1:T + 1],
                                                   ALU.mult, ALU.add).then_inc(S["mixed_chunks"], 1)

        def mix_gpsimd(pool, L):
            for k in range(KC):
                pool.wait_ge(S["h_chunks"], KC * NORM_OF[3 * L] + k + 1)
                nc.gpsimd.tensor_tensor(xx[:, k, :], h[:, k, 0:T], h[:, k, 1:T + 1], ALU.subtract)\
                    .then_inc(S["xx_ready"], 1)
            for j, dst in ((0, mixed[2]), (1, mixed[3])):
                for k in range(KC):
                    pool.wait_ge(S["vg_scaled"], KC * (2 * L + j) + k + 1)
                    nc.gpsimd.tensor_tensor(dst[:, k, :], dst[:, k, :], h[:, k, 1:T + 1], ALU.add)\
                        .then_inc(S["mixed_vg"], 1)

        def scale_scalar(act, L, m, dst):
            for k in range(KC):
                if m == "v":
                    act.wait_ge(S["xx_ready"], KC * L + k + 1)
                nc.scalar.activation(dst[:, k, :], xx[:, k, :], ACT.Copy, scale=pcol("a_mu", (6 * L + MU.index(m)) * KC + k))\
                    .then_inc(S["vg_scaled"], 1)

        def lora_scalar(act, L):
            p = at[f"lora{3 * L}"]
            for j in range(p.tiles):
                t = p.t + j
                rows = MVL if j == 2 else LORA
                tile_done(act, t)
                nc.scalar.activation(lora_h[0:rows, j, :], bank[t % 2][0:rows, 0:T], ACT.Tanh if j == 0 else ACT.Copy)\
                    .then_inc(S["lora_h_ready"], 1)
                act.wait_ge(S["lora_h_ready"], 2 * L + j + 1)
                act.sem_inc(taken[t % 2], 1)
                if j == 1:
                    scale_scalar(act, L, "g", mixed[3])

        FILL = dict(start=4, s1=2, s2=2, lx=2, ly=3, lz=3, gh=3, seqa=1, seqb=1, mean=1, var=3)

        def group_tensor(pe, L, i, ng, ns, pb, pt, first, project_it, scan_it):
            made = [0]

            def gemm(count):
                if not project_it:
                    out = at[f"out{3 * L}"]
                    for _ in range(min(count, 2)):
                        q, k = divmod(made[0], KC - 1)
                        if q == BEGUN:
                            return
                        made[0] += 1
                        if made[0] == 1:
                            pe.wait_ge(S["o_tiles"], O_BEFORE[3 * L] + KC - 1)
                        project_part(pe, lambda k: obuf[:, k, :], out.b + q, out.t + q, k, k + 1)
                    return
                for _ in range(count):
                    q, k = divmod(made[0], KC)
                    if q == 4:
                        return
                    made[0] += 1
                    b, t = pb + q, pt + q
                    if k == 0:
                        block_loaded(pe, b, i, 4)
                        bank_free(pe, t, i, 4)
                    if first:
                        wait_mixed(pe, "krvg"[q], L, k)
                    w = ring[:, b % SLOTS, :].rearrange("p (k n) -> p k n", k=KC)
                    ins = nc.tensor.matmul(bank[t % 2][:, 0:T], w[:, k, :], mixed[q][:, k, :],
                                           start=(k == 0), stop=(k == KC - 1))
                    if k == KC - 1:
                        ins.then_inc(S["tile_ready"], 1)

            def each(out_bank, lhs, rhs, sig):
                for u in range(NU):
                    ins = nc.tensor.matmul(bank[out_bank][:, u * P:(u + 1) * P], lhs[:, u, :], rhs[:, u, :],
                                           start=True, stop=True)
                ins.then_inc(sig, 1)

            def transposes(out_bank, src, sig):
                for u in range(NU):
                    ins = nc.tensor.transpose(bank[out_bank][:, u * P:(u + 1) * P], src[:, u, :], cst("ident"))
                ins.then_inc(sig, 1)

            def kk_norm():
                pe.wait_ge(S["ksq_ready"], ng)
                if L:
                    pe.wait_ge(S["vt_ready"], ng - KC)
                elif scan_it:
                    pe.wait_ge(S["bon_ready"], ns)
                nc.tensor.matmul(bank[3][:, 0:T], cst("headones"), R["ksq"], start=True, stop=True)\
                    .then_inc(S["kk_ps"], 1)

            def lora():
                pe.wait_ge(S["lora_loaded"], 16 * ng)
                if first:
                    p = at[f"lora{3 * L}"]
                    pe.wait_ge(S["lora_h_ready"], [2, 5][L])
                if scan_it:
                    pe.wait_ge(S["bon_ready"], ns)
                elif L:
                    pe.wait_ge(S["yrstd_ready"], ns)
                nc.tensor.matmul(bank[2][:, 0:T], lora_w[:, 0, :], lora_h[:, 0, :], start=True, stop=True)
                ins = nc.tensor.matmul(bank[2][:, T:2 * T], lora_w[:, 1, :], lora_h[:, 1, :], start=True, stop=True)
                if L:
                    ins = nc.tensor.matmul(bank[3][:, T:2 * T], lora_w[0:MVL, 2, :], lora_h[0:MVL, 2, :],
                                           start=True, stop=True)
                ins.then_inc(S["lora_ps"], 1)

            ars, atri, ktri, z, xm, ym = (units(v) for v in (R["ars"], R["atri"], R["ktri"], R["z"], R["xm"], R["ym"]))
            vtok, ghin, rb, rk, gbd, hbd, r2m = (units(v) for v in (R["vtok"], R["ghin"], R["rb"], R["rk"], R["gbd"], R["hbd"], R["r2m"]))
            if not scan_it:
                gemm(KC)
                lora()
                gemm(KC)
                kk_norm()
                gemm(2 * KC)
                return
            pe.wait_ge(S["rkr_ready"], ns)
            nc.tensor.matmul(bank[3][:, 0:T], cst("headones"), R["rkr"], start=True, stop=True).then_inc(S["bonus_ps"], 1)
            pe.wait_ge(S["abd_ready"], ns)
            transposes(4, units(R["abd"]), S["tokA_ps"])
            pe.wait_ge(S["bbd_ready"], ns)
            transposes(5, units(R["bbd"]), S["tokB_ps"])
            pe.wait_ge(S["kbd_ready"], ns)
            transposes(6, units(R["kbd"]), S["tokK_ps"])
            pe.wait_ge(S["vbd_ready"], ns)
            transposes(7, units(R["vbd"]), S["tokV_ps"])
            gemm(FILL["start"])
            pe.wait_ge(S["ars_ready"], ns)
            pe.wait_ge(S["tok_act"], 3 * ns - 2)
            pe.wait_ge(S["tok_dve"], 3 * ns - 2)
            each(4, units(R["bbd"]), ars, S["s1_ps"])
            gemm(FILL["s1"])
            pe.wait_ge(S["tok_act"], 3 * ns - 1)
            pe.wait_ge(S["tok_dve"], 3 * ns - 1)
            each(5, units(R["kbd"]), ars, S["s2_ps"])
            gemm(FILL["s2"])
            pe.wait_ge(S["tok_act"], 3 * ns)
            pe.wait_ge(S["tok_dve"], 3 * ns)
            pe.wait_ge(S["z_ready"], (LEVELS + 1) * ns - LEVELS)
            transposes(6, z, S["xt_ps"])
            if project_it:
                lora()
            pe.wait_ge(S["vtok_ready"], ns)
            pe.wait_ge(S["arb_ready"], ns)
            for l in range(LEVELS):
                gemm(FILL["lx"])
                if project_it and l == 3:
                    kk_norm()
                pe.wait_ge(S["xt_ready"], LEVELS * ns - LEVELS + 1 + l)
                each(7, atri, xm, S["yl_ps"])
                gemm(FILL["ly"])
                pe.wait_ge(S["ym_ready"], LEVELS * ns - LEVELS + 1 + l)
                each(4, ym, z, S["zl_ps"])
                gemm(FILL["lz"])
                if l == 0:
                    pe.wait_ge(S["ark_ready"], ns)
                    each(5, ktri, vtok, S["q0_ps"])
                pe.wait_ge(S["z_ready"], (LEVELS + 1) * ns - LEVELS + 1 + l)
                if l < LEVELS - 1:
                    transposes(6, z, S["xt_ps"])
            pe.wait_ge(S["q0_act"], ns)
            pe.wait_ge(S["q0_dve"], ns)
            each(7, z, ghin, S["gh_ps"])
            gemm(FILL["gh"])
            pe.wait_ge(S["gh_act"], ns)
            pe.wait_ge(S["gh_dve"], ns)
            each(4, gbd, rb, S["r2m_ps"])
            for u in range(NU):
                o = bank[5 + u % 2][:, 0:P]
                if u >= 2:
                    pe.wait_ge(S["y_ready"], NU * ns - NU + u - 1)
                nc.tensor.matmul(o, hbd[:, u, :], rb[:, u, :], start=True, stop=False)
                ins = nc.tensor.matmul(o, vtok[:, u, :], rk[:, u, :], start=False, stop=(u == 0))
                gemm(FILL["seqa"])
                if u:
                    if u == 1:
                        pe.wait_ge(S["r2m_ready"], ns)
                    pe.wait_ge(S["pbd_ready"], (NU - 1) * ns - NU + 1 + u)
                    ins = nc.tensor.matmul(o, R["pbd"], r2m[:, u, :], start=False, stop=True)
                ins.then_inc(S["seq_ps"], 1)
                gemm(FILL["seqb"])
                if u < NU - 1:
                    pe.wait_ge(S["sbd_ready"], (NU - 1) * ns - NU + 2 + u)
                    nc.tensor.transpose(bank[7][:, 0:P], R["sbd"].rearrange("p a c -> p (a c)"), cst("ident"))\
                        .then_inc(S["pt_ps"], 1)
            gemm(FILL["mean"])
            pe.wait_ge(S["y_ready"], NU * ns)
            if project_it:
                pe.wait_ge(S["wdec_ready"], ng)
            nc.tensor.matmul(bank[2][:, 0:T], cst("headones"), R["y"].rearrange("p u c -> p (u c)"),
                             start=True, stop=True).then_inc(S["mean_ps"], 1)
            gemm(FILL["var"])
            pe.wait_ge(S["ysq_ready"], ns)
            nc.tensor.matmul(bank[2][:, 0:T], cst("headones"), R["ysq"], start=True, stop=True).then_inc(S["var_ps"], 1)
            gemm(4 * KC)

        def release(eng, sig, n, t):
            eng.wait_ge(sig, n)
            eng.sem_inc(taken[t % 2], 1)

        def gh_diagonal(rows, blk):
            return gh[rows, :, :, blk, :]

        def gh_product(rows):
            return bank[7][rows, :].rearrange("p (u a c) -> p a u c", u=NU, a=2)

        def group_scalar(act, c, L, i, ng, ns, jg, js, pt, first, project_it, scan_it):
            def half_rows(dst, b, ps, sig):
                rows, _ = halves[0]
                act.wait_ge(ps, ns)
                nc.scalar.copy(dst[rows], bank[b][rows, :].rearrange("p (u a c) -> p u a c", u=NU, a=2)[:, :, 0, :])\
                    .then_inc(sig, 1)

            def lora():
                if not (first and L == 0):
                    act.wait_ge(S["k2_ready"], ng - 1)
                act.wait_ge(S["lora_ps"], ng)
                if L:
                    nc.scalar.activation(R["ysq"], bank[3][:, T:2 * T], ACT.Tanh, bias=pcol("a_v0", jg, half), scale=0.5)\
                        .then_inc(S["vt_ready"], 1)
                nc.scalar.activation(R["asig"], bank[2][:, T:2 * T], ACT.Tanh, bias=pcol("a_a0", L * KC + jg, half),
                                     scale=0.5).then_inc(S["ta_ready"], 1)
                c.did(nc.scalar.activation(R["wdec"], bank[2][:, 0:T], ACT.Tanh, bias=pcol("a_w0", L * KC + jg, half),
                                           scale=0.5))
                c.wait()
                nc.scalar.activation(R["wdec"], R["wdec"], ACT.Exp, bias=cst("negdecay"), scale=-0.5 * DECAY)\
                    .then_inc(S["wdec_ready"], 1)

            def k_tile():
                tile_done(act, pt, i, 4)
                if not (first and L == 0):
                    act.wait_ge(S["k2_ready"], ng - 1)
                nc.scalar.copy(R["kraw"], bank[pt % 2][:, 0:T]).then_inc(S["kraw_ready"], 1)
                release(act, S["kraw_ready"], ng, pt)
                nc.scalar.activation(R["ksq"], R["kraw"], ACT.Square, scale=pcol("a_k_k", L * KC + jg))\
                    .then_inc(S["ksq_ready"], 1)

            def kk_inverse():
                nc.scalar.preload_act_table_set("natural_log_exp_and_others")
                act.wait_ge(S["ssc_ready"], ng)
                c.did(nc.scalar.activation(R["kinv"], R["kinv"], ACT.Ln, scale=65536.0))
                c.wait()
                nc.scalar.activation(R["kinv"], R["kinv"], ACT.Exp, bias=cst("ln2_8"), scale=-0.5).then_inc(S["kinv_ready"], 1)

            def r_tile():
                tile_done(act, pt + 1, i, 4)
                nc.scalar.copy(R["rraw"], bank[(pt + 1) % 2][:, 0:T]).then_inc(S["rraw_ready"], 1)
                release(act, S["rraw_ready"], ng, pt + 1)

            def a_blocks():
                act.wait_ge(S["at_ready"], ng)
                for rows, blk in halves:
                    ins = nc.scalar.copy(R["abd"][rows, :, blk, :], R["at"][rows])
                ins.then_inc(S["abd_ready"], 1)

            if scan_it:
                half_rows(R["ghin"][:, :, 0, :], 4, S["tokA_ps"], S["tok_act"])
                half_rows(R["rb"][:, :, 1, :], 5, S["tokB_ps"], S["tok_act"])
                half_rows(R["rk"][:, :, 1, :], 6, S["tokK_ps"], S["tok_act"])
                act.wait_ge(S["tokV_ps"], ns)
                nc.scalar.copy(flat(R["vtok"]), bank[7][:, :]).then_inc(S["vtok_ready"], 1)
                tile_done(act, pt - 1, i, 4)
                act.wait_ge(S["bon_ready"], ns)
                nc.scalar.activation(R["gs"], bank[(pt - 1) % 2][:, 0:T], ACT.Tanh, scale=0.5).then_inc(S["gt_ready"], 1)
                for l in range(LEVELS):
                    act.wait_ge(S["xt_ps"], LEVELS * ns - LEVELS + 1 + l)
                    nc.scalar.copy(flat(R["xm"]), bank[6][:, :]).then_inc(S["xt_ready"], 1)
                    if project_it and l == 0:
                        lora()
                    if l == 1:
                        half_rows(R["ghin"][:, :, 1, :], 5, S["q0_ps"], S["q0_act"])
                    if project_it and l == 2:
                        k_tile()
            else:
                lora()
                k_tile()
            if project_it:
                r_tile()
                kk_inverse()
            if scan_it:
                rows, blk = halves[0]
                act.wait_ge(S["gh_ps"], ns)
                nc.scalar.copy(gh_diagonal(rows, blk), gh_product(rows)).then_inc(S["gh_act"], 1)
            if project_it:
                a_blocks()
            if scan_it:
                for u in range(NU - 1):
                    act.wait_ge(S["pt_ps"], (NU - 1) * ns - NU + 2 + u)
                    nc.scalar.copy(R["pbd"], bank[7][:, 0:P]).then_inc(S["pbd_ready"], 1)
            if project_it:
                tv = pt + 2
                if L == 0:
                    tile_done(act, tv, i, 4)
                    if scan_it:
                        act.wait_ge(S["bon_ready"], ns)
                        act.wait_ge(S["v_stored"], 16 * ns)
                    nc.scalar.copy(R["vraw"], bank[tv % 2][:, 0:T]).then_inc(S["v_ready"], 1)
                    release(act, S["v_ready"], ng, tv)
                else:
                    act.wait_ge(S["v_ready"], ng)
                for rows, blk in halves:
                    ins = nc.scalar.copy(R["vbd"][rows, :, blk, :], chunks(R["vraw"])[rows])
                ins.then_inc(S["vbd_ready"], 1)
            if scan_it:
                act.wait_ge(S["yc_ready"], ns)
                nc.scalar.activation(R["ysq"], R["yc"], ACT.Square).then_inc(S["ysq_ready"], 1)
                act.wait_ge(S["var_ps"], ns)
                c.did(nc.scalar.activation(R["ysq"], bank[2][:, 0:T], ACT.Ln, bias=cst("lneps"), scale=1.0 / CH))
                c.wait()
                nc.scalar.activation(R["ysq"], R["ysq"], ACT.Exp, scale=-0.5).then_inc(S["yrstd_ready"], 1)

        def group_vector(dve, c, L, i, ng, ns, jg, js, pt, first, project_it, scan_it):
            def half_rows(dst, b, ps, sig):
                rows, _ = halves[1]
                dve.wait_ge(ps, ns)
                nc.vector.tensor_copy(dst[rows], bank[b][rows, :].rearrange("p (u a c) -> p u a c", u=NU, a=2)[:, :, 1, :])\
                    .then_inc(sig, 1)

            def psum4(b):
                return bank[b][:, :].rearrange("p (u a c) -> p u a c", u=NU, a=2)

            def decays():
                dve.wait_ge(S["ta_ready"], ng)
                c.did(nc.vector.tensor_scalar(R["asig"], R["asig"], 0.5, 0.5, ALU.mult, ALU.add))
                dve.wait_ge(S["wdec_ready"], ng)
                w = chunks(R["wdec"])
                for u in range(NU):
                    c.did(nc.vector.tensor_tensor_scan(R["wx"][:, u, 1:CH + 1], w[:, u, :], cst("zeros"), 1.0,
                                                       ALU.mult, ALU.add))
                    c.did(nc.vector.tensor_tensor_scan(R["sf"][:, u, CH - 1::-1], w[:, u, ::-1], cst("zeros"), 1.0,
                                                       ALU.mult, ALU.add))
                c.wait()
                c.did(nc.vector.reciprocal(R["iwc"], R["wx"][:, :, CH]))

            def kk_floor():
                dve.wait_ge(S["kk_ps"], ng)
                nc.vector.tensor_scalar(R["kinv"], bank[3][:, 0:T], 1e-24, None, ALU.max).then_inc(S["ssc_ready"], 1)

            def prep_a():
                dve.wait_ge(S["kinv_ready"], ng)
                c.did(nc.vector.scalar_tensor_tensor(R["kkc"], R["kraw"], pcol("a_k_k", L * KC + jg), R["kinv"],
                                                     ALU.mult, ALU.mult))
                c.wait()
                nc.vector.scalar_tensor_tensor(R["at"], R["wx"][:, :, 0:CH], -1.0, chunks(R["kkc"]), ALU.mult, ALU.mult)\
                    .then_inc(S["at_ready"], 1)

            def prep_bk():
                nc.vector.tensor_tensor(R["bvec"], R["kkc"], R["asig"], ALU.mult)
                c.did(nc.vector.tensor_scalar(R["k2"], R["asig"], 1.0, pcol("a_k_a", L * KC + jg), ALU.subtract, ALU.mult))
                c.wait()
                nc.vector.scalar_tensor_tensor(R["k2"], R["k2"], 1.0, R["kraw"], ALU.add, ALU.mult).then_inc(S["k2_ready"], 1)

            def prep_b():
                for rows, blk in halves:
                    ins = nc.vector.tensor_tensor(R["bbd"][rows, :, blk, :], chunks(R["bvec"])[rows], R["sf"][rows, :, 1:CH + 1],
                                                  ALU.mult)
                ins.then_inc(S["bbd_ready"], 1)

            def prep_k():
                dve.wait_ge(S["k2_ready"], ng)
                for rows, blk in halves:
                    ins = nc.vector.tensor_tensor(R["kbd"][rows, :, blk, :], chunks(R["k2"])[rows], R["sf"][rows, :, 1:CH + 1],
                                                  ALU.mult)
                ins.then_inc(S["kbd_ready"], 1)

            def prep_r():
                dve.wait_ge(S["rraw_ready"], ng)
                nc.vector.scalar_tensor_tensor(R["rkr"], R["rraw"], pcol("a_r_k", L * KC + jg), R["k2"], ALU.mult, ALU.mult)\
                    .then_inc(S["rkr_ready"], 1)
                c.did(nc.vector.tensor_tensor(R["rd"][:, :, 0, :], R["wx"][:, :, 1:CH + 1], chunks(R["rraw"]), ALU.mult))
                c.did(nc.vector.tensor_tensor(R["rd"][:, :, 1, :], cst("idstack").unsqueeze(1).to_broadcast([P, NU, CH]),
                                              R["wx"][:, :, CH:CH + 1].to_broadcast([P, NU, CH]), ALU.mult))
                dve.wait_ge(S["at_ready"], ng)
                inv = R["iwc"].unsqueeze(2).to_broadcast([P, NU, CH])
                nc.vector.tensor_tensor(R["ars"][:, :, 0, :], R["at"], inv, ALU.mult)
                c.wait()
                nc.vector.tensor_tensor(R["ars"][:, :, 1, :], R["rd"][:, :, 0, :], inv, ALU.mult).then_inc(S["ars_ready"], 1)

            if scan_it:
                half_rows(R["ghin"][:, :, 0, :], 4, S["tokA_ps"], S["tok_dve"])
                half_rows(R["rb"][:, :, 1, :], 5, S["tokB_ps"], S["tok_dve"])
                half_rows(R["rk"][:, :, 1, :], 6, S["tokK_ps"], S["tok_dve"])
                dve.wait_ge(S["bonus_ps"], ns)
                dve.wait_ge(S["v_ready"], ns)
                nc.vector.tensor_tensor(R["bon"], bank[3][:, 0:T], R["vraw"], ALU.mult).then_inc(S["bon_ready"], 1)
                dve.wait_ge(S["s1_ps"], ns)
                nc.vector.tensor_tensor(R["atri"], both(psum4(4)[:, :, 0, :]), mask4("strict"), ALU.mult)\
                    .then_inc(S["atri_ready"], 1)
                nc.vector.tensor_tensor(R["rb"][:, :, 0, :], psum4(4)[:, :, 1, :],
                                        cst("incl").unsqueeze(1).to_broadcast([P, NU, CH]), ALU.mult)\
                    .then_inc(S["arb_ready"], 1)
                dve.wait_ge(S["atri_ready"], ns)
                c.did(nc.vector.tensor_tensor(R["z"], R["atri"], mask4("mask1"), ALU.mult))
                c.wait()
                nc.vector.tensor_tensor(R["z"], R["z"], mask4("ident"), ALU.add).then_inc(S["z_ready"], 1)
                dve.wait_ge(S["s2_ps"], ns)
                nc.vector.tensor_tensor(R["ktri"], both(psum4(5)[:, :, 0, :]), mask4("strict"), ALU.mult)
                nc.vector.tensor_tensor(R["rk"][:, :, 0, :], psum4(5)[:, :, 1, :],
                                        cst("incl").unsqueeze(1).to_broadcast([P, NU, CH]), ALU.mult)\
                    .then_inc(S["ark_ready"], 1)
                for l in range(LEVELS):
                    dve.wait_ge(S["yl_ps"], LEVELS * ns - LEVELS + 1 + l)
                    nc.vector.tensor_tensor(R["ym"], psum4(7), mask4(f"level{l}"), ALU.mult).then_inc(S["ym_ready"], 1)
                    if project_it and l == 0:
                        decays()
                    if l == 0:
                        dve.wait_ge(S["gt_ready"], ns)
                        nc.vector.scalar_tensor_tensor(R["gs"], R["gs"], 1.0, bank[(pt - 1) % 2][:, 0:T], ALU.add, ALU.mult)\
                            .then_inc(S["gs_ready"], 1)
                        release(dve, S["gs_ready"], ns, pt - 1)
                    if l == 1:
                        half_rows(R["ghin"][:, :, 1, :], 5, S["q0_ps"], S["q0_dve"])
                    dve.wait_ge(S["zl_ps"], LEVELS * ns - LEVELS + 1 + l)
                    dve.wait_ge(S["z_ready"], (LEVELS + 1) * ns - LEVELS + l)
                    nc.vector.tensor_tensor(R["z"], psum4(4), R["z"], ALU.add).then_inc(S["z_ready"], 1)
                    if project_it and l == 3:
                        kk_floor()
                rows, blk = halves[1]
                dve.wait_ge(S["gh_ps"], ns)
                nc.vector.tensor_copy(gh_diagonal(rows, blk), gh_product(rows)).then_inc(S["gh_dve"], 1)
            else:
                decays()
                kk_floor()
            if project_it:
                prep_a()
            if scan_it:
                dve.wait_ge(S["r2m_ps"], ns)
                nc.vector.tensor_tensor(R["r2m"], psum4(4), R["rd"], ALU.add).then_inc(S["r2m_ready"], 1)
                for u in range(NU):
                    dve.wait_ge(S["seq_ps"], NU * ns - NU + 1 + u)
                    o = bank[5 + u % 2]
                    if u < NU - 1:
                        nc.vector.tensor_tensor(R["sbd"], o[:, CH:P].unsqueeze(1).to_broadcast([P, 2, CH]),
                                                cst("headones").rearrange("p (a c) -> p a c", a=2), ALU.mult)\
                            .then_inc(S["sbd_ready"], 1)
                    nc.vector.tensor_copy(R["y"][:, u, :], o[:, 0:CH]).then_inc(S["y_ready"], 1)
                    if project_it and u < NU - 1:
                        (prep_bk, prep_b, prep_k)[u]()
            elif project_it:
                prep_bk()
                prep_b()
                prep_k()
            if project_it and L:
                tv = bank[(pt + 2) % 2][:, 0:T]
                dve.wait_ge(S["vt_ready"], ng - KC)
                c.did(nc.vector.tensor_scalar(R["ysq"], R["ysq"], 0.5, 0.5, ALU.mult, ALU.add))
                dve.wait_ge(S["vf_loaded"], 16 * (ng - KC))
                tile_done(dve, pt + 2, i, 4)
                c.did(nc.vector.scalar_tensor_tensor(R["vf"], tv, -1.0, R["vf"], ALU.mult, ALU.add))
                c.wait()
                c.did(nc.vector.tensor_tensor(R["vf"], R["vf"], R["ysq"], ALU.mult))
                c.wait()
                nc.vector.tensor_tensor(R["vraw"], tv, R["vf"], ALU.add).then_inc(S["v_ready"], 1)
                release(dve, S["v_ready"], ng, pt + 2)
            if scan_it:
                dve.wait_ge(S["mean_ps"], ns)
                dve.wait_ge(S["y_ready"], NU * ns)
                nc.vector.scalar_tensor_tensor(R["yc"], bank[2][:, 0:T], -1.0 / CH, R["y"].rearrange("p u c -> p (u c)"),
                                               ALU.mult, ALU.add).then_inc(S["yc_ready"], 1)
            if project_it:
                prep_r()
            if scan_it:
                dve.wait_ge(S["yrstd_ready"], ns)
                dve.wait_ge(S["yc_ready"], ns)
                c.did(nc.vector.tensor_tensor(R["yc"], R["yc"], R["ysq"], ALU.mult))
                c.wait()
                c.did(nc.vector.tensor_scalar(R["yc"], R["yc"], pcol("a_lnx_w", L * KC + js), pcol("a_lnx_b", L * KC + js),
                                              ALU.mult, ALU.add))
                c.wait()
                dve.wait_ge(S["bon_ready"], ns)
                c.did(nc.vector.tensor_tensor(R["yc"], R["yc"], R["bon"], ALU.add))
                c.wait()
                dve.wait_ge(S["gs_ready"], ns)
                nc.vector.scalar_tensor_tensor(obuf[:, bass.ds(js, 1), :].rearrange("p a t -> p (a t)"), R["yc"], 0.5,
                                               R["gs"], ALU.mult, ALU.mult).then_inc(S["o_tiles"], 1)

        def groups(L, eng, run, c=None, per=0):
            p, base = at[f"rwkv{3 * L}"], KC * L
            run(0, base + 1, base, 0, -1, p.b, p.t, True, True, False)
            with eng.Fori(0, KC - 1) as i:
                if c:
                    c.enter(i, per)
                run(i, i + (base + 2), i + (base + 1), i + 1, i, p.b + 4, p.t + 4, False, True, True)
            if c:
                c.leave(KC - 1)
            run(0, base + KC + 1, base + KC, KC, KC - 1, p.b + 4 * KC, p.t + 4 * KC, False, False, True)

        def rwkv_tensor(pe, L, n):
            lora_tensor(pe, L)
            groups(L, pe, lambda i, ng, ns, jg, js, pb, pt, first, pr, sc:
                   group_tensor(pe, L, i, ng, ns, pb, pt, first, pr, sc))
            out_tensor(pe, f"out{3 * L}", KC, O_BEFORE[3 * L] + KC, n, BEGUN)

        def rwkv_scalar(act, c, L, n):
            norm_scalar(act, c, n)
            scale_scalar(act, L, "v", mixed[2])
            lora_scalar(act, L)
            act.wait_ge(S["zeros_ready"], L + 1)
            groups(L, act, lambda i, ng, ns, jg, js, pb, pt, first, pr, sc:
                   group_scalar(act, c, L, i, ng, ns, jg, js, pt, first, pr, sc), c, PER["rwkv_scalar"])

        def rwkv_vector(dve, c, L, n):
            norm_vector(dve, n, "norm_w", 3 * L * KC)
            mix_vector(dve, c, L)
            wait_mixed(dve, "r", L)
            wait_mixed(dve, "g", L)
            for v in (R["abd"], R["bbd"], R["kbd"], R["vbd"], R["gbd"], R["hbd"]):
                nc.vector.memset(flat(v), 0.0)
            nc.vector.memset(R["wx"][:, :, 0:1], 1.0)
            nc.vector.memset(R["sf"][:, :, CH:CH + 1], 1.0).then_inc(S["zeros_ready"], 1)
            dve.wait_ge(S["zeros_ready"], L + 1)
            groups(L, dve, lambda i, ng, ns, jg, js, pb, pt, first, pr, sc:
                   group_vector(dve, c, L, i, ng, ns, jg, js, pt, first, pr, sc), c, PER[f"rwkv_vector{L}"])
            out_vector(dve, f"out{3 * L}", n)
            if L == 0:
                dve.wait_ge(S["v_stored"], 16 * KC)

        def rwkv_gpsimd(pool, L):
            base = KC * L

            def one(j, n, first):
                if not first:
                    pool.wait_ge(S["lora_ps"], n - 1)
                    if L:
                        pool.wait_ge(S["v_ready"], n - 1)
                    pool.dma_start(lora_w[:, :, :], a["lora2"][L, bass.ds(j, 1)].rearrange("a p s n -> p (a s) n"))\
                        .then_inc(S["lora_loaded"], 16)
                if L:
                    if first:
                        pool.wait_ge(S["zeros_ready"], L + 1)
                    pool.dma_start(R["vf"], v_first[bass.ds(j, 1)].rearrange("a p t -> p (a t)")).then_inc(S["vf_loaded"], 16)
                else:
                    pool.wait_ge(S["v_ready"], n)
                    pool.dma_start(v_first[bass.ds(j, 1)].rearrange("a p t -> p (a t)"), R["vraw"])\
                        .then_inc(S["v_stored"], 16)

            if L:
                pool.wait_ge(S["lora_ps"], base)
            pool.dma_start(lora_w[:, :, :], a["lora2"][L, 0:1].rearrange("a p s n -> p (a s) n"))\
                .then_inc(S["lora_loaded"], 16)
            mix_gpsimd(pool, L)
            one(0, base + 1, True)
            with pool.Fori(0, KC - 1) as i:
                one(i + 1, i + (base + 2), False)
            if L == 0:
                pool.wait_ge(S["v_stored"], 16 * KC)

        def final_scalar(act, c, n):
            norm_scalar(act, c, n)
            act.wait_ge(S["final_ready"], 1)
            act.dma_start(a["out"], obuf[:, :, :]).then_inc(S["out_stored"], 16)
            act.wait_ge(S["out_stored"], 16)

        def final_vector(dve, c, n):
            dve.wait_ge(S["norm_rstd"], n + 1)
            for k in range(KC):
                ins = nc.vector.scalar_tensor_tensor(obuf[:, k, :], x[:, k, :], pcol("final_gain_2", k),
                                                     rstd[:, :], ALU.mult, ALU.mult)
            ins.then_inc(S["final_ready"], 1)

        def heads(eng, p, base, run, tail, c=None, per=0):
            nb, nt = p.blocks // HEADS, p.tiles // HEADS
            for hh in range(2):
                run(0, base + hh + 1, hh, p.b + hh * nb, p.t + hh * nt, hh == 0)
            with eng.Fori(0, HEADS // 2 - 1) as i:
                if c:
                    c.enter(i, per)
                for hh in range(2):
                    run(i, i * 2 + (base + hh + 3), i * 2 + (hh + 2), p.b + (hh + 2) * nb, p.t + (hh + 2) * nt, False)
            if c:
                c.leave(HEADS // 2 - 1)
            if tail:
                tail(base + HEADS + 1, HEADS)

        def token_tile(pe, b, t, turn=0, perb=0, pert=0):
            w = ring[:, b % SLOTS, :].rearrange("p (k n) -> p k n", k=KC)
            block_loaded(pe, b, turn, perb)
            bank_free(pe, t, turn, pert)
            for tt in range(TS):
                for k in range(KC):
                    ins = nc.tensor.matmul(bank[t % 2][:, tt * P:(tt + 1) * P], h[:, k, 1 + tt * P:1 + (tt + 1) * P],
                                           w[:, k, :], start=(k == 0), stop=(k == KC - 1))
            ins.then_inc(S["tile_ready"], 1)

        def hk(k):
            return h[:, k, 1:T + 1]

        def hk_arriving(pe, l):
            def chunk(k):
                pe.wait_ge(S["h_chunks"], KC * NORM_OF[l] + k + 1)
                return hk(k)
            return chunk

        def bank_now_free(eng, t, turn=0, per=0):
            eng.wait_ge(taken[t % 2], turn * (per // 2) + t // 2 + 1)

        def wcarve(at0, sizes):
            out = {}
            for name, dims in sizes.items():
                n = int(np.prod(dims))
                v = work[:, at0:at0 + n]
                if len(dims) > 1:
                    names = "abcd"[:len(dims)]
                    v = v.rearrange("p (" + " ".join(names) + ") -> p " + " ".join(names), **dict(zip(names, dims)))
                out[name] = v
                at0 += n
            assert at0 <= LATER0, at0
            return out

        NQ = 2 * GROUPS
        NS = [GROUPS * P, GROUPS * T]
        NB = 3 * GROUPS
        Q = wcarve(KC * T, dict(qk=(NQ, T), sq=(NQ, T), rs=(NQ, T), t1=(NQ, T), v=(GROUPS, T), sc=(NS[0] + NS[1],),
                                pt=(NB, P), gs=(T,), cos=(T,), sin=(T,), pos=(T,), mx=(TS,), sum=(TS,), inv=(TS,)))
        ATT_SCALE = float(P) ** -0.5
        span = [slice(0, NS[0]), slice(NS[0], NS[0] + NS[1])]

        def att_tensor(pe, n):
            p = at["heads1"]
            base = HEAD_BASE[1]

            def finish(n):
                pe.wait_ge(S["probs_ready"], n)
                for g in range(GROUPS):
                    for j, src in ((2 * g, slice(g * P, (g + 1) * P)),
                                   (2 * g + 1, slice(NS[0] + g * T, NS[0] + g * T + P)),
                                   (2 * GROUPS + g, slice(NS[0] + g * T + P, NS[0] + (g + 1) * T))):
                        ins = nc.tensor.transpose(bank[2 + j // 4][:, (j % 4) * P:(j % 4 + 1) * P], Q["sc"][:, src],
                                                  cst("ident"))
                ins.then_inc(S["probt_ps"], 1)
                pe.wait_ge(S["probt_ready"], n)
                pe.wait_ge(S["av_ready"], GROUPS * n)
                for g in range(GROUPS):
                    nc.tensor.matmul(bank[5][:, 0:T], Q["v"][:, g, 0:P], Q["pt"][:, 2 * g:2 * g + 2, :],
                                     start=(g == 0), stop=False)
                for g in range(GROUPS):
                    ins = nc.tensor.matmul(bank[5][:, P:T], Q["v"][:, g, P:T], Q["pt"][:, 2 * GROUPS + g, :],
                                           start=False, stop=(g == GROUPS - 1))
                ins.then_inc(S["pv_ps"], 1)

            def run(i, n, hh, b, t, first):
                for j in range(NQ):
                    project(pe, hk_arriving(pe, 1) if first and j == 0 else hk, b + j, t + j, i, 20, 20)
                if not first:
                    finish(n - 1)
                pe.wait_ge(S["qsq_ready"], NQ * n)
                for j in range(GROUPS):
                    ins = nc.tensor.matmul(bank[2 + j][:, :], ones[:, :], Q["sq"][:, 2 * j:2 * j + 2, :],
                                           start=True, stop=True)
                ins.then_inc(S["qstat_ps"], 1)
                token_tile(pe, b + 6, t + 6, i, 20, 20)
                token_tile(pe, b + 7, t + 7, i, 20, 20)
                pe.wait_ge(S["rope_ready"], n)
                if not first:
                    pe.wait_ge(S["o_tiles"], O_BEFORE[1] + (n - base - 1))
                for g in range(GROUPS):
                    nc.tensor.matmul(bank[5][:, g * P:(g + 1) * P], Q["qk"][:, g, 0:P], Q["qk"][:, GROUPS + g, 0:P],
                                     start=True, stop=True)
                for g in range(GROUPS):
                    o = bank[6][:, g * T:(g + 1) * T] if g < 2 else bank[7][:, 0:T]
                    ins = nc.tensor.matmul(o, Q["qk"][:, g, P:T], Q["qk"][:, GROUPS + g, :], start=True, stop=True)
                ins.then_inc(S["scores_ps"], 1)
                token_tile(pe, b + 8, t + 8, i, 20, 20)
                project(pe, hk, b + 9, t + 9, i, 20, 20)

            heads(pe, p, base, run, None)
            out_tensor(pe, "out1", HEADS, O_BEFORE[1] + HEADS, n, before_last=lambda: finish(base + HEADS))

        def att_scalar(act, c, n):
            norm_scalar(act, c, n)
            p = at["heads1"]
            base = HEAD_BASE[1]

            act.wait_ge(S["angles_ready"], 1)
            nc.scalar.activation(Q["sin"][0:RD], Q["sin"][0:RD], ACT.Sin)
            nc.scalar.activation(Q["cos"][0:RD], Q["cos"][0:RD], ACT.Sin).then_inc(S["angles_ready"], 1)

            def finish(n):
                act.wait_ge(S["probt_ps"], n)
                for j, m in ((0, 4), (1, 4), (2, 1)):
                    ins = nc.scalar.copy(Q["pt"][:, 4 * j:4 * j + m, :],
                                         bank[2 + j][:, 0:m * P].rearrange("p (a b) -> p a b", a=m))
                ins.then_inc(S["probt_ready"], 1)

            def run(i, n, hh, b, t, first):
                for j in range(NQ):
                    tile_done(act, t + j, i, 20)
                    if not first and j == 0:
                        act.wait_ge(S["scores_ps"], n - 1)
                    nc.scalar.copy(Q["qk"][:, j, :], bank[(t + j) % 2][:, 0:T]).then_inc(taken[(t + j) % 2], 1)
                    bank_now_free(act, t + j, i, 20)
                    nc.scalar.activation(Q["sq"][:, j, :], Q["qk"][:, j, :], ACT.Square).then_inc(S["qsq_ready"], 1)
                if not first:
                    finish(n - 1)
                act.wait_ge(S["qstat_ps"], n)
                for j in range(GROUPS):
                    ins = nc.scalar.activation(Q["rs"][:, 2 * j:2 * j + 2, :],
                                               bank[2 + j][:, :].rearrange("p (a b) -> p a b", a=2), ACT.Ln,
                                               bias=cst("eps"), scale=1.0 / P)
                c.did(ins)
                c.wait()
                nc.scalar.activation(Q["rs"], Q["rs"], ACT.Exp, scale=-0.5).then_inc(S["qrs_ready"], 1)
                act.wait_ge(S["qn_ready"], n)
                nc.scalar.copy(Q["rs"][0:32], Q["qk"][32:64])
                nc.scalar.copy(Q["rs"][32:64], Q["qk"][0:32]).then_inc(S["rotated"], 1)
                for g in range(GROUPS):
                    tt = t + NQ + g
                    tile_done(act, tt, i, 20)
                    nc.scalar.copy(Q["v"][:, g, :], bank[tt % 2][:, 0:T]).then_inc(S["av_ready"], 1)
                    act.wait_ge(S["av_ready"], GROUPS * n - GROUPS + g + 1)
                    act.sem_inc(taken[tt % 2], 1)
                act.wait_ge(S["smax_ready"], n)
                for tt in range(TS):
                    ins = nc.scalar.activation(Q["sc"][:, span[tt]], Q["sc"][:, span[tt]], ACT.Exp, bias=Q["mx"][:, tt:tt + 1],
                                               accum_out=Q["sum"][:, tt:tt + 1])
                ins.then_inc(S["exp_ready"], 1)
                tile_done(act, t + 9, i, 20)
                nc.scalar.activation(Q["gs"], bank[(t + 9) % 2][:, 0:T], ACT.Tanh, scale=0.5).then_inc(S["ggate_ready"], 1)

            heads(act, p, base, run, lambda n, hh: finish(n - 1), c, 2)

        def att_vector(dve, c, n):
            norm_vector(dve, n, "norm_w", KC)
            p = at["heads1"]
            base = HEAD_BASE[1]
            two_pi = 2 * np.pi
            c1 = 6.28125
            c2 = float(np.float32(np.floor((two_pi - c1) * 2 ** 20) / 2 ** 20))
            c3 = float(np.float32(two_pi - c1 - c2))
            r, k = Q["sin"][0:RD], Q["cos"][0:RD]
            dve.wait_ge(S["later_loaded"], LATER_COUNT[1])
            posi = Q["pos"][0:RD].bitcast(I32)

            def step(ins):
                c.did(ins)
                c.wait()

            step(nc.vector.tensor_copy(r, posi))
            step(nc.vector.tensor_scalar(r, r, later("attention", "invfreq")[0:RD], None, ALU.mult))
            step(nc.vector.tensor_scalar(k, r, float(1 / two_pi), 12582912.0, ALU.mult, ALU.add))
            step(nc.vector.tensor_scalar(k, k, 12582912.0, None, ALU.subtract))
            for part in (c1, c2, c3):
                step(nc.vector.scalar_tensor_tensor(r, k, -part, r, ALU.mult, ALU.add))
            edge = 3.1415925
            step(nc.vector.tensor_scalar(r, r, edge, -edge, ALU.min, ALU.max))
            step(nc.vector.tensor_scalar(k, r, float(np.pi / 2), None, ALU.is_gt))
            step(nc.vector.scalar_tensor_tensor(k, k, -float(two_pi), r, ALU.mult, ALU.add))
            step(nc.vector.tensor_scalar(k, k, float(np.pi / 2), None, ALU.add))
            nc.vector.tensor_scalar(k, k, edge, -edge, ALU.min, ALU.max).then_inc(S["angles_ready"], 1)
            dve.wait_ge(S["angles_ready"], 2)

            def finish(n, hh):
                dve.wait_ge(S["pv_ps"], n)
                dve.wait_ge(S["agate_ready"], n)
                nc.vector.scalar_tensor_tensor(obuf[:, bass.ds(hh, 1), :].rearrange("p a t -> p (a t)"),
                                               bank[5][:, 0:T], 0.5, Q["gs"], ALU.mult, ALU.mult).then_inc(S["o_tiles"], 1)

            def run(i, n, hh, b, t, first):
                if not first:
                    finish(n - 1, hh - 1)
                dve.wait_ge(S["qrs_ready"], n)
                for j in range(NQ):
                    gain = pcol("b_qn_w", j) if j < GROUPS else pcol("b_kn_w", j - GROUPS)
                    ins = nc.vector.scalar_tensor_tensor(Q["qk"][:, j, :], Q["qk"][:, j, :], gain, Q["rs"][:, j, :],
                                                         ALU.mult, ALU.mult)
                ins.then_inc(S["qn_ready"], 1)
                dve.wait_ge(S["qn_ready"], n)
                c.did(nc.vector.tensor_tensor(Q["t1"][0:RD], Q["qk"][0:RD], Q["cos"][0:RD].unsqueeze(1).to_broadcast([RD, NQ, T]),
                                              ALU.mult))
                dve.wait_ge(S["rotated"], n)
                c.did(nc.vector.tensor_tensor(Q["rs"][0:RD], Q["rs"][0:RD], Q["sin"][0:RD].unsqueeze(1).to_broadcast([RD, NQ, T]),
                                              ALU.mult))
                c.wait()
                nc.vector.tensor_tensor(Q["qk"][0:RD], Q["t1"][0:RD], Q["rs"][0:RD], ALU.add).then_inc(S["rope_ready"], 1)
                dve.wait_ge(S["scores_ps"], n)
                s0, s1 = NS[0], NS[0] + 2 * T
                nc.vector.scalar_tensor_tensor(Q["sc"][:, 0:s0], bank[5][:, 0:s0], ATT_SCALE, later("attention", "att0"),
                                               ALU.mult, ALU.add)
                nc.vector.scalar_tensor_tensor(Q["sc"][:, s0:s1], bank[6][:, :], ATT_SCALE,
                                               later("attention", "att1")[:, 0:2 * T], ALU.mult, ALU.add)
                c.did(nc.vector.scalar_tensor_tensor(Q["sc"][:, s1:s1 + T], bank[7][:, 0:T], ATT_SCALE,
                                                     later("attention", "att1")[:, 2 * T:3 * T], ALU.mult, ALU.add))
                c.wait()
                for tt in range(TS):
                    ins = nc.vector.tensor_reduce(Q["mx"][:, tt:tt + 1], Q["sc"][:, span[tt]], AX.X, ALU.max, negate=True)
                ins.then_inc(S["smax_ready"], 1)
                dve.wait_ge(S["exp_ready"], n)
                c.did(nc.vector.reciprocal(Q["inv"], Q["sum"]))
                c.wait()
                for tt in range(TS):
                    ins = nc.vector.tensor_scalar(Q["sc"][:, span[tt]], Q["sc"][:, span[tt]], Q["inv"][:, tt:tt + 1], None,
                                                  ALU.mult)
                ins.then_inc(S["probs_ready"], 1)
                dve.wait_ge(S["ggate_ready"], n)
                nc.vector.scalar_tensor_tensor(Q["gs"], Q["gs"], 1.0, bank[(t + 9) % 2][:, 0:T], ALU.add, ALU.mult)\
                    .then_inc(S["agate_ready"], 1)
                release(dve, S["agate_ready"], n, t + 9)

            heads(dve, p, base, run, lambda n, hh: finish(n - 1, hh - 1), c, 8)
            out_vector(dve, "out1", NORM_OF[1])

        PADT = 16
        W = wcarve(0, dict(diff=(KC, T), gate=(KC, T), u=(4, PADT + T), s1=(4, PADT + T), s2=(4, PADT + T)))

        def four(v):
            return v[:, :, PADT:PADT + T]

        def pool_tensor(pe, n):
            for name in ("pool_u", "pool_gate"):
                p = at[name]
                peeled = SLOTS * (name == "pool_u")
                for j in range(peeled):
                    project(pe, hk if j else hk_arriving(pe, 2), p.b + j, p.t + j)
                with pe.Fori(0, (KC - peeled) // SLOTS) as i:
                    for j in range(SLOTS):
                        project(pe, hk, p.b + peeled + j, p.t + peeled + j, i, SLOTS, SLOTS)
            p = at["pool_mix"]
            for g in range(4):
                pe.wait_ge(S["diff_ready"], g + 1)
                project(pe, lambda k: W["diff"][:, 4 * g + k, :], p.b + g, p.t + 4 * g, width=4, kc=4)
            out_tensor(pe, "out2", KC, O_BEFORE[2] + KC, n)

        def pool_scalar(act, c, n):
            norm_scalar(act, c, n)
            p = at["pool_gate"]
            with act.Fori(0, KC // 2) as i:
                for j in range(2):
                    tile_done(act, p.t + j, i, 2)
                    nc.scalar.activation(W["gate"][:, bass.ds(2 * i + j, 1), :].rearrange("p a t -> p (a t)"),
                                         bank[(p.t + j) % 2][:, 0:T], ACT.Tanh, scale=0.5).then_inc(S["pgate_tanh"], 1)

        def pool_vector(dve, c, n):
            norm_vector(dve, n, "norm_w", 2 * KC)
            dve.wait_ge(S["later_loaded"], LATER_COUNT[2])
            p = at["pool_u"]
            for v in (W["u"], W["s1"], W["s2"]):
                c.did(nc.vector.memset(v[:, :, 0:PADT], 0.0))
            c.wait()
            for g in range(4):
                for j in range(4):
                    t = p.t + 4 * g + j
                    tile_done(dve, t)
                    nc.vector.tensor_copy(W["u"][:, j, PADT:], bank[t % 2][:, 0:T]).then_inc(taken[t % 2], 1)
                    bank_now_free(dve, t)
                src = W["u"]
                for l in range(g + 1):
                    dst = (W["s1"], W["s2"])[l % 2]
                    s = 1 << l
                    c.did(nc.vector.tensor_tensor(four(dst), four(src), src[:, :, PADT - s:PADT - s + T], ALU.add))
                    c.wait()
                    src = dst
                inv = later("pool", "poolcnt")[:, g * T:(g + 1) * T].unsqueeze(1).to_broadcast([P, 4, T])
                c.did(nc.vector.tensor_tensor(four(src), four(src), inv, ALU.mult))
                c.wait()
                nc.vector.tensor_tensor(W["diff"][:, 4 * g:4 * g + 4, :], four(src), four(W["u"]), ALU.subtract)\
                    .then_inc(S["diff_ready"], 1)
                dve.wait_ge(S["diff_ready"], g + 1)
            p = at["pool_gate"]
            with dve.Fori(0, KC // 2) as i:
                for j in range(2):
                    dve.wait_ge(S["pgate_tanh"], 2 * i + (j + 1))
                    gm = W["gate"][:, bass.ds(2 * i + j, 1), :].rearrange("p a t -> p (a t)")
                    nc.vector.scalar_tensor_tensor(gm, gm, 1.0, bank[(p.t + j) % 2][:, 0:T], ALU.add, ALU.mult)\
                        .then_inc(S["pgate_ready"], 1)
                    release(dve, S["pgate_ready"], 2 * i + (j + 1), p.t + j)
            p = at["pool_mix"]
            with dve.Fori(0, KC // 2) as i:
                for j in range(2):
                    tile_done(dve, p.t + j, i, 2)
                    m = 2 * i + j
                    nc.vector.scalar_tensor_tensor(
                        obuf[:, bass.ds(m, 1), :].rearrange("p a t -> p (a t)"), bank[(p.t + j) % 2][:, 0:T],
                        pcol("c_scale", m, half), W["gate"][:, bass.ds(m, 1), :].rearrange("p a t -> p (a t)"),
                        ALU.mult, ALU.mult).then_inc(S["o_tiles"], 1)
                    release(dve, S["o_tiles"], m + (O_BEFORE[2] + 1), p.t + j)
            out_vector(dve, "out2", NORM_OF[2])

        def later_gpsimd(pool, l):
            if NORM_OF[l]:
                pool.wait_ge(S["o_tiles"], O_BEFORE[l])
            name = {1: "attention", 2: "pool", 4: "even", 5: "odd"}[l]
            pool.dma_start(work[:, LATER0:LATER0 + NLATER[name]], a["const_" + name]).then_inc(S["later_loaded"], 16)
            if l == 1:
                pool.dma_start(Q["pos"][0:RD].bitcast(I32), a["positions"]).then_inc(S["later_loaded"], 16)
            if l == 5:
                pool.dma_start(gw, a["gates_w"]).then_inc(S["later_loaded"], 16)

        KV = 2
        E = wcarve(5 * KC * T // 4, dict(k=(KV, T), v=(KV, T), q=(T,), sq=(T,), rs=(T,), t1=(T,), vcur=(T,), p=(TS, T), pt=(4, P),
                                gs=(T,), mx=(TS,), sum=(TS,), inv=(TS,)))
        G = wcarve(0, dict(xl=(T + 3,), xc=(T,), r=(4, T), a=(2, T), th=(2, T), m=(2, T), u=(2, T), hf=(T,), hb=(T,),
                           gs=(T,), w=(4, P), lam=(16,), e=(16,), z=(16,), z2=(16,), s=(16,), nlam=(16,)))
        HP = float(P) ** -0.5

        def even_tensor(pe, n):
            p = at["kv4"]
            for j in range(KV):
                project(pe, hk if j else hk_arriving(pe, 4), p.b + j, p.t + j)
            for j in range(KV):
                token_tile(pe, p.b + KV + j, p.t + KV + j)
            pe.wait_ge(S["later_loaded"], LATER_COUNT[4])
            for j in range(KV):
                pe.wait_ge(S["ksq2_ready"], j + 1)
                nc.tensor.matmul(bank[2 + j][:, 0:T], ones[:, :], E["rs"] if j else E["sq"], start=True, stop=True)\
                    .then_inc(S["kstat_ps"], 1)
            for j in range(KV):
                pe.wait_ge(S["kn_ready"], j + 1)
                nc.tensor.matmul(bank[2 + j][:, 0:T], later("even", "rotax"), E["k"][:, j, :], start=True, stop=True)\
                    .then_inc(S["krotated"], 1)
            p = at["heads4"]
            base = HEAD_BASE[4]

            def turn_probs(n):
                pe.wait_ge(S["probs_ready"], n)
                for s in range(TS):
                    for t in range(TS):
                        ins = nc.tensor.transpose(bank[5][:, (s * TS + t) * P:(s * TS + t + 1) * P],
                                                  E["p"][:, t, s * P:(s + 1) * P], cst("ident"))
                ins.then_inc(S["probt_ps"], 1)

            def finish(n):
                pe.wait_ge(S["probt_ready"], n)
                pe.wait_ge(S["vcur_ready"], n - base)
                for s in range(TS):
                    ins = nc.tensor.matmul(bank[6][:, 0:T], E["vcur"][:, s * P:(s + 1) * P],
                                           E["pt"][:, TS * s:TS * s + TS, :], start=(s == 0), stop=(s == TS - 1))
                ins.then_inc(S["pv_ps"], 1)

            def run(i, n, hh, b, t, first):
                project(pe, hk, b, t, i, 4, 4)
                if not first:
                    turn_probs(n - 1)
                project_part(pe, hk, b + 1, t + 1, 0, 4, i, 4, 4)
                pe.wait_ge(S["qsq4_ready"], n - base)
                if first:
                    pe.wait_ge(S["kv4_ready"], KV)
                nc.tensor.matmul(bank[2][:, 0:T], ones[:, :], E["sq"], start=True, stop=True).then_inc(S["qstat_ps"], 1)
                if not first:
                    finish(n - 1)
                project_part(pe, hk, b + 1, t + 1, 4, 12, i, 4, 4)
                pe.wait_ge(S["qn_ready"], n)
                nc.tensor.matmul(bank[3][:, 0:T], later("even", "rotax"), E["q"], start=True, stop=True)\
                    .then_inc(S["rotated"], 1)
                project_part(pe, hk, b + 1, t + 1, 12, KC, i, 4, 4)
                pe.wait_ge(S["rope_ready"], n)
                for tt in range(TS):
                    ins = nc.tensor.matmul(bank[4][:, tt * T:(tt + 1) * T], E["q"][:, tt * P:(tt + 1) * P], E["t1"],
                                           start=True, stop=True)
                ins.then_inc(S["scores_ps"], 1)

            heads(pe, p, base, run, None)
            p = at["lru4"]

            def lru(i, n, hh, b, t, first):
                project(pe, hk, b, t, i, 4, 4)
                project(pe, hk, b + 1, t + 1, i, 4, 4)
                if first:
                    turn_probs(base + HEADS)
                    finish(base + HEADS)
                pe.wait_ge(S["lruw_loaded"], 16 * n)
                pe.wait_ge(S["xc_ready"], n)
                for j in range(4):
                    ins = nc.tensor.matmul(bank[2 + j // 2][:, (j % 2) * T:(j % 2 + 1) * T], G["w"][:, j, :], G["xc"],
                                           start=True, stop=True)
                ins.then_inc(S["lru_ps"], 1)

            heads(pe, p, 0, lru, None)
            out_tensor(pe, "out4", KC, O_BEFORE[4] + KC, n)

        def even_scalar(act, c, n):
            norm_scalar(act, c, n)
            p = at["kv4"]
            for j in range(KV):
                t = p.t + j
                tile_done(act, t)
                nc.scalar.copy(E["k"][:, j, :], bank[t % 2][:, 0:T]).then_inc(taken[t % 2], 1)
                bank_now_free(act, t)
                nc.scalar.activation(E["rs"] if j else E["sq"], E["k"][:, j, :], ACT.Square).then_inc(S["ksq2_ready"], 1)
            for j in range(KV):
                t = p.t + KV + j
                tile_done(act, t)
                nc.scalar.copy(E["v"][:, j, :], bank[t % 2][:, 0:T]).then_inc(taken[t % 2], 1)
                bank_now_free(act, t)
            for j in range(KV):
                act.wait_ge(S["kstat_ps"], j + 1)
                if j:
                    act.wait_ge(S["kn_ready"], 1)
                c.did(nc.scalar.activation(E["gs"], bank[2 + j][:, 0:T], ACT.Ln, bias=cst("eps"), scale=1.0 / P))
                c.wait()
                nc.scalar.activation(E["gs"], E["gs"], ACT.Exp, scale=-0.5).then_inc(S["krs_ready"], 1)
            lam = par[:, PARAM_AT["lru_lambda_2"]:PARAM_AT["lru_lambda_2"] + 16]
            c.did(nc.scalar.activation(G["e"], lam, ACT.Abs))
            c.wait()
            nc.scalar.activation(G["e"], G["e"], ACT.Exp, scale=-1.0).then_inc(S["lam_ready"], 1)
            p = at["heads4"]
            base = HEAD_BASE[4]

            def finish(n):
                act.wait_ge(S["probt_ps"], n)
                nc.scalar.copy(E["pt"], bank[5][:, :].rearrange("p (a b) -> p a b", a=4)).then_inc(S["probt_ready"], 1)

            def run(i, n, hh, b, t, first):
                tile_done(act, t, i, 4)
                if not first:
                    act.wait_ge(S["scores_ps"], n - 1)
                nc.scalar.copy(E["q"], bank[t % 2][:, 0:T]).then_inc(taken[t % 2], 1)
                bank_now_free(act, t, i, 4)
                if first:
                    act.wait_ge(S["kstat_ps"], KV)
                nc.scalar.activation(E["sq"], E["q"], ACT.Square).then_inc(S["qsq4_ready"], 1)
                if not first:
                    finish(n - 1)
                act.wait_ge(S["qstat_ps"], n)
                if first:
                    act.wait_ge(S["kv4_ready"], KV)
                c.did(nc.scalar.activation(E["rs"], bank[2][:, 0:T], ACT.Ln, bias=cst("eps"), scale=1.0 / P))
                c.wait()
                nc.scalar.activation(E["rs"], E["rs"], ACT.Exp, scale=-0.5).then_inc(S["qrs_ready"], 1)
                tile_done(act, t + 1, i, 4)
                if not first:
                    act.wait_ge(S["o_tiles"], O_BEFORE[4] + hh)
                nc.scalar.activation(E["gs"], bank[(t + 1) % 2][:, 0:T], ACT.Tanh, scale=0.5).then_inc(S["ggate_ready"], 1)
                act.wait_ge(S["smax_ready"], n)
                for tt in range(TS):
                    ins = nc.scalar.activation(E["p"][:, tt, :], bank[4][:, tt * T:(tt + 1) * T], ACT.Exp,
                                               bias=E["mx"][:, tt:tt + 1], scale=HP, accum_out=E["sum"][:, tt:tt + 1])
                ins.then_inc(S["exp_ready"], 1)

            heads(act, p, base, run, lambda n, hh: finish(n - 1), c, 2)

            act.wait_ge(S["lru_wait"], 1)
            act.wait_ge(S["lam_ready"], 2)
            p = at["lru4"]

            def lru(i, n, hh, b, t, first):
                tile_done(act, t, i, 4)
                if not first:
                    act.wait_ge(S["xc_ready"], n - 1)
                nc.scalar.copy(G["xl"][:, 2:T + 2], bank[t % 2][:, 0:T]).then_inc(S["xl_ready"], 1)
                release(act, S["xl_ready"], n, t)
                tile_done(act, t + 1, i, 4)
                if not first:
                    act.wait_ge(S["o_tiles"], O_BEFORE[4] + HEADS + hh)
                nc.scalar.activation(G["gs"], bank[(t + 1) % 2][:, 0:T], ACT.Tanh, scale=0.5).then_inc(S["lgate_tanh"], 1)
                act.wait_ge(S["lru_ps"], n)
                for j in range(4):
                    name = "lru_ba_2" if j < 2 else "lru_bx_2"
                    ins = nc.scalar.activation(G["r"][:, j, :], bank[2 + j // 2][:, (j % 2) * T:(j % 2 + 1) * T], ACT.Tanh,
                                               bias=pcol(name, hh + 8 * (j % 2), half), scale=0.5)
                ins.then_inc(S["lrt_ready"], 1)
                act.wait_ge(S["lr_ready"], n)
                for j in range(2):
                    c.did(nc.scalar.activation(G["a"][:, j, :], G["r"][:, j, :], ACT.Exp, scale=G["lam"][:, bass.ds(hh + 8 * j, 1)]))
                    ins = nc.scalar.activation(G["th"][:, j, :], G["r"][:, j, :], ACT.Tanh,
                                               scale=G["nlam"][:, bass.ds(hh + 8 * j, 1)])
                ins.then_inc(S["la_ready"], 1)
                act.wait_ge(S["lm_ready"], n)
                nc.scalar.activation(G["m"], G["m"], ACT.Sqrt).then_inc(S["lsq_ready"], 1)

            heads(act, p, 0, lru, None, c, 4)

        def even_vector(dve, c, n):
            norm_vector(dve, n, "norm_gain_2", 0)
            dve.wait_ge(S["later_loaded"], LATER_COUNT[4])
            axcos, axsin, base = later("even", "axcos"), later("even", "axsin"), HEAD_BASE[4]
            for j in range(KV):
                dve.wait_ge(S["krs_ready"], j + 1)
                nc.vector.scalar_tensor_tensor(E["k"][:, j, :], E["k"][:, j, :], pcol("k_norm_gain_2", 0), E["gs"],
                                               ALU.mult, ALU.mult).then_inc(S["kn_ready"], 1)
            for j in range(KV):
                dve.wait_ge(S["krotated"], j + 1)
                if not j:
                    dve.wait_ge(S["kn_ready"], KV)
                c.did(nc.vector.tensor_tensor(E["k"][:, j, :], E["k"][:, j, :], axcos, ALU.mult))
                c.did(nc.vector.tensor_tensor(E["rs"], bank[2 + j][:, 0:T], axsin, ALU.mult))
                c.wait()
                nc.vector.tensor_tensor(E["k"][:, j, :], E["k"][:, j, :], E["rs"], ALU.add).then_inc(S["kv4_ready"], 1)
                dve.wait_ge(S["kv4_ready"], j + 1)
            p = at["heads4"]

            def step(ins):
                c.did(ins)
                c.wait()

            def lru_rates():
                c.did(nc.vector.memset(G["xl"], 0.0))
                c.wait()
                nc.vector.memset(G["s"], 1.0 / 15.0).then_inc(S["lru_wait"], 1)
                dve.wait_ge(S["lru_wait"], 1)
                dve.wait_ge(S["lam_ready"], 1)

                step(nc.vector.tensor_scalar(G["z"], G["e"], 2.0, None, ALU.add))
                step(nc.vector.reciprocal(G["z"], G["z"]))
                step(nc.vector.tensor_tensor(G["z"], G["z"], G["e"], ALU.mult))
                step(nc.vector.tensor_tensor(G["z2"], G["z"], G["z"], ALU.mult))
                for k in (13, 11, 9, 7, 5, 3, 1):
                    step(nc.vector.tensor_tensor(G["s"], G["s"], G["z2"], ALU.mult))
                    step(nc.vector.tensor_scalar(G["s"], G["s"], 1.0 / k, None, ALU.add))
                step(nc.vector.tensor_tensor(G["s"], G["s"], G["z"], ALU.mult))
                lam = par[:, PARAM_AT["lru_lambda_2"]:PARAM_AT["lru_lambda_2"] + 16]
                step(nc.vector.tensor_scalar(G["lam"], lam, 0.0, 8.0, ALU.min, ALU.mult))
                step(nc.vector.scalar_tensor_tensor(G["lam"], G["s"], -16.0, G["lam"], ALU.mult, ALU.add))
                nc.vector.tensor_scalar(G["nlam"], G["lam"], -1.0, None, ALU.mult).then_inc(S["lam_ready"], 1)

            def finish(n, hh):
                dve.wait_ge(S["pv_ps"], n)
                dve.wait_ge(S["agate_ready"], n)
                nc.vector.scalar_tensor_tensor(obuf[:, bass.ds(hh, 1), :].rearrange("p a t -> p (a t)"),
                                               bank[6][:, 0:T], 0.5, E["gs"], ALU.mult, ALU.mult).then_inc(S["o_tiles"], 1)

            def run(i, n, hh, b, t, first):
                dve.wait_ge(S["qrs_ready"], n)
                nc.vector.scalar_tensor_tensor(E["q"], E["q"], pcol("q_norm_gain_2", 0), E["rs"], ALU.mult, ALU.mult)\
                    .then_inc(S["qn_ready"], 1)
                if not first:
                    finish(n - 1, hh - 1)
                dve.wait_ge(S["rotated"], n)
                dve.wait_ge(S["qn_ready"], n)
                c.did(nc.vector.tensor_tensor(E["rs"], bank[3][:, 0:T], axsin, ALU.mult))
                c.did(nc.vector.tensor_tensor(E["q"], E["q"], axcos, ALU.mult))
                kv = hh // 4 if isinstance(hh, int) else nc.s_assert_within(
                    hh >> 2, 0, KV - 1, skip_runtime_bounds_check_because="there are 8 heads")
                nc.vector.tensor_copy(E["t1"], E["k"][:, bass.ds(kv, 1), :].rearrange("p a t -> p (a t)"))
                nc.vector.tensor_copy(E["vcur"], E["v"][:, bass.ds(kv, 1), :].rearrange("p a t -> p (a t)"))\
                    .then_inc(S["vcur_ready"], 1)
                c.wait()
                nc.vector.tensor_tensor(E["q"], E["q"], E["rs"], ALU.add).then_inc(S["rope_ready"], 1)
                dve.wait_ge(S["scores_ps"], n)
                c.did(nc.vector.tensor_reduce(E["mx"], bank[4][:, :].rearrange("p (a b) -> p a b", a=TS), AX.X, ALU.max))
                c.wait()
                nc.vector.tensor_scalar(E["mx"], E["mx"], -HP, None, ALU.mult).then_inc(S["smax_ready"], 1)
                dve.wait_ge(S["ggate_ready"], n)
                nc.vector.scalar_tensor_tensor(E["gs"], E["gs"], 1.0, bank[(t + 1) % 2][:, 0:T], ALU.add, ALU.mult)\
                    .then_inc(S["agate_ready"], 1)
                release(dve, S["agate_ready"], n, t + 1)
                dve.wait_ge(S["exp_ready"], n)
                c.did(nc.vector.reciprocal(E["inv"], E["sum"]))
                c.wait()
                for tt in range(TS):
                    ins = nc.vector.tensor_scalar(E["p"][:, tt, :], E["p"][:, tt, :], E["inv"][:, tt:tt + 1], None, ALU.mult)
                ins.then_inc(S["probs_ready"], 1)
                if first:
                    lru_rates()

            heads(dve, p, base, run, lambda n, hh: finish(n - 1, hh - 1), c, 8)

            def lru(i, n, hh, b, t, first):
                dve.wait_ge(S["xl_ready"], n)
                if not first:
                    dve.wait_ge(S["lru_ps"], n - 1)
                c.did(nc.vector.tensor_scalar(G["xc"], G["xl"][:, 0:T], pcol("conv_w_2", hh), pcol("conv_b_2", hh),
                                              ALU.mult, ALU.add))
                c.wait()
                for j in range(1, 4):
                    ins = nc.vector.scalar_tensor_tensor(G["xc"], G["xl"][:, j:T + j], pcol("conv_w_2", hh + 8 * j), G["xc"],
                                                         ALU.mult, ALU.add)
                    if j < 3:
                        step(ins)
                ins.then_inc(S["xc_ready"], 1)
                dve.wait_ge(S["lgate_tanh"], n)
                nc.vector.scalar_tensor_tensor(G["gs"], G["gs"], 1.0, bank[(t + 1) % 2][:, 0:T], ALU.add, ALU.mult)\
                    .then_inc(S["lgate_ready"], 1)
                release(dve, S["lgate_ready"], n, t + 1)
                dve.wait_ge(S["lrt_ready"], n)
                nc.vector.tensor_scalar(G["r"], G["r"], 0.5, 0.5, ALU.mult, ALU.add).then_inc(S["lr_ready"], 1)
                dve.wait_ge(S["lr_ready"], n)
                dve.wait_ge(S["xc_ready"], n)
                c.did(nc.vector.tensor_tensor(G["u"], G["r"][:, 2:4, :], G["xc"].unsqueeze(1).to_broadcast([P, 2, T]), ALU.mult))
                dve.wait_ge(S["la_ready"], n)
                step(nc.vector.tensor_tensor(G["m"], G["a"], G["a"], ALU.mult))
                step(nc.vector.scalar_tensor_tensor(G["m"], G["m"], 1.0, G["th"], ALU.add, ALU.mult))
                nc.vector.tensor_scalar(G["m"], G["m"], 1e-30, None, ALU.max).then_inc(S["lm_ready"], 1)
                dve.wait_ge(S["lsq_ready"], n)
                step(nc.vector.tensor_tensor(G["u"], G["u"], G["m"], ALU.mult))
                c.did(nc.vector.tensor_tensor_scan(G["hf"], G["a"][:, 0, :], G["u"][:, 0, :], 0.0, ALU.mult, ALU.add))
                step(nc.vector.tensor_tensor_scan(G["hb"][:, ::-1], G["a"][:, 1, ::-1], G["u"][:, 1, ::-1], 0.0,
                                                  ALU.mult, ALU.add))
                step(nc.vector.tensor_tensor(G["hf"], G["hf"], G["hb"], ALU.add))
                dve.wait_ge(S["lgate_ready"], n)
                nc.vector.scalar_tensor_tensor(obuf[:, bass.ds(hh + HEADS, 1), :].rearrange("p a t -> p (a t)"),
                                               G["hf"], 0.5, G["gs"], ALU.mult, ALU.mult).then_inc(S["o_tiles"], 1)

            heads(dve, at["lru4"], 0, lru, None, c, 20)
            out_vector(dve, "out4", NORM_OF[4])

        def even_gpsimd(pool):
            pool.wait_ge(S["norm_sum"], NORM_OF[4] + 1)

            def one(j, n):
                if not isinstance(j, int):
                    pool.wait_ge(S["lru_ps"], n - 1)
                pool.dma_start(G["w"], a["lru_w"][bass.ds(j, 1)].rearrange("a p m n -> p (a m) n"))\
                    .then_inc(S["lruw_loaded"], 16)

            one(0, 1)
            with pool.Fori(0, HEADS - 1) as i:
                one(i + 1, i + 2)

        NG = 2 * HEADS
        M = wcarve(KC * T, dict(gi=(T,), gf=(T,), tmp=(T,), bsum=(2, T), g=(2, T), mf=(2, 2, T), gcol=(TS, NG), q=(T,),
                                k=(T,), v=(TS, 2, P), mh=(4, T), fl=(2, T), mm=(2, 2, P), e=(2, TS, T), dn=(2, T),
                                w=(TS, T), osig=(2, T), hs=(2, T), hsq=(2, T), rs=(T,), zs=(2, T), gw=(KC, 32)))
        gw = M["gw"]

        def odd_tensor(pe, n):
            p = at["gates5"]
            pe.wait_ge(S["later_loaded"], LATER_COUNT[5])
            arriving = hk_arriving(pe, 5)
            bank_free(pe, p.t)
            for j in range(2):
                for k in range(KC):
                    ins = nc.tensor.matmul(bank[p.t % 2][0:NG, j * T:(j + 1) * T], gw[:, k, NG * j:NG * (j + 1)],
                                           hk(k) if j else arriving(k),
                                           start=(k == 0), stop=(k == KC - 1))
            ins.then_inc(S["tile_ready"], 1)
            p = at["heads5"]

            def finish(n):
                pe.wait_ge(S["mw_ready"], n)
                for vt in range(2):
                    for s in range(TS):
                        ins = nc.tensor.matmul(bank[6][:, vt * T:(vt + 1) * T], M["v"][:, s, vt, :], M["w"][:, s, :],
                                               start=(s == 0), stop=(s == TS - 1))
                ins.then_inc(S["mpv_ps"], 1)

            def run(i, n, hh, b, t, first):
                project(pe, hk, b, t, i, 16, 16)
                project(pe, hk, b + 1, t + 1, i, 16, 16)
                if first:
                    pe.wait_ge(S["gates_dve"], 3)
                    for j in range(2):
                        for tt in range(TS):
                            ins = nc.tensor.transpose(bank[2][:, (2 * j + tt) * NG:(2 * j + tt + 1) * NG],
                                                      M["g"][0:NG, j, tt * P:(tt + 1) * P], cst("ident")[0:NG, 0:NG])
                    ins.then_inc(S["gt_ps"], 1)
                    pe.wait_ge(S["gates_dve"], 4)
                pe.wait_ge(S["mh_ready"], n)
                nc.tensor.matmul(bank[2][:, :], ones[0:NG, :], M["mh"][0:NG, 0:2, :], start=True, stop=True)
                nc.tensor.matmul(bank[3][:, :], ones[0:NG, :], M["mh"][0:NG, 2:4, :], start=True, stop=True)\
                    .then_inc(S["mbc_ps"], 1)
                token_tile(pe, b + 2, t + 2, i, 16, 16)
                pe.wait_ge(S["mk_ready"], n)
                for s in range(TS):
                    ins = nc.tensor.matmul(bank[4][:, s * T:(s + 1) * T], M["k"][:, s * P:(s + 1) * P], M["q"],
                                           start=True, stop=True)
                ins.then_inc(S["ms_ps"], 1)
                token_tile(pe, b + 3, t + 3, i, 16, 16)
                pe.wait_ge(S["me_ready"], n)
                for d in range(2):
                    for s in range(TS):
                        ins = nc.tensor.matmul(bank[5][:, d * T:(d + 1) * T], ones[:, :], M["e"][:, d, s, :],
                                               start=(s == 0), stop=(s == TS - 1))
                ins.then_inc(S["mden_ps"], 1)
                project(pe, hk, b + 4, t + 4, i, 16, 16)
                project(pe, hk, b + 5, t + 5, i, 16, 16)
                pe.wait_ge(S["mv_ready"], 2 * n)
                finish(n)
                project(pe, hk, b + 6, t + 6, i, 16, 16)
                pe.wait_ge(S["mhsq_ready"], n)
                for vt in range(2):
                    ins = nc.tensor.matmul(bank[7][:, 0:T], ones[:, :], M["hsq"][:, vt, :], start=(vt == 0), stop=(vt == 1))
                ins.then_inc(S["mstat_ps"], 1)
                project(pe, hk, b + 7, t + 7, i, 16, 16)

            heads(pe, p, 0, run, None)
            out_tensor(pe, "out5", KC, O_BEFORE[5] + KC, n)

        def odd_scalar(act, c, n):
            norm_scalar(act, c, n)
            g = slice(0, NG)
            act.wait_ge(S["gates_dve"], 1)
            c.did(nc.scalar.activation(M["tmp"][g], M["gf"][g], ACT.Abs))
            c.wait()
            c.did(nc.scalar.activation(M["tmp"][g], M["tmp"][g], ACT.Exp, scale=-1.0))
            c.wait()
            nc.scalar.activation(M["tmp"][g], M["tmp"][g], ACT.Ln, bias=cst("one")[g]).then_inc(S["gates_act"], 1)
            act.wait_ge(S["gates_dve"], 2)
            nc.scalar.activation(M["mf"][g, 1], M["mf"][g, 1], ACT.Exp, scale=-1.0).then_inc(S["gates_act"], 1)
            p = at["heads5"]

            def run(i, n, hh, b, t, first):
                tile_done(act, t, i, 16)
                if not first:
                    act.wait_ge(S["ms_ps"], n - 1)
                nc.scalar.copy(M["q"], bank[t % 2][:, 0:T]).then_inc(taken[t % 2], 1)
                tile_done(act, t + 1, i, 16)
                nc.scalar.mul(M["k"], bank[(t + 1) % 2][:, 0:T], HP).then_inc(S["mk_ready"], 1)
                release(act, S["mk_ready"], n, t + 1)
                act.wait_ge(S["mbc_ps"], n)
                if not first:
                    act.wait_ge(S["mdn_ready"], n - 1)
                c.did(nc.scalar.copy(M["fl"], bank[3][:, :].rearrange("p (a b) -> p a b", a=2)))
                act.wait_ge(S["mm2_ready"], n)
                if not first:
                    act.wait_ge(S["mw_ready"], n - 1)
                gf0, gf1 = (M["gcol"][:, s, bass.ds(hh, 1)] for s in range(2))
                gb0, gb1 = (M["gcol"][:, s, bass.ds(hh + HEADS, 1)] for s in range(2))
                nc.scalar.activation(M["e"][:, 0, 0, 0:P], M["mm"][:, 0, 0, :], ACT.Exp, bias=gf0)
                nc.scalar.activation(M["e"][:, 0, 0, P:T], bank[2][:, P:T], ACT.Exp, bias=gf0, scale=-1.0)
                nc.scalar.activation(M["e"][:, 0, 1, P:T], M["mm"][:, 0, 1, :], ACT.Exp, bias=gf1)
                nc.scalar.activation(M["e"][:, 1, 0, 0:P], M["mm"][:, 1, 0, :], ACT.Exp, bias=gb0)
                nc.scalar.activation(M["e"][:, 1, 1, 0:P], bank[2][:, T:T + P], ACT.Exp, bias=gb1, scale=-1.0)
                nc.scalar.activation(M["e"][:, 1, 1, P:T], M["mm"][:, 1, 1, :], ACT.Exp, bias=gb1).then_inc(S["mexp_ready"], 1)
                for j in range(2):
                    tile_done(act, t + 2 + j, i, 16)
                    if j == 0 and not first:
                        act.wait_ge(S["mpv_ps"], n - 1)
                    nc.scalar.copy(M["v"][:, :, j, :], bank[(t + j) % 2][:, 0:T].rearrange("p (a b) -> p a b", a=TS))\
                        .then_inc(S["mv_ready"], 1)
                    release(act, S["mv_ready"], 2 * n - 1 + j, t + 2 + j)
                for j in range(2):
                    tile_done(act, t + 4 + j, i, 16)
                    nc.scalar.activation(M["osig"][:, j, :], bank[(t + j) % 2][:, 0:T], ACT.Tanh, scale=0.5)\
                        .then_inc(S["mo_ready"], 1)
                    release(act, S["mo_ready"], 2 * n - 1 + j, t + 4 + j)
                act.wait_ge(S["mhs_ready"], n)
                nc.scalar.activation(M["hsq"], M["hs"], ACT.Square).then_inc(S["mhsq_ready"], 1)
                act.wait_ge(S["mstat_ps"], n)
                c.did(nc.scalar.activation(M["rs"], bank[7][:, 0:T], ACT.Ln, bias=cst("eps"), scale=0.25 / (2 * P)))
                c.wait()
                nc.scalar.activation(M["rs"], M["rs"], ACT.Exp, scale=-0.5).then_inc(S["mrs_ready"], 1)
                for j in range(2):
                    tile_done(act, t + 6 + j, i, 16)
                    nc.scalar.activation(M["zs"][:, j, :], bank[(t + j) % 2][:, 0:T], ACT.Tanh, scale=0.5)\
                        .then_inc(S["mz_ready"], 1)

            heads(act, p, 0, run, None, c, 4)

        def odd_vector(dve, c, n):
            norm_vector(dve, n, "norm_gain_2", KC)
            dve.wait_ge(S["later_loaded"], LATER_COUNT[5])
            g = slice(0, NG)
            t = at["gates5"].t
            tile_done(dve, t)

            def step(ins):
                c.did(ins)
                c.wait()

            nc.vector.tensor_scalar(M["gi"][g], bank[t % 2][g, 0:T], pcol("gate_bias", 0)[g], None, ALU.add)
            nc.vector.tensor_scalar(M["gf"][g], bank[t % 2][g, T:2 * T], pcol("gate_bias", 1)[g], None, ALU.add)\
                .then_inc(S["gates_dve"], 1)
            release(dve, S["gates_dve"], 1, t)
            dve.wait_ge(S["gates_act"], 1)
            step(nc.vector.tensor_scalar(M["gf"][g], M["gf"][g], 0.0, None, ALU.min))
            step(nc.vector.tensor_tensor(M["gf"][g], M["gf"][g], M["tmp"][g], ALU.subtract))
            step(nc.vector.memset(M["tmp"][g], 0.0))
            c.did(nc.vector.tensor_tensor_scan(M["bsum"][g, 0, :], M["gf"][g], M["tmp"][g], 0.0, ALU.add, ALU.add))
            step(nc.vector.tensor_tensor_scan(M["bsum"][g, 1, ::-1], M["gf"][g, ::-1], M["tmp"][g], 0.0, ALU.add, ALU.add))
            step(nc.vector.tensor_tensor(M["g"][g], M["gi"][g].unsqueeze(1).to_broadcast([NG, 2, T]), M["bsum"][g], ALU.subtract))
            c.did(nc.vector.tensor_tensor_scan(M["mf"][g, 0, 0, :], M["g"][g, 0, :], M["g"][g, 0, :], 0.0, ALU.max, ALU.max))
            step(nc.vector.tensor_tensor_scan(M["mf"][g, 0, 1, ::-1], M["g"][g, 1, ::-1], M["g"][g, 1, ::-1], 0.0,
                                              ALU.max, ALU.max))
            nc.vector.tensor_tensor(M["mf"][g, 1], M["mf"][g, 0], M["bsum"][g], ALU.add).then_inc(S["gates_dve"], 1)
            nc.vector.memset(M["e"][:, 0, 1, 0:P], 0.0)
            nc.vector.memset(M["e"][:, 1, 0, P:T], 0.0).then_inc(S["gates_dve"], 1)
            dve.wait_ge(S["gt_ps"], 1)
            for j in range(2):
                for tt in range(TS):
                    src = bank[2][:, (2 * j + tt) * NG + HEADS * j:(2 * j + tt) * NG + HEADS * (j + 1)]
                    ins = nc.vector.tensor_copy(M["gcol"][:, tt, HEADS * j:HEADS * (j + 1)], src)
            ins.then_inc(S["gates_dve"], 1)
            dve.wait_ge(S["gates_act"], 2)
            p = at["heads5"]

            def run(i, n, hh, b, t, first):
                if not first:
                    dve.wait_ge(S["mbc_ps"], n - 1)
                for d in range(2):
                    pick = cst("ident")[g, bass.ds(hh + HEADS * d, 1)]
                    nc.vector.tensor_scalar(M["mh"][g, d, :], M["mf"][g, 0, d, :], pick, None, ALU.mult)
                    ins = nc.vector.tensor_scalar(M["mh"][g, 2 + d, :], M["mf"][g, 1, d, :], pick, None, ALU.mult)
                ins.then_inc(S["mh_ready"], 1)
                dve.wait_ge(S["mbc_ps"], n)
                for d, name in ((0, "triu"), (1, "tril")):
                    ins = nc.vector.tensor_tensor(M["mm"][:, d], later("odd", name).unsqueeze(1).to_broadcast([P, TS, P]),
                                                  bank[2][:, d * T:(d + 1) * T].rearrange("p (a b) -> p a b", a=TS),
                                                  ALU.subtract)
                ins.then_inc(S["mm2_ready"], 1)
                dve.wait_ge(S["ms_ps"], n)
                dve.wait_ge(S["mexp_ready"], n)
                for d in range(2):
                    ins = nc.vector.tensor_tensor(M["e"][:, d], M["e"][:, d], bank[4][:, :].rearrange("p (a b) -> p a b", a=TS),
                                                  ALU.mult)
                ins.then_inc(S["me_ready"], 1)
                dve.wait_ge(S["mden_ps"], n)
                den = bank[5][:, :].rearrange("p (a b) -> p a b", a=2)
                step(nc.vector.scalar_tensor_tensor(M["dn"], den, -1.0, M["fl"], ALU.mult, ALU.max))
                nc.vector.tensor_tensor(M["dn"], den, M["dn"], ALU.max).then_inc(S["mdn_ready"], 1)
                dve.wait_ge(S["mdn_ready"], n)
                step(nc.vector.reciprocal(M["dn"], M["dn"]))
                dve.wait_ge(S["me_ready"], n)
                for d in range(2):
                    ins = nc.vector.tensor_tensor(M["e"][:, d], M["e"][:, d],
                                                  M["dn"][:, d, :].unsqueeze(1).to_broadcast([P, TS, T]), ALU.mult)
                step(ins)
                nc.vector.tensor_tensor(M["w"], M["e"][:, 0], M["e"][:, 1], ALU.add).then_inc(S["mw_ready"], 1)
                dve.wait_ge(S["mpv_ps"], n)
                dve.wait_ge(S["mo_ready"], 2 * n)
                nc.vector.scalar_tensor_tensor(M["hs"], M["osig"], 1.0, bank[6][:, :].rearrange("p (a b) -> p a b", a=2),
                                               ALU.add, ALU.mult).then_inc(S["mhs_ready"], 1)
                dve.wait_ge(S["mrs_ready"], n)
                dve.wait_ge(S["mhs_ready"], n)
                for j in range(2):
                    step(nc.vector.scalar_tensor_tensor(M["hs"][:, j, :], M["hs"][:, j, :], pcol("odd_norm_gain_2", hh * 2 + j),
                                                        M["rs"], ALU.mult, ALU.mult))
                for j in range(2):
                    dve.wait_ge(S["mz_ready"], 2 * n - 1 + j)
                    nc.vector.scalar_tensor_tensor(M["zs"][:, j, :], M["zs"][:, j, :], 1.0, bank[(t + j) % 2][:, 0:T],
                                                   ALU.add, ALU.mult).then_inc(S["mzs_ready"], 1)
                    release(dve, S["mzs_ready"], 2 * n - 1 + j, t + 6 + j)
                nc.vector.scalar_tensor_tensor(obuf[:, bass.ds(hh * 2, 2), :], M["hs"], 0.25, M["zs"], ALU.mult, ALU.mult)\
                    .then_inc(S["o_tiles"], 2)

            heads(dve, p, 0, run, None, c, 10)
            out_vector(dve, "out5", NORM_OF[5])

        NORM_OF = {l: n for n, l in enumerate(layers)}
        O_MADE = {0: KC, 1: HEADS, 2: KC, 3: KC, 4: KC, 5: KC}
        O_BEFORE, made = {}, 0
        for l in layers:
            O_BEFORE[l] = made
            made += O_MADE[l]
        HEAD_BASE = {1: 0, 4: HEADS * (1 in layers)}
        LATER_COUNT, made = {}, 0
        for l in layers:
            made += {0: 0, 3: 0, 1: 32, 2: 16, 4: 16, 5: 32}[l]
            LATER_COUNT[l] = made

        @block.sync
        def _(sp):
            sp.wait_ge(x_loaded[1], 16)
            where = []
            for name, p in at.items():
                where += [(p.t + (j + 1) * (p.tiles // p.blocks)) for j in range(p.blocks)]

            def load(b, row):
                sp.dma_start(ring[:, b % SLOTS, :], a["stream"][bass.ds(row, 1)].rearrange("a p n -> p (a n)"))\
                    .then_inc(loaded[b % SLOTS], 16)

            for name, p in at.items():
                if not p.blocks:
                    continue
                width = p.tiles // p.blocks
                turns = max(0, (p.blocks - SLOTS) // SLOTS)
                turns = turns if turns > 1 else 0
                for b in range(p.b, p.b + min(SLOTS, p.blocks)):
                    if b >= SLOTS:
                        sp.wait_ge(S["tile_ready"], where[b - SLOTS])
                    load(b, b)
                if turns:
                    with sp.Fori(0, turns) as i:
                        for j in range(SLOTS):
                            sp.wait_ge(S["tile_ready"], i * (SLOTS * width) + (p.t + (j + 1) * width))
                            load(p.b + j, i * SLOTS + (p.b + SLOTS + j))
                for b in range(p.b + SLOTS + turns * SLOTS, p.b + p.blocks):
                    sp.wait_ge(S["tile_ready"], where[b - SLOTS])
                    load(b, b)

        @block.gpsimd
        def _(pool):
            pool.dma_start(const[:, :], a["const"]).then_inc(S["consts_loaded"], 16)
            pool.dma_start(par[:, :], a["par"]).then_inc(S["consts_loaded"], 16)
            pool.wait_ge(S["consts_loaded"], 32)
            nc.gpsimd.tensor_scalar(half[:, :], par[:, :], 0.5, None, ALU.mult).then_inc(S["half_ready"], 1)
            for l in layers:
                if l in (0, 3):
                    rwkv_gpsimd(pool, l // 3)
                else:
                    later_gpsimd(pool, l)
                if l == 4:
                    even_gpsimd(pool)

        @block.scalar
        def _(act):
            for q in range(4):
                act.dma_start(x[:, 4 * q:4 * q + 4, :], a["x_cm"][:, 4 * q:4 * q + 4, :]).then_inc(x_loaded[q], 16)
            c = Steps(act, S["act_steps"])
            for n, l in enumerate(layers):
                if l in (0, 3):
                    rwkv_scalar(act, c, l // 3, n)
                if l == 1:
                    att_scalar(act, c, n)
                if l == 2:
                    pool_scalar(act, c, n)
                if l == 4:
                    even_scalar(act, c, n)
                if l == 5:
                    odd_scalar(act, c, n)
            if final:
                final_scalar(act, c, len(layers))

        @block.vector
        def _(dve):
            nc.vector.memset(ones[:, :], 1.0).then_inc(S["ones_ready"], 1)
            dve.wait_ge(S["consts_loaded"], 32)
            dve.wait_ge(S["half_ready"], 1)
            for q in range(4):
                dve.wait_ge(x_loaded[q], 16)
            c = Steps(dve, S["dve_steps"])
            for n, l in enumerate(layers):
                if l in (0, 3):
                    rwkv_vector(dve, c, l // 3, n)
                if l == 1:
                    att_vector(dve, c, n)
                if l == 2:
                    pool_vector(dve, c, n)
                if l == 4:
                    even_vector(dve, c, n)
                if l == 5:
                    odd_vector(dve, c, n)
            if final:
                final_vector(dve, c, len(layers))

        @block.tensor
        def _(pe):
            pe.wait_ge(S["ones_ready"], 1)
            norm_tensor(pe)
            pe.wait_ge(S["consts_loaded"], 32)
            for n, l in enumerate(layers):
                if l in (0, 3):
                    rwkv_tensor(pe, l // 3, n)
                if l == 1:
                    att_tensor(pe, n)
                if l == 2:
                    pool_tensor(pe, n)
                if l == 4:
                    even_tensor(pe, n)
                if l == 5:
                    odd_tensor(pe, n)




def blocks(w):
    k, n = w.shape
    cols = D * P // k
    return np.ascontiguousarray(w.reshape(k // P, P, n // cols, cols).transpose(2, 1, 0, 3)).reshape(-1, P, D)


def padded(w):
    return np.concatenate([w, np.zeros((w.shape[0], P - w.shape[1]), w.dtype)], 1)


def chunked(v):
    return v.reshape(-1, P).T


def woven(parts):
    turns = [b.reshape(-1, n, P, D) for b, n in parts]
    return np.concatenate(turns, 1).reshape(-1, P, D)


def stream_parts(i):
    def rwkv(n):
        w = i["a_w_in"][n]
        r, k, v, g = (blocks(w[j]) for j in range(4))
        return woven([(k, 1), (r, 1), (v, 1), (g, 1)])

    def lora(n):
        ws = [i["a_w1"][n], i["a_a1"][n]] + ([i["a_v1"][0]] if n else [])
        return np.concatenate([blocks(padded(w)) for w in ws])

    b = blocks(i["b_w_in"][0])
    qkv = b[:72].reshape(3, GROUPS, HEADS, P, D).transpose(2, 0, 1, 3, 4).reshape(-1, P, D)
    qkv = qkv.reshape(HEADS, 3, GROUPS, P, KC, P)
    qkv = np.concatenate([qkv[:, 0:2][..., ROPE_ORDER], qkv[:, 2:3]], 1).reshape(-1, P, D)
    heads1 = woven([(qkv, 9), (b[72:80], 1)])
    c = blocks(i["c_w_in"][0])
    e = blocks(i["even_w_in_2"][0])
    w = i["odd_w_in_2"][0]
    q, k, v, o, z = (blocks(w[:, a0:a1]) for a0, a1 in ((0, 1024), (1024, 2048), (2048, 4096), (4096, 6144),
                                                        (6144, 8192)))
    return {
        "lora0": lora(0), "rwkv0": rwkv(0), "out0": blocks(i["a_w_out"][0]),
        "heads1": heads1, "out1": blocks(i["b_w_out"][0]),
        "pool_u": c[:16], "pool_gate": c[16:], "pool_mix": np.concatenate([blocks(g) for g in i["c_w_grp"][0]]),
        "out2": blocks(i["c_w_out"][0]),
        "lora3": lora(1), "rwkv3": rwkv(1), "out3": blocks(i["a_w_out"][1]),
        "kv4": e[8:12], "heads4": woven([(e[0:8], 1), (e[12:20], 1)]),
        "lru4": woven([(e[20:28], 1), (e[28:36], 1)]), "out4": blocks(i["even_w_out_2"][0]),
        "gates5": np.zeros((0, P, D), np.float32),
        "heads5": woven([(q, 1), (k, 1), (v, 2), (o, 2), (z, 2)]), "out5": blocks(i["odd_w_out_2"][0]),
    }


def layouts(i, phases=None):
    parts = stream_parts(i)
    out = {"stream": np.concatenate([parts[n] for n, _, _ in STREAM if phases is None or n in phases])}
    out["x_cm"] = np.ascontiguousarray(i["x"][0].T.reshape(KC, P, T).transpose(1, 0, 2))
    lay = {"norm_w": 0}
    bias = i["odd_gate_bias_2"][0].reshape(2, 2 * HEADS).T
    special = {"b_qn_w": chunked(i["b_qn_w"])[ROPE_ORDER], "b_kn_w": chunked(i["b_kn_w"])[ROPE_ORDER],
               "gate_bias": np.concatenate([bias, np.zeros((P - 2 * HEADS, 2), np.float32)], 0)}
    out["par"] = np.concatenate([special[n] if n in special else chunked(i[n]) for n, _ in PARAMS], 1)
    out["const"] = np.concatenate([CONST[k] for k in RESIDENT], 1)
    for layer, names in LATER.items():
        out["const_" + layer] = np.concatenate([CONST[k] for k in names], 1)
    v2 = np.zeros((LORA, D), np.float32)
    v2[:MVL] = i["a_v2"][0]
    lora2 = [np.stack([i["a_w2"][n], i["a_a2"][n], v2 if n else np.zeros((LORA, D), np.float32)], 1) for n in range(2)]
    out["lora2"] = np.ascontiguousarray(np.stack([m.reshape(LORA, 3, KC, P).transpose(2, 0, 1, 3) for m in lora2]))
    wa, wx = i["lru_wa_2"][0], i["lru_wx_2"][0]
    out["lru_w"] = np.ascontiguousarray(np.stack([wa[0], wa[1], wx[0], wx[1]], 2))
    g = i["odd_w_in_2"][0][:, 8192:]
    out["gates_w"] = np.ascontiguousarray(g.reshape(KC, P, 32).transpose(1, 0, 2))
    out["positions"] = np.ascontiguousarray(np.broadcast_to(i["positions"], (RD, T)))
    return {k: np.ascontiguousarray(v) for k, v in out.items()}


def kernel(**inputs):
    import concourse.bacc as bacc
    from concourse.bass_utils import run_bass_kernel_spmd

    nc = bacc.Bacc("TRN2", target_bir_lowering=False, num_devices=1)
    arrays = layouts({k: np.asarray(v) for k, v in inputs.items()})
    a = {n: nc.dram_tensor(n, v.shape, mybir.dt.from_np(v.dtype), kind="ExternalInput").ap() for n, v in arrays.items()}
    a["out"] = nc.dram_tensor("out", (P, KC, T), F32, kind="ExternalOutput").ap()
    build(nc, a)
    r = run_bass_kernel_spmd(nc, [arrays], core_ids=[0])
    return r.results[0]["out"].transpose(1, 0, 2).reshape(D, T).T[None]
```
